# Optimizing a Trainium2 kernel written in Bass

```python
import jax, jax.numpy as jnp
from jax import lax
import numpy as np
import jax
import jax.numpy as jnp

D_MODEL = 1024
BATCH = 1
SEQ = 256
DEPTH = 2

GRID_W = 64
Q_BLOCK = 128
ROPE_THETA = 10000.0
EPS = 1e-6
MLA_HEADS = 6
MLA_NOPE = 64
MLA_ROPE = 32
MLA_V = 64
MLA_Q_RANK = 256
MLA_KV_RANK = 128
GQA_HEADS = 6
GQA_KV_HEADS = 2
GQA_DIM = 64
GMLP_GROUPS = 4
GMLP_DIM = 64
GMLP_CHUNK = 128
W_A = MLA_HEADS * MLA_V
W_B = GQA_HEADS * GQA_DIM
W_C = GMLP_GROUPS * GMLP_DIM
D_MIX = W_A + W_B + W_C
IN_SPLITS = (MLA_Q_RANK, MLA_KV_RANK, MLA_ROPE, W_B, GQA_KV_HEADS * GQA_DIM, GQA_KV_HEADS * GQA_DIM, 2 * W_C)
D_IN = 1568
MEM_TOKENS = 256
MEM_HEADS = 4
MEM_DIM = 128
D_FF = 2816
CONV_W = 3


def rms_norm(x, g):
    xf = x.astype(jnp.float32)
    y = xf * lax.rsqrt(jnp.mean(xf * xf, axis=-1, keepdims=True) + EPS)
    return (y * g.astype(jnp.float32)).astype(x.dtype)

def axial_rope_table(S, d_rot):
    rows = S // GRID_W
    row = jnp.repeat(jnp.arange(rows, dtype=jnp.float32), GRID_W)
    col = jnp.tile(jnp.arange(GRID_W, dtype=jnp.float32), rows)
    n = d_rot // 4
    inv = ROPE_THETA ** (-jnp.arange(n, dtype=jnp.float32) / n)
    ang = jnp.concatenate([row[:, None] * inv, col[:, None] * inv], axis=-1)
    return jnp.cos(ang)[:, None, :], jnp.sin(ang)[:, None, :]

def apply_rope(x, cos, sin):
    d = x.shape[-1]
    xp = x.reshape(*x.shape[:-1], d // 2, 2)
    a, b = xp[..., 0], xp[..., 1]
    c, s = cos.astype(x.dtype), sin.astype(x.dtype)
    return jnp.stack([a * c - b * s, a * s + b * c], axis=-1).reshape(x.shape)

def block_attention(q, k, v, scale):
    B, S, H, dk = q.shape
    Hk, dv = k.shape[2], v.shape[-1]
    G = H // Hk
    nb = S // Q_BLOCK
    qb = q.reshape(B, nb, Q_BLOCK, Hk, G, dk).transpose(1, 0, 2, 3, 4, 5)

    def one_block(qi):
        s = jnp.einsum('bqhgd,bkhd->bhgqk', qi, k, preferred_element_type=jnp.float32) * scale
        p = jax.nn.softmax(s, axis=-1).astype(v.dtype)
        return jnp.einsum('bhgqk,bkhe->bqhge', p, v)

    ob = lax.map(one_block, qb)
    return ob.transpose(1, 0, 2, 3, 4, 5).reshape(B, S, H * dv)

def hybrid_mixer(h, rope_a, rope_b, w_in, mla_q_norm, mla_w_uq, mla_kv_norm, mla_w_ukv,
                 gqa_q_norm, gqa_k_norm, gmlp_v_norm, gmlp_w_s, gmlp_b_s, out_norm, w_out):
    B, S, _ = h.shape
    z = h @ w_in
    offs = [int(i) for i in np.cumsum(IN_SPLITS)[:-1]]
    c_q, c_kv, k_rope, g_q, g_k, g_v, g_m = jnp.split(z, offs, axis=-1)

    qa = (rms_norm(c_q, mla_q_norm) @ mla_w_uq).reshape(B, S, MLA_HEADS, MLA_NOPE + MLA_ROPE)
    q_nope, q_pe = qa[..., :MLA_NOPE], apply_rope(qa[..., MLA_NOPE:], *rope_a)
    kva = (rms_norm(c_kv, mla_kv_norm) @ mla_w_ukv).reshape(B, S, MLA_HEADS, MLA_NOPE + MLA_V)
    k_nope, v_a = kva[..., :MLA_NOPE], kva[..., MLA_NOPE:]
    k_pe = apply_rope(k_rope.reshape(B, S, 1, MLA_ROPE), *rope_a)
    q_a = jnp.concatenate([q_nope, q_pe], axis=-1)
    k_a = jnp.concatenate([k_nope, jnp.broadcast_to(k_pe, (B, S, MLA_HEADS, MLA_ROPE))], axis=-1)
    y_a = block_attention(q_a, k_a, v_a, (MLA_NOPE + MLA_ROPE) ** -0.5)

    q_b = apply_rope(rms_norm(g_q.reshape(B, S, GQA_HEADS, GQA_DIM), gqa_q_norm), *rope_b)
    k_b = apply_rope(rms_norm(g_k.reshape(B, S, GQA_KV_HEADS, GQA_DIM), gqa_k_norm), *rope_b)
    v_b = g_v.reshape(B, S, GQA_KV_HEADS, GQA_DIM)
    y_b = block_attention(q_b, k_b, v_b, GQA_DIM ** -0.5)

    g_m = jax.nn.gelu(g_m)
    u, vv = g_m[..., :W_C], g_m[..., W_C:]
    vv = rms_norm(vv, gmlp_v_norm).reshape(B, S // GMLP_CHUNK, GMLP_CHUNK, GMLP_GROUPS, GMLP_DIM)
    mixed = jnp.einsum('gpq,bnqgc->bnpgc', gmlp_w_s, vv) + gmlp_b_s.T[None, None, :, :, None]
    y_c = u * mixed.reshape(B, S, W_C)

    y = jnp.concatenate([rms_norm(y_a, out_norm[:W_A]),
                         rms_norm(y_b, out_norm[W_A:W_A + W_B]),
                         rms_norm(y_c, out_norm[W_A + W_B:])], axis=-1)
    return y @ w_out

def memory_cross_attention(h, mem, mem_kv_norm, mem_w_q, mem_w_kv, mem_w_o):
    B, S, _ = h.shape
    T = mem.shape[1]
    q = (h @ mem_w_q).reshape(B, S, MEM_HEADS, MEM_DIM)
    kv = rms_norm(mem, mem_kv_norm) @ mem_w_kv
    k = kv[..., :MEM_HEADS * MEM_DIM].reshape(B, T, MEM_HEADS, MEM_DIM)
    v = kv[..., MEM_HEADS * MEM_DIM:].reshape(B, T, MEM_HEADS, MEM_DIM)
    return block_attention(q, k, v, MEM_DIM ** -0.5) @ mem_w_o

def conv_gated_ffn(h, w_up, conv_w, conv_b, w_down):
    a = h @ w_up
    ap = jnp.pad(a, ((0, 0), (1, 1), (0, 0)))
    a = ap[:, :-2] * conv_w[0] + ap[:, 1:-1] * conv_w[1] + ap[:, 2:] * conv_w[2] + conv_b
    gate, val = a[..., :D_FF], a[..., D_FF:]
    return (jax.nn.silu(gate) * val) @ w_down

def first_inputs(seed: int = 0) -> dict:
    key = jax.random.key(seed)
    ks = iter(jax.random.split(key, 48))

    def nrm(shape, scale):
        return jax.random.normal(next(ks), shape, jnp.float32) * scale

    def gain(shape):
        return 1.0 + nrm(shape, 0.05)

    L = DEPTH
    return {
        "x": nrm((BATCH, SEQ, D_MODEL), 1.0),
        "mem": nrm((BATCH, MEM_TOKENS, D_MODEL), 1.0),
        "mix_norm": gain((L, D_MODEL)),
        "w_in": nrm((L, D_MODEL, D_IN), D_MODEL ** -0.5),
        "mla_q_norm": gain((L, MLA_Q_RANK)),
        "mla_w_uq": nrm((L, MLA_Q_RANK, MLA_HEADS * (MLA_NOPE + MLA_ROPE)), MLA_Q_RANK ** -0.5),
        "mla_kv_norm": gain((L, MLA_KV_RANK)),
        "mla_w_ukv": nrm((L, MLA_KV_RANK, MLA_HEADS * (MLA_NOPE + MLA_V)), MLA_KV_RANK ** -0.5),
        "gqa_q_norm": gain((L, GQA_DIM)),
        "gqa_k_norm": gain((L, GQA_DIM)),
        "gmlp_v_norm": gain((L, W_C)),
        "gmlp_w_s": nrm((L, GMLP_GROUPS, GMLP_CHUNK, GMLP_CHUNK), GMLP_CHUNK ** -0.5),
        "gmlp_b_s": gain((L, GMLP_GROUPS, GMLP_CHUNK)),
        "out_norm": gain((L, D_MIX)),
        "w_out": nrm((L, D_MIX, D_MODEL), D_MIX ** -0.5),
        "mem_x_norm": gain((L, D_MODEL)),
        "mem_kv_norm": gain((L, D_MODEL)),
        "mem_w_q": nrm((L, D_MODEL, MEM_HEADS * MEM_DIM), D_MODEL ** -0.5),
        "mem_w_kv": nrm((L, D_MODEL, 2 * MEM_HEADS * MEM_DIM), D_MODEL ** -0.5),
        "mem_w_o": nrm((L, MEM_HEADS * MEM_DIM, D_MODEL), (MEM_HEADS * MEM_DIM) ** -0.5),
        "ffn_norm": gain((L, D_MODEL)),
        "ffn_w_up": nrm((L, D_MODEL, 2 * D_FF), D_MODEL ** -0.5),
        "ffn_conv_w": nrm((L, CONV_W, 2 * D_FF), CONV_W ** -0.5),
        "ffn_conv_b": nrm((L, 2 * D_FF), 0.01),
        "ffn_w_down": nrm((L, D_FF, D_MODEL), D_FF ** -0.5),
        "final_norm": gain((D_MODEL,)),
    }

def first_block(x, mem, mix_norm, w_in, mla_q_norm, mla_w_uq, mla_kv_norm, mla_w_ukv,
              gqa_q_norm, gqa_k_norm, gmlp_v_norm, gmlp_w_s, gmlp_b_s, out_norm, w_out,
              mem_x_norm, mem_kv_norm, mem_w_q, mem_w_kv, mem_w_o,
              ffn_norm, ffn_w_up, ffn_conv_w, ffn_conv_b, ffn_w_down, final_norm):
    S = x.shape[1]
    rope_a = axial_rope_table(S, MLA_ROPE)
    rope_b = axial_rope_table(S, GQA_DIM)
    for l in range(DEPTH):
        h = rms_norm(x, mix_norm[l])
        x = x + hybrid_mixer(h, rope_a, rope_b, w_in[l], mla_q_norm[l], mla_w_uq[l], mla_kv_norm[l],
                             mla_w_ukv[l], gqa_q_norm[l], gqa_k_norm[l], gmlp_v_norm[l], gmlp_w_s[l],
                             gmlp_b_s[l], out_norm[l], w_out[l])
        h = rms_norm(x, mem_x_norm[l])
        x = x + memory_cross_attention(h, mem, mem_kv_norm[l], mem_w_q[l], mem_w_kv[l], mem_w_o[l])
        h = rms_norm(x, ffn_norm[l])
        x = x + conv_gated_ffn(h, ffn_w_up[l], ffn_conv_w[l], ffn_conv_b[l], ffn_w_down[l])
    return rms_norm(x, final_norm)


CTX_LEN = 256
N_MOD = 9
NA_HEADS = 8
NA_HEAD_DIM = 64
NA_WIDTH = NA_HEADS * NA_HEAD_DIM
NA_KH = 8
NA_KW = 16
POOL_WINDOWS = (2, 4, 8, 16)
POOL_GROUPS = len(POOL_WINDOWS)
POOL_WIDTH = D_MODEL - NA_WIDTH
POOL_GROUP_DIM = POOL_WIDTH // POOL_GROUPS
EVEN_IN_WIDTH = 3 * NA_WIDTH + POOL_WIDTH
EVEN_MIX_WIDTH = NA_WIDTH + POOL_WIDTH
CONV_WIDTH = D_MODEL
CONV_K = 3
N_EVEN = (DEPTH + 1) // 2
N_ODD = DEPTH // 2
RMS_EPS = 1e-6
NEG_INF = -1e30


def rms_norm_2(x, g):
    x32 = x.astype(jnp.float32)
    y = x32 * lax.rsqrt(jnp.mean(x32 * x32, axis=-1, keepdims=True) + RMS_EPS)
    return (y * g.astype(jnp.float32)).astype(x.dtype)

def modulate(h, shift, scale):
    return h * (1 + scale) + shift

def adaln(cond, w, b):
    m = jax.nn.silu(cond) @ w + b
    return m.reshape(m.shape[:-1] + (N_MOD, D_MODEL))

def swiglu(h, w13, w2):
    a, b = jnp.split(h @ w13, 2, axis=-1)
    return (jax.nn.silu(a) * b) @ w2

def ffn_sublayer(h, m, g, w13, w2, base):
    hn = modulate(rms_norm_2(h, g), m[:, :, base], m[:, :, base + 1])
    return h + 0.5 * m[:, :, base + 2] * swiglu(hn, w13, w2)

def split_heads(t):
    return t.reshape(t.shape[:2] + (NA_HEADS, NA_HEAD_DIM))

def neighbourhood_attention(q, k, v, k_ctx, v_ctx, rpb):
    B, L, H, dh = q.shape
    R = L // GRID_W
    kh = min(NA_KH, R)
    kw = NA_KW
    scale = dh ** -0.5
    qg = q.reshape(B, R, GRID_W, H, dh)
    kg = k.reshape(B, R, GRID_W, H, dh)
    vg = v.reshape(B, R, GRID_W, H, dh)
    r = jnp.arange(R)
    row_start = jnp.clip(r - kh // 2, 0, R - kh)
    ridx = row_start[:, None] + jnp.arange(kh)[None, :]
    k_blk = kg[:, ridx]
    v_blk = vg[:, ridx]
    col = jnp.arange(GRID_W)
    col_start = jnp.clip(col - kw // 2, 0, GRID_W - kw)
    col_ok = (col[None, :] >= col_start[:, None]) & (col[None, :] < col_start[:, None] + kw)
    ri = ridx - r[:, None] + (NA_KH - 1)
    ci = jnp.clip(col[None, :] - col[:, None] + (NA_KW - 1), 0, 2 * NA_KW - 2)
    bias = rpb[:, ri[:, None, :, None], ci[None, :, None, :]].astype(jnp.float32)
    s_win = jnp.einsum('brqhd,brkwhd->bhrqkw', qg, k_blk).astype(jnp.float32) * scale + bias
    s_win = jnp.where(col_ok[:, None, :], s_win, NEG_INF)
    n_win = kh * GRID_W
    s_win = s_win.reshape(B, H, R, GRID_W, n_win)
    s_ctx = jnp.einsum('brqhd,bchd->bhrqc', qg, k_ctx).astype(jnp.float32) * scale
    p = jax.nn.softmax(jnp.concatenate([s_win, s_ctx], axis=-1), axis=-1).astype(v.dtype)
    p_win = p[..., :n_win].reshape(B, H, R, GRID_W, kh, GRID_W)
    o = (jnp.einsum('bhrqkw,brkwhd->brqhd', p_win, v_blk)
         + jnp.einsum('bhrqc,bchd->brqhd', p[..., n_win:], v_ctx))
    return o.reshape(B, L, H * dh)

def context_attention(q, k, v):
    B, C, H, dh = q.shape
    s = jnp.einsum('bqhd,bkhd->bhqk', q, k).astype(jnp.float32) * dh ** -0.5
    p = jax.nn.softmax(s, axis=-1).astype(v.dtype)
    return jnp.einsum('bhqk,bkhd->bqhd', p, v).reshape(B, C, H * dh)

def multiscale_pool(u, pool_w, pool_scale):
    B, L, _ = u.shape
    t = jnp.arange(L)
    ug = u.reshape(B, L, POOL_GROUPS, POOL_GROUP_DIM)
    outs = []
    for g, w in enumerate(POOL_WINDOWS):
        xg = ug[:, :, g].astype(jnp.float32)
        cs = jnp.pad(jnp.cumsum(xg, axis=1), ((0, 0), (1, 0), (0, 0)))
        lo = jnp.clip(t - w // 2, 0, L)
        hi = jnp.clip(t - w // 2 + w, 0, L)
        cnt = (hi - lo).astype(jnp.float32)[None, :, None]
        mean = (jnp.take(cs, hi, axis=1) - jnp.take(cs, lo, axis=1)) / cnt
        outs.append((mean - xg).astype(u.dtype) @ pool_w[g])
    return jnp.concatenate(outs, axis=-1) * pool_scale

def even_mixer(hl, hc, w_in, w_out, rpb, pool_w, pool_scale, ctx_out):
    q, k, v, u = jnp.split(hl @ w_in, [NA_WIDTH, 2 * NA_WIDTH, 3 * NA_WIDTH], axis=-1)
    k_c, v_c = jnp.split(hc @ w_in[:, NA_WIDTH:3 * NA_WIDTH], 2, axis=-1)
    k_c, v_c = split_heads(k_c), split_heads(v_c)
    att = neighbourhood_attention(split_heads(q), split_heads(k), split_heads(v), k_c, v_c, rpb)
    pool = multiscale_pool(u, pool_w, pool_scale)
    y_lat = jnp.concatenate([att, pool], axis=-1) @ w_out
    y_ctx = None
    if ctx_out:
        q_c = split_heads(hc @ w_in[:, :NA_WIDTH])
        u_c = hc @ w_in[:, 3 * NA_WIDTH:]
        att_c = context_attention(q_c, k_c, v_c)
        pool_c = multiscale_pool(u_c, pool_w, pool_scale)
        y_ctx = jnp.concatenate([att_c, pool_c], axis=-1) @ w_out
    return y_lat, y_ctx

def short_conv_mixer(h, w_in, conv_w, w_out):
    bg, cg, xin = jnp.split(h @ w_in, 3, axis=-1)
    z = cg * xin
    L = h.shape[1]
    zp = jnp.pad(z, ((0, 0), (1, 1), (0, 0)))
    y = zp[:, 0:L] * conv_w[0] + zp[:, 1:L + 1] * conv_w[1] + zp[:, 2:L + 2] * conv_w[2]
    return (bg * y) @ w_out

def second_inputs(seed: int = 0) -> dict:
    key = jax.random.key(seed)
    ks = jax.random.split(key, 18)
    D = D_MODEL

    def nrm(k, shape, s):
        return jax.random.normal(k, shape, jnp.float32) * s

    return {
        "x": nrm(ks[0], (BATCH, SEQ, D), 1.0),
        "c": nrm(ks[1], (BATCH, D), 1.0),
        "ctx": nrm(ks[2], (BATCH, CTX_LEN, D), 1.0),
        "c_ctx": nrm(ks[3], (D,), 1.0),
        "mod_w": nrm(ks[4], (DEPTH, D, N_MOD * D), 0.5 * D ** -0.5),
        "mod_b": nrm(ks[5], (DEPTH, N_MOD * D), 0.01),
        "norm_g": 1.0 + nrm(ks[6], (DEPTH, 3, D), 0.02),
        "ffn_w13": nrm(ks[7], (DEPTH, 2, D, 2 * D_FF), D ** -0.5),
        "ffn_w2": nrm(ks[8], (DEPTH, 2, D_FF, D), D_FF ** -0.5),
        "even_w_in": nrm(ks[9], (N_EVEN, D, EVEN_IN_WIDTH), D ** -0.5),
        "even_w_out": nrm(ks[10], (N_EVEN, EVEN_MIX_WIDTH, D), EVEN_MIX_WIDTH ** -0.5),
        "na_rpb": nrm(ks[11], (N_EVEN, NA_HEADS, 2 * NA_KH - 1, 2 * NA_KW - 1), 0.1),
        "pool_w": nrm(ks[12], (N_EVEN, POOL_GROUPS, POOL_GROUP_DIM, POOL_GROUP_DIM), POOL_GROUP_DIM ** -0.5),
        "pool_scale": 1.0 + nrm(ks[13], (N_EVEN, POOL_WIDTH), 0.1),
        "conv_w_in": nrm(ks[14], (N_ODD, D, 3 * CONV_WIDTH), D ** -0.5),
        "conv_w": nrm(ks[15], (N_ODD, CONV_K, CONV_WIDTH), CONV_K ** -0.5),
        "conv_w_out": nrm(ks[16], (N_ODD, CONV_WIDTH, D), CONV_WIDTH ** -0.5),
        "final_g": 1.0 + nrm(ks[17], (D,), 0.02),
    }

def second_block(x, c, ctx, c_ctx, mod_w, mod_b, norm_g, ffn_w13, ffn_w2, even_w_in, even_w_out,
              na_rpb, pool_w, pool_scale, conv_w_in, conv_w, conv_w_out, final_g):
    for i in range(DEPTH):
        even = (i % 2 == 0)
        ctx_out = any(j % 2 == 0 for j in range(i + 1, DEPTH))
        ctx_here = even or ctx_out
        m_l = adaln(c[:, None, :], mod_w[i], mod_b[i])
        m_c = adaln(c_ctx[None, None, :], mod_w[i], mod_b[i])

        x = ffn_sublayer(x, m_l, norm_g[i, 0], ffn_w13[i, 0], ffn_w2[i, 0], 0)
        if ctx_here:
            ctx = ffn_sublayer(ctx, m_c, norm_g[i, 0], ffn_w13[i, 0], ffn_w2[i, 0], 0)

        xn = modulate(rms_norm_2(x, norm_g[i, 1]), m_l[:, :, 3], m_l[:, :, 4])
        y_c = None
        if even:
            e = i // 2
            cn = modulate(rms_norm_2(ctx, norm_g[i, 1]), m_c[:, :, 3], m_c[:, :, 4])
            y_l, y_c = even_mixer(xn, cn, even_w_in[e], even_w_out[e], na_rpb[e],
                                  pool_w[e], pool_scale[e], ctx_out)
        else:
            o = i // 2
            y_l = short_conv_mixer(xn, conv_w_in[o], conv_w[o], conv_w_out[o])
            if ctx_out:
                cn = modulate(rms_norm_2(ctx, norm_g[i, 1]), m_c[:, :, 3], m_c[:, :, 4])
                y_c = short_conv_mixer(cn, conv_w_in[o], conv_w[o], conv_w_out[o])
        x = x + m_l[:, :, 5] * y_l

        x = ffn_sublayer(x, m_l, norm_g[i, 2], ffn_w13[i, 1], ffn_w2[i, 1], 6)
        if ctx_out:
            ctx = ctx + m_c[:, :, 5] * y_c
            ctx = ffn_sublayer(ctx, m_c, norm_g[i, 2], ffn_w13[i, 1], ffn_w2[i, 1], 6)

    return rms_norm_2(x, final_g)


def setup_inputs(seed=0):
    out = dict(first_inputs(seed))
    for name, value in second_inputs(seed + 1).items():
        if name != "x":
            out[name + "_2"] = value
    return out


def reference(
    x, mem, mix_norm, w_in, mla_q_norm, mla_w_uq, mla_kv_norm, mla_w_ukv, gqa_q_norm,
    gqa_k_norm, gmlp_v_norm, gmlp_w_s, gmlp_b_s, out_norm, w_out, mem_x_norm, mem_kv_norm,
    mem_w_q, mem_w_kv, mem_w_o, ffn_norm, ffn_w_up, ffn_conv_w, ffn_conv_b, ffn_w_down,
    final_norm, c_2, ctx_2, c_ctx_2, mod_w_2, mod_b_2, norm_g_2, ffn_w13_2, ffn_w2_2,
    even_w_in_2, even_w_out_2, na_rpb_2, pool_w_2, pool_scale_2, conv_w_in_2, conv_w_2,
    conv_w_out_2, final_g_2,
):
    x = first_block(
        x, mem, mix_norm, w_in, mla_q_norm, mla_w_uq, mla_kv_norm, mla_w_ukv, gqa_q_norm,
        gqa_k_norm, gmlp_v_norm, gmlp_w_s, gmlp_b_s, out_norm, w_out, mem_x_norm, mem_kv_norm,
        mem_w_q, mem_w_kv, mem_w_o, ffn_norm, ffn_w_up, ffn_conv_w, ffn_conv_b, ffn_w_down,
        final_norm,
    )
    return second_block(
        x, c_2, ctx_2, c_ctx_2, mod_w_2, mod_b_2, norm_g_2, ffn_w13_2, ffn_w2_2, even_w_in_2,
        even_w_out_2, na_rpb_2, pool_w_2, pool_scale_2, conv_w_in_2, conv_w_2, conv_w_out_2,
        final_g_2,
    )


_drawn_inputs = setup_inputs


def setup_inputs(seed=0):
    import zlib

    import numpy as np

    out = dict(_drawn_inputs(seed))
    spreads = {}
    factors = {'gmlp_v_norm': 2.925,
     'gmlp_b_s': 3.085,
     'mem_x_norm': 8.0,
     'mem_kv_norm': 6.295,
     'ffn_conv_b': 6.422,
     'mod_b_2': 3.265,
     'norm_g_2': 4.061,
     'na_rpb_2': 8.0,
     'pool_scale_2': 3.022,
     'final_g_2': 2.83}
    for name, (base, spread) in spreads.items():
        noise = np.random.default_rng([zlib.crc32(name.encode()), seed]).standard_normal(out[name].shape)
        drawn = base * np.exp(spread * noise) if base else spread * noise
        out[name] = jnp.asarray(drawn.astype(out[name].dtype))
    for name, factor in factors.items():
        out[name] = (out[name] * factor).astype(out[name].dtype)
    return out
```

```python
from contextlib import ExitStack

import numpy as np

import concourse.bass as bass
from concourse import mybir

F32 = mybir.dt.float32
F32R = mybir.dt.float32r
BF16 = mybir.dt.bfloat16
ALU = mybir.AluOpType
ACT = mybir.ActivationFunctionType
AXX = mybir.AxisListType.X

P, T, D, DEPTH = 128, 256, 1024, 2
KT = D // P
DFF = 2816
NF = DFF // P
NG = NF // 2
TPB = 16
RAW, RING, MODRING = 3, 3, 2
LOOPS = (NG - 1) // 2
PERIT = 6
NMOD = 9 * KT
FFNS = ["f0", "f1", "ctx", "x0a", "x0b", "x1a", "x1b"]
MODS_PER_IT = {"f0": 8, "f1": 6, "ctx": 6, "x0a": 4, "x0b": 4}
MODS_AFTER = {"f1": 2, "x0b": 2}
MOD_START = {"f0": 0, "f1": 40, "ctx": 72, "x0a": 102, "x0b": 122}
NMODC = 5 * KT



def stage_sizes():
    out = []
    for l in range(DEPTH):
        out += [(f"in{l}", 88), (f"vv{l}", 16), (f"uq{l}", 12), (f"nope{l}", 3), (f"va{l}", 3), (f"pad{l}", 6),
                (f"out{l}", 64), (f"mk{l}", 32), (f"mv{l}", 32), (f"mq{l}", 32), (f"mo{l}", 32), (f"f{l}", 33 * TPB)]
    out += [("ctx", 33 * TPB), ("x0a", 33 * TPB), ("ck", 32), ("cv", 64 - 32), ("eq", 32), ("ek", 32), ("ev", 32), ("eu", 32),
            ("pool", 4), ("padp", 12), ("eo", 64), ("x0b", 33 * TPB), ("x1a", 33 * TPB),
            ("cin", 192), ("co", 64), ("x1b", 33 * TPB)]
    return out


P0, _p = {}, 0
for _name, _n in stage_sizes():
    P0[_name] = _p
    _p += _n
assert _p % TPB == 0
NBLK = _p // TPB



def output_counts():
    out = []
    for l in range(DEPTH):
        out += [(f"in{l}", 11), (f"vv{l}", 2), (f"gvt{l}", 1), (f"krot{l}", 1), (f"mix{l}", 1), (f"uq{l}", 6), (f"nope{l}", 3),
                (f"va{l}", 2), (f"gqrot{l}", 2), (f"qrot{l}", 3), (f"att{l}", 12), (f"out{l}", 8), (f"mk{l}", 4),
                (f"mv{l}", 4), (f"mq{l}", 4), (f"matt{l}", 4), (f"mo{l}", 8)]
    out += [("ck", 4), ("cv", 4), ("eq", 4), ("ek", 4), ("ev", 4), ("eu", 4), ("pooled", 4), ("pool", 4), ("natt", 8),
            ("eo", 8), ("cin", 24), ("co", 8)]
    return out


O0, _o = {}, 0
for _name, _n in output_counts():
    O0[_name] = _o
    _o += _n

BLOCK_END, FULL_COUNT = {}, {}
_full = [0] * 4
for _name, _n in output_counts():
    _stage = _name.rstrip("01") if _name[-1] in "01" else _name
    for _j in range(_n):
        _end = None
        if _stage in ("mv", "cv", "ev", "eu"):
            _end = P0[_name] + 16 * (_j // 2 + 1) if _j % 2 else None
        elif _stage in ("in", "out", "mk", "mq", "ck", "eq", "ek", "eo", "cin", "co"):
            _end = P0[_name] + KT * (_j + 1)
        elif _stage == "uq":
            _end = P0[_name] + 2 * (_j + 1)
        elif _stage == "mo":
            _end = P0[_name] + 4 * (_j + 1)
        if _end is not None and _end % TPB == 0:
            BLOCK_END[O0[_name] + _j] = _end // TPB
        else:
            _full[(O0[_name] + _j) % 4] += 1
            FULL_COUNT[O0[_name] + _j] = _full[(O0[_name] + _j) % 4]

NORMS = []
for _l in range(DEPTH):
    NORMS += [(f"mix{_l}", 8, ((0, 8, D),)), (f"c{_l}", 3, ((0, 1, 128), (1, 3, 256))),
              (f"y{_l}", 8, ((0, 3, 384), (3, 6, 384), (6, 8, 256))),
              (f"mem{_l}", 8, ((0, 8, D),)), (f"memx{_l}", 8, ((0, 8, D),)), (f"my{_l}", 4, None), (f"f{_l}", 8, ((0, 8, D),))]
NORMS += [("mid", 8, ((0, 8, D),)), ("ctx", 8, ((0, 8, D),)), ("x0a", 8, ((0, 8, D),)), ("cn", 8, ((0, 8, D),)), ("xn", 8, ((0, 8, D),)),
          ("ey", 8, None), ("x0b", 8, ((0, 8, D),)), ("x1a", 8, ((0, 8, D),)), ("x1n", 8, ((0, 8, D),)), ("oy", 8, None),
          ("x1b", 8, ((0, 8, D),)), ("final", 8, ((0, 8, D),))]
NK, NSUMS, NTILES = {}, {}, {}
_k = _s = _t = 0
for _name, _n, _g in NORMS:
    NK[_name], NSUMS[_name], NTILES[_name] = _k, _s, _t
    _k, _s, _t = _k + 1, _s + (_g is not None), _t + (0 if _name == "mid" else _n)

PCOL, _c = {}, 0
for _name, _n in ([(f"{a}{l}", n) for l in range(DEPTH) for a, n in (
        ("mix", 8), ("c", 3), ("gq", 1), ("gk", 1), ("y", 8), ("mem", 8), ("memx", 8), ("f", 8), ("conv", 4 * 2 * NF))]
        + [(f"ng{i}{j}", 8) for i in range(DEPTH) for j in range(3)]
        + [("ps", 4), ("cw", 24), ("mid", 8), ("final", 8), ("mb0", NMOD), ("mb1", NMOD)]):
    PCOL[_name] = _c
    _c += _n
NPAR = _c

CCOL, _c = {}, 0
for _name, _n in (("ident", 128), ("ones", 128), ("bd", 128), ("rot", 128), ("ck", 256), ("sk", 256), ("cg", 256),
                  ("sg", 256), ("eps", 1), ("mask", 64)):
    CCOL[_name] = _c
    _c += _n
NCON = _c

A_QM, A_KM, A_VM, A_QB, A_VB, A_C, A_KP, A_GV, A_U, A_VV, A_RT = 0, 1536, 3072, 3840, 4864, 5120, 5888, 6144, 6400, 6912, 7424
A_MK, A_MV, A_MQ = 0, 1024, 2048
A_Q, A_KL, A_KC, A_VL, A_VC, A_UT, A_BP = 0, 1024, 2048, 3072, 4096, 5120, 6144
A_CG, A_CV = 0, 512
A_Z, A_ZC = 0, 256
NAR = 8192


NAV = 5


def EV(l, what):
    return NAV * l + {"c": 1, "gv": 2, "uq": 3, "va": 4, "mq": 5, "eu": 1, "ps": 2}[what]


def YV(what, j=0):
    return 4 * DEPTH + {"pool_lo": j + 1, "natt": 5, "eo": 6, "cin": 7 + j, "co": 15}[what]


def GX(ffn):
    return 4 if ffn in ("x0b", "x1a", "x1b") else 0


class Chain:

    def __init__(self, eng, sem):
        self.eng, self.sem, self.n, self.i, self.per = eng, sem, 0, None, 0

    def value(self):
        return self.n if self.i is None else self.n + self.i * self.per

    def link(self, ins):
        self.n += 1
        ins.then_inc(self.sem, 1)
        self.eng.wait_ge(self.sem, self.value())

    def enter(self, i, per):
        self.i, self.per, self.start = i, per, self.n

    def leave(self, trips):
        assert self.n - self.start == self.per, (self.n - self.start, self.per)
        self.n = self.start + self.per * trips
        self.i = None


def two_blocks(nc, stream, modstream, x, mem, ctxin, crow, ccrow, params, consts, smallw, smallb, smallg, bpool, rpb, out):
    es = ExitStack()
    with es:
        def sb(name, shape, dt=F32):
            return es.enter_context(nc.sbuf_tensor(name, shape, dt))

        def sem(name):
            return es.enter_context(nc.semaphore(name))

        wraw = sb("wraw", [P, RAW, 2048])
        whi = sb("whi", [P, RING, 2048], F32R)
        wlo = sb("wlo", [P, RING, 2048], F32R)
        modw = sb("modw", [P, MODRING, D])
        cb = sb("cb", [P, 2, D])
        X = sb("X", [P, KT, T])
        CX = sb("CX", [P, KT, T])
        Hh = sb("Hh", [P, KT, T], F32R)
        Hl = sb("Hl", [P, KT, T], F32R)
        NS = sb("NS", [P, 2, KT, T])
        SQ, TN = NS[:, 0], NS[:, 1]
        Gh = sb("Gh", [P, 4, T], F32R)
        Gl = sb("Gl", [P, 4, T], F32R)
        Y = sb("Y", [P, KT, T])
        PR = sb("PR", [P, 2, 512])
        PT = sb("PT", [P, 4, T])
        STD = PT
        AR = sb("AR", [P, NAR])
        SW = sb("SW", [P, 1024])
        CON = sb("CON", [P, NCON])
        PAR = sb("PAR", [P, NPAR])
        ZB = sb("ZB", [P, 512], BF16)
        GS = sb("GS", [P, 8])
        HG = sb("HG", [P, 8])
        MODL = sb("MODL", [P, DEPTH * NMOD])
        MODC = sb("MODC", [P, NMODC])
        MSC = sb("MSC", [P, 2, 8])
        NM = sb("NM", [P, 4])
        SM = sb("SM", [P, 4])
        RI = sb("RI", [P, 4])
        VS = sb("VS", [P, 6])

        bank = [es.enter_context(nc.psum_tensor(f"bank{b}", [P, 512], F32)) for b in range(8)]

        raw_loaded = [sem(f"raw_loaded{s}") for s in range(RAW)]
        mod_loaded = [sem(f"mod_loaded{s}") for s in range(MODRING)]
        hi_ready, lo_ready, w_used, mod_used = sem("hi_ready"), sem("lo_ready"), sem("w_used"), sem("mod_used")
        full = [sem(f"psum_full{b}") for b in range(4)]
        free = [sem(f"psum_free{b}") for b in range(4)]
        act_step, dve_step = sem("act_step"), sem("dve_step")
        n_sq, n_sum, n_std, n_app, n_hi, n_lo = (sem(s) for s in (
            "norm_squared", "norm_summed", "norm_deviation", "norm_applied", "norm_hi", "norm_lo"))
        gain_ready = sem("gain_ready")
        up_free, affine, silu_done, gate_out, g_hi, g_lo = (sem(s) for s in (
            "up_read", "conv_centre", "silu_done", "gate_out", "g_hi", "g_lo"))
        down_read = sem("down_read")
        s_full, max_ready, exp_done, prob_ready, pt_full, pt_copied = (sem(s) for s in (
            "scores_full", "max_ready", "exp_done", "prob_ready", "pt_full", "pt_copied"))
        const_in, par_in, x_in, mem_in, ctx_in, c_in, sw_in, bp_in, bias_in, out_done = (sem(s) for s in (
            "const_in", "par_in", "x_in", "mem_in", "ctx_in", "c_in", "sw_in", "bp_in", "bias_in", "out_done"))
        c_silu, zeros_ready = sem("c_silu"), sem("zeros_ready")
        evac, qk_std, vv_std, vv_ready, kp_raw, y_half, qk_norm, rope_in = (sem(s) for s in (
            "act_evacuated", "qk_deviation", "vv_deviation", "vv_normed", "kp_raw", "dve_evacuated", "qk_normed", "roped"))
        qk_sq, qk_sum, cx_free, mixed_done, ubuf, out_ready, z_copy, mask_done = (sem(s) for s in (
            "qk_squared", "qk_summed", "context_buffer_free", "spatial_mixed", "u_read", "result_ready", "cg_copied",
            "bias_masked"))

        def con(name, n=128):
            return CON[:, CCOL[name]:CCOL[name] + n]

        def par(name, j=0, n=1):
            return PAR[:, PCOL[name] + j:PCOL[name] + j + n]

        def ar(off, n, w=T):
            return AR[:, off:off + n * w].rearrange("p (n w) -> p n w", w=w)

        def backwards(v):
            return v.rearrange("p (r c) -> p r c", r=4)[:, :, ::-1]

        def obank(o):
            return bank[4 + o % 4]

        def wait_full(eng, o):
            if o in BLOCK_END:
                eng.wait_ge(w_used, BLOCK_END[o])
            else:
                eng.wait_ge(full[o % 4], FULL_COUNT[o])

        ident, ones, bdiag, rot = con("ident"), con("ones"), con("bd"), con("rot")
        eps = con("eps", 1)
        KBUF = {"h": (Hh, Hl), "g": (Gh, Gl)}

        def gain(name, t):
            if name in MODULATED:
                return GS[:, t:t + 1]
            return par(name, t)

        MODULATED = {"ctx": (MODC, 0, 0, "ng00"), "x0a": (MODL, 0, 0, "ng00"), "cn": (MODC, 0, 3, "ng01"),
                     "xn": (MODL, 0, 3, "ng01"), "x0b": (MODL, 0, 6, "ng02"), "x1a": (MODL, NMOD, 0, "ng10"),
                     "x1n": (MODL, NMOD, 3, "ng11"), "x1b": (MODL, NMOD, 6, "ng12")}
        MODORD = {n: i for i, n in enumerate(["ctx", "x0a", "cn", "xn", "x0b", "x1a", "x1n", "x1b"])}

        def shift(name, t):
            m, base, j, _ = MODULATED[name]
            return m[:, base + j * 8 + t:base + j * 8 + t + 1]

        def source(name):
            if name.startswith("c") and name[1:].isdigit():
                return ar(A_C, 3)
            if name.startswith("y") or name.startswith("my") or name in ("ey", "oy"):
                return Y[:, :, :]
            if (name.startswith("mem") and not name.startswith("memx")) or name in ("ctx", "cn"):
                return CX[:, :, :]
            return X[:, :, :]

        def target(name):
            return KBUF["g"] if name.startswith("c") and name[1:].isdigit() else KBUF["h"]

        NINFO = {n: (t, g) for n, t, g in NORMS}
        FI = {n: i for i, n in enumerate(FFNS)}

        block = es.enter_context(nc.Block())

        @block.sync
        def _(sp):
            sp.dma_start(X[:, :, :], x).then_inc(x_in, 16)
            sp.dma_start(CON[:, :], consts).then_inc(const_in, 16)
            sp.dma_start(PAR[:, :], params).then_inc(par_in, 16)
            loaded = 0

            def load(n, i=None, step=0):
                if n >= RAW or i is not None:
                    sp.wait_ge(lo_ready, n - RAW + 1 if i is None else i * PERIT + (n - RAW + 1))
                src = stream[n] if i is None else stream[bass.ds(i * PERIT + n, 1)].rearrange("o p f -> (o p) f")
                sp.dma_start(wraw[:, n % RAW, :], src).then_inc(raw_loaded[n % RAW], 16)

            def load_mod(u, i=None, per=0):
                sp.wait_ge(mod_used, u + 1 if i is None else i * per + (u + 1))
                src = modstream[u] if i is None else modstream[bass.ds(i * per + u, 1)].rearrange("o p f -> (o p) f")
                sp.dma_start(modw[:, u % MODRING, :], src).then_inc(mod_loaded[u % MODRING], 16)

            for f in FFNS:
                b0 = P0[f] // TPB
                for n in range(loaded, b0 + 4):
                    load(n)
                per = MODS_PER_IT.get(f, 0)
                with sp.Fori(0, LOOPS) as i:
                    for c in range(2):
                        for k in range(3):
                            load(b0 + 4 + 3 * c + k, i)
                        for k in range(per // 2):
                            load_mod(MOD_START[f] + per // 2 * c + k, i, per)
                for k in range(MODS_AFTER.get(f, 0)):
                    load_mod(MOD_START[f] + per * LOOPS + k)
                loaded = b0 + 34
            sp.wait_ge(out_ready, 1)
            sp.dma_start(out, SQ).then_inc(out_done, 16)
            sp.wait_ge(out_done, 16)

        @block.gpsimd
        def _(pool):
            pool.dma_start(CX[:, :, :], mem).then_inc(mem_in, 16)
            pool.dma_start(cb[:, 0, :], crow.partition_broadcast(P)).then_inc(c_in, 16)
            pool.dma_start(cb[:, 1, :], ccrow.partition_broadcast(P)).then_inc(c_in, 16)
            for l in range(DEPTH):
                if l:
                    pool.wait_ge(mixed_done, l)
                pool.dma_start(SW[:, 0:512], smallw[l]).then_inc(sw_in, 16)
                pool.dma_start(SW[:, 512:768], smallg[l].partition_broadcast(P)).then_inc(sw_in, 16)
                for g in range(4):
                    r = 64 * (g % 2)
                    pool.dma_start(SW[r:r + 64, 768 + 128 * (g // 2):896 + 128 * (g // 2)],
                                   smallb[l, g].partition_broadcast(64)).then_inc(sw_in, 16)
            pool.wait_ge(n_hi, NTILES["mem1"] + 8)
            pool.wait_ge(n_app, NSUMS["mem1"] + 1)
            pool.dma_start(CX[:, :, :], ctxin).then_inc(ctx_in, 16)
            pool.wait_ge(n_lo, NTILES["f1"] + 8)
            pool.dma_start(AR[:, A_BP:A_BP + 2048], bpool).then_inc(bp_in, 16)
            pool.wait_ge(n_lo, NTILES["xn"] + 8)
            pool.wait_ge(n_hi, NTILES["xn"] + 8)
            for t in range(2):
                for r in range(2):
                    for h in range(8):
                        src = bass.AP(tensor=rpb.tensor, offset=h * 15 * 128 + (7 - (2 * t + r)) * 128,
                                      ap=[[1, 64], [128, 4], [1, 64]])
                        dst = NS[64 * r:64 * r + 64].rearrange("p a k t -> p (a k) t")[:, 2 * h + t, :] \
                            .rearrange("p (a b) -> p a b", a=4)
                        pool.dma_start(dst, src).then_inc(bias_in, 16)

        @block.tensor
        def _(pe):
            state = {"block": -1}

            def open_block(n, i=None):
                pe.wait_ge(lo_ready, n + 1 if i is None else i * PERIT + (n + 1))

            def tile_at(p, w=1):
                c = (p % TPB) * P
                return whi[:, (p // TPB) % RING, c:c + w * P], wlo[:, (p // TPB) % RING, c:c + w * P]

            def need(p):
                if p // TPB != state["block"]:
                    assert p // TPB == state["block"] + 1
                    state["block"] = p // TPB
                    open_block(p // TPB)

            def three(outp, whl, ahl, start, stop, flip=False, skip=False):
                last = None
                for j, (a, b) in enumerate(((0, 0), (0, 1), (1, 0))):
                    st, en = start and j == 0, stop and j == 2
                    lhs, rhs = (ahl[b], whl[a]) if flip else (whl[a], ahl[b])
                    last = pe.matmul(outp, lhs, rhs, start=st, stop=en, skip_group_check=skip)
                return last

            def claim(o):
                if o // 4 > 0:
                    pe.wait_ge(free[o % 4], o // 4)

            def wait_h(name, k):
                pe.wait_ge(n_lo, NTILES[name] + k + 1)

            def feature(stage, name, outs, kt, src="h", k0=0, first=0, p=None, o=None):
                hh, hl = KBUF[src]
                p = P0[stage] if p is None else p
                o = O0[stage] if o is None else o
                for m in range(outs):
                    claim(o)
                    for k in range(kt):
                        need(p)
                        if m == 0 and name:
                            wait_h(name, k0 + k)
                        last = three(obank(o)[:, 0:T], tile_at(p), (hh[:, k0 + k, :], hl[:, k0 + k, :]), k == 0, k == kt - 1)
                        p += 1
                        if p % TPB == 0 and k < kt - 1:
                            last.then_inc(w_used, 1)
                    last.then_inc(w_used if p % TPB == 0 else full[o % 4], 1)
                    o += 1

            def tokens(stage, name, kt, w, src="h", k0=0, p=None, o=None):
                hh, hl = KBUF[src]
                p = P0[stage] if p is None else p
                o = O0[stage] if o is None else o
                for tt in range(2):
                    claim(o + tt)
                for k in range(kt):
                    need(p)
                    if name:
                        wait_h(name, k0 + k)
                    for tt in range(2):
                        s = slice(tt * P, tt * P + P)
                        last = three(obank(o + tt)[:, 0:w * P], tile_at(p, w),
                                     (hh[:, k0 + k, s], hl[:, k0 + k, s]), k == 0, k == kt - 1, flip=True)
                        if k == kt - 1 and tt == 0:
                            last.then_inc(full[(o + tt) % 4], 1)
                    p += w
                    if p % TPB == 0 and k < kt - 1:
                        last.then_inc(w_used, 1)
                last.then_inc(w_used if p % TPB == 0 else full[(o + 1) % 4], 1)

            def norm_sum(name):
                n, groups = NINFO[name]
                pe.wait_ge(n_sq, NSUMS[name] + 1)
                for g, (a, b, _) in enumerate(groups):
                    for t in range(a, b):
                        last = pe.matmul(bank[g // 2][:, T * (g % 2):T * (g % 2) + T], ones, SQ[:, t, :],
                                         start=(t == a), stop=(t == b - 1))
                last.then_inc(n_sum, 1)

            def skip_pad(p):
                last = pe.matmul(bank[0][:, 0:P], ZB[:, 0:P], ZB[:, 0:P], start=True, stop=True)
                last.then_inc(w_used, 1)

            def attention(h0, n, o0, keys, single, q_of, k_of, v_of, place):
                nk = keys // P

                def scores(a):
                    h = h0 + a
                    wait = h if single else h - 1
                    if wait > 0:
                        pe.wait_ge(exp_done, wait)
                    for qt in range(2):
                        for kk in range(keys // T):
                            b = bank[qt][:, kk * T:kk * T + T] if single else bank[h % 2][:, qt * T:qt * T + T]
                            last = pe.matmul(b, q_of(a)[:, qt * P:qt * P + P], k_of(a, kk), start=True, stop=True)
                    last.then_inc(s_full, 1)

                def transposes(a):
                    h = h0 + a
                    pe.wait_ge(prob_ready, h + 1)
                    wait = h if single else h - 1
                    if wait > 0:
                        pe.wait_ge(pt_copied, wait)
                    for qt in range(2):
                        for k in range(nk):
                            b = bank[2 + k // 2][:, (k % 2) * T + qt * P:(k % 2) * T + qt * P + P] if single else \
                                bank[2 + h % 2][:, k * T + qt * P:k * T + qt * P + P]
                            src = PR[:, qt, k * P:k * P + P] if single else PR[:, h % 2, qt * T + k * P:qt * T + k * P + P]
                            last = pe.transpose(b, src, ident)
                    last.then_inc(pt_full, 1)

                def values(a):
                    h, o = h0 + a, o0 + a
                    pe.wait_ge(pt_copied, h + 1)
                    claim(o)
                    r0, r1 = place(a)
                    for k in range(nk):
                        pt = PT[:, k, :] if single else PT[:, 2 * (h % 2) + k, :]
                        last = pe.matmul(obank(o)[r0:r1, 0:T], v_of(a, k), pt, start=(k == 0), stop=(k == nk - 1))
                    last.then_inc(full[o % 4], 1)

                for a in range(n + 2):
                    if a < n:
                        scores(a)
                    if 1 <= a <= n:
                        transposes(a - 1)
                    if a >= 2:
                        values(a - 2)

            def ffn(name):
                f, b0 = FI[name], P0[name] // TPB
                pe.wait_ge(n_std, NSUMS[name] + 1)
                for b in range(4):
                    pe.matmul(bank[b][:, :], ZB[:, 0:P], ZB[:, :], start=True, stop=False, skip_group_check=True)

                def up(g2, n, i, gval):
                    pe.wait_ge(up_free, gval)
                    for half in range(2):
                        open_block(n + half, i)
                        for ft in range(2):
                            for k in range(KT):
                                if i is None and half == 0 and ft == 0:
                                    wait_h(name, k)
                                last = three(bank[4 + 2 * g2 + half][:, ft * T:ft * T + T],
                                             tile_at((n + half) * TPB + ft * KT + k), (Hh[:, k, :], Hl[:, k, :]),
                                             k == 0, k == KT - 1)
                        last.then_inc(w_used, 1)

                def down(g2, n, i, gval, final=False):
                    open_block(n, i)
                    pe.wait_ge(g_lo, gval)
                    for ft in range(2):
                        for m in range(KT):
                            last = three(bank[m // 2][:, T * (m % 2):T * (m % 2) + T], tile_at(n * TPB + ft * KT + m),
                                         (Gh[:, 2 * g2 + ft, :], Gl[:, 2 * g2 + ft, :]), False, final and ft == 1, skip=True)
                    last.then_inc(w_used, 1)

                up(0, b0, None, NG * f + 1)
                with pe.Fori(0, LOOPS) as i:
                    for c in range(2):
                        n = b0 + 2 + 3 * c
                        up((1 + c) % 2, n, i, i * 2 + (NG * f + c + 1))
                        down(c % 2, n + 2, i, i * 2 + (NG * f + c + 1))
                down(0, b0 + 32, None, NG * f + NG, final=True)
                state["block"] = b0 + 32

            pe.wait_ge(const_in, 16)
            pe.wait_ge(zeros_ready, 1)
            for l in range(DEPTH):
                QM, KM, VM = ar(A_QM, 6), ar(A_KM, 6), ar(A_VM, 2, 384)
                QB, VB, GV, VV, KP = ar(A_QB, 4), ar(A_VB, 2, 128), ar(A_GV, 1), ar(A_VV, 2), ar(A_KP, 1)
                norm_sum(f"mix{l}")
                feature(f"in{l}", f"mix{l}", 7, KT)
                norm_sum(f"c{l}")
                feature(f"in{l}", None, 4, KT, p=P0[f"in{l}"] + 56, o=O0[f"in{l}"] + 7)
                tokens(f"vv{l}", None, KT, 2)
                o = O0[f"gvt{l}"]
                claim(o)
                pe.wait_ge(evac, EV(l, "gv"))
                for tt in range(2):
                    last = pe.transpose(obank(o)[:, tt * P:tt * P + P], GV[:, 0, tt * P:tt * P + P], ident)
                last.then_inc(full[o % 4], 1)
                o = O0[f"krot{l}"]
                claim(o)
                pe.matmul(obank(o)[:, 0:T], rot, KP[:, 0, :], start=True, stop=True).then_inc(full[o % 4], 1)
                pe.wait_ge(qk_sq, l + 1)
                for j in range(2):
                    last = pe.matmul(bank[2 + j][:, :], bdiag,
                                     SQ[:, 4 + 2 * j:6 + 2 * j, :].rearrange("p a t -> p (a t)"), start=True, stop=True)
                last.then_inc(qk_sum, 1)
                o = O0[f"mix{l}"]
                claim(o)
                pe.wait_ge(vv_ready, l + 1)
                pe.wait_ge(sw_in, 96 * (l + 1))
                for n in range(2):
                    for g in range(4):
                        last = pe.matmul(obank(o)[64 * (g % 2):64 * (g % 2) + 64, (g // 2) * T + n * P:(g // 2) * T + n * P + P],
                                         VV[:, n, g * 64:g * 64 + 64], SW[:, g * P:g * P + P], start=True, stop=True)
                last.then_inc(full[o % 4], 1)
                feature(f"uq{l}", f"c{l}", 6, 2, src="g", k0=1)
                feature(f"nope{l}", f"c{l}", 3, 1, src="g", k0=0)
                tokens(f"va{l}", None, 1, 3, src="g", k0=0)
                skip_pad(None)
                pe.wait_ge(qk_norm, l + 1)
                for j in range(2):
                    o = O0[f"gqrot{l}"] + j
                    claim(o)
                    pe.matmul(obank(o)[:, :], rot, QB[:, 2 * j:2 * j + 2, :].rearrange("p a t -> p (a t)"),
                              start=True, stop=True).then_inc(full[o % 4], 1)
                pe.wait_ge(evac, EV(l, "uq"))
                for j in range(3):
                    o = O0[f"qrot{l}"] + j
                    claim(o)
                    pe.matmul(obank(o)[:, :], rot, QM[:, 2 * j:2 * j + 2, :].rearrange("p a t -> p (a t)"),
                              start=True, stop=True).then_inc(full[o % 4], 1)
                pe.wait_ge(rope_in, l + 1)
                pe.wait_ge(evac, EV(l, "va"))

                def qh(a):
                    if a < 6:
                        return QM[:, a, :]
                    b = a - 6
                    return QB[64 * (b // 3):64 * (b // 3) + 64, b % 3, :]

                def kh(a, kk):
                    if a < 6:
                        return KM[:, a, :]
                    b = a - 6
                    return QB[64 * (b // 3):64 * (b // 3) + 64, 3, :]

                def vh(a, k):
                    if a < 6:
                        return VM[:, k, 64 * a:64 * a + 64]
                    b = a - 6
                    return VB[:, k, 64 * (b // 3):64 * (b // 3) + 64]

                def row(a):
                    r = 64 * (a % 2) if a < 6 else 64 * ((a - 6) // 3)
                    return r, r + 64

                attention(16 * l, 12, O0[f"att{l}"], T, False, qh, kh, vh, row)
                norm_sum(f"y{l}")
                feature(f"out{l}", f"y{l}", 8, KT)
                norm_sum(f"mem{l}")
                feature(f"mk{l}", f"mem{l}", 4, KT)
                tokens(f"mv{l}", None, KT, 2)
                tokens(f"mv{l}", None, KT, 2, p=P0[f"mv{l}"] + 16, o=O0[f"mv{l}"] + 2)
                norm_sum(f"memx{l}")
                feature(f"mq{l}", f"memx{l}", 4, KT)
                pe.wait_ge(evac, EV(l, "mq"))
                MK, MV, MQ = ar(A_MK, 4), ar(A_MV, 2, 512), ar(A_MQ, 4)
                attention(16 * l + 12, 4, O0[f"matt{l}"], T, False, lambda a: MQ[:, a, :], lambda a, kk: MK[:, a, :],
                          lambda a, k: MV[:, k, P * a:P * a + P], lambda a: (0, P))
                feature(f"mo{l}", f"my{l}", 8, 4)
                norm_sum(f"f{l}")
                ffn(f"f{l}")
            norm_sum("mid")
            for name in ("ctx", "x0a"):
                norm_sum(name)
                ffn(name)
            norm_sum("cn")
            feature("ck", "cn", 4, KT)
            tokens("cv", None, KT, 2)
            tokens("cv", None, KT, 2, p=P0["cv"] + 16, o=O0["cv"] + 2)
            norm_sum("xn")
            feature("eq", "xn", 4, KT)
            feature("ek", None, 4, KT)
            for s in ("ev", "eu"):
                tokens(s, None, KT, 2)
                tokens(s, None, KT, 2, p=P0[s] + 16, o=O0[s] + 2)
            pe.wait_ge(evac, EV(2, "eu"))
            pe.wait_ge(bp_in, 16)
            UT, BP = ar(A_UT, 2, 512), AR[:, A_BP:A_BP + 2048].rearrange("p (g s t) -> p g s t", g=4, s=2)
            for g in range(4):
                o = O0["pooled"] + g
                claim(o)
                for s in range(2):
                    last = pe.matmul(obank(o)[:, 0:T], UT[:, s, g * P:g * P + P], BP[:, g, s, :], start=(s == 0), stop=(s == 1))
                last.then_inc(full[o % 4], 1)
            p = P0["pool"]
            for g in range(4):
                o = O0["pool"] + g
                claim(o)
                need(p)
                pe.wait_ge(y_half, YV("pool_lo", g))
                three(obank(o)[:, 0:T], tile_at(p), (Gh[:, g, :], Gl[:, g, :]), True, True).then_inc(full[o % 4], 1)
                p += 1
            skip_pad(None)
            Q, KL, KC = ar(A_Q, 4), ar(A_KL, 4), ar(A_KC, 4)
            VL, VC = ar(A_VL, 2, 512), ar(A_VC, 2, 512)

            def half(a):
                return slice(64 * (a % 2), 64 * (a % 2) + 64)

            attention(32, 8, O0["natt"], 512, True, lambda a: Q[half(a), a // 2, :],
                      lambda a, kk: (KL if kk == 0 else KC)[half(a), a // 2, :],
                      lambda a, k: (VL if k < 2 else VC)[:, k % 2, 64 * a:64 * a + 64],
                      lambda a: (64 * (a % 2), 64 * (a % 2) + 64))
            feature("eo", "ey", 8, KT)
            norm_sum("x0b")
            ffn("x0b")
            norm_sum("x1a")
            ffn("x1a")
            norm_sum("x1n")
            feature("cin", "x1n", 24, KT)
            feature("co", "oy", 8, KT)
            norm_sum("x1b")
            ffn("x1b")
            norm_sum("final")

        @block.scalar
        def _(act):
            chain = Chain(act, act_step)
            st = {"hi": 0, "ev": 0}

            def split_hi(n, i=None):
                slot = n % RAW
                loads = 16 * (n // RAW + 1)
                act.wait_ge(raw_loaded[slot], loads if i is None else i * (16 * PERIT // RAW) + loads)
                if n >= RING:
                    act.wait_ge(w_used, n - RING + 1 if i is None else i * PERIT + (n - RING + 1))
                act.activation(whi[:, n % RING, :], wraw[:, slot, :], ACT.Copy).then_inc(hi_ready, 1)

            def hi_upto(n):
                while st["hi"] <= min(n, NBLK):
                    split_hi(st["hi"])
                    st["hi"] += 1

            def source_ready(name):
                marks = {"ey": YV("natt"), "oy": YV("cin", KT - 1), "x0b": YV("eo"), "x1b": YV("co")}
                for l in range(DEPTH):
                    marks.update({f"y{l}": 4 * l + 1, f"memx{l}": 4 * l + 2, f"my{l}": 4 * l + 3, f"f{l}": 4 * l + 4})
                if name in marks:
                    act.wait_ge(y_half, marks[name])

            def norm(name):
                n, groups = NINFO[name]
                if groups:
                    norm_square(name)
                    norm_rest(name)
                else:
                    plain_hi(name)

            def norm_square(name):
                n, groups = NINFO[name]
                src = source(name)
                source_ready(name)
                if NTILES[name]:
                    act.wait_ge(n_lo, NTILES[name])
                act.activation(SQ[:, 0:n, :], src[:, 0:n, :], ACT.Square).then_inc(n_sq, 1)

            def norm_rest(name):
                n, groups = NINFO[name]
                hh, _ = target(name)
                k = NSUMS[name]
                act.wait_ge(n_sum, k + 1)
                for g, (a, b, width) in enumerate(groups):
                    last = act.activation(STD[:, g, :], bank[g // 2][:, T * (g % 2):T * (g % 2) + T], ACT.Sqrt,
                                          bias=eps, scale=1.0 / width)
                last.then_inc(n_std, 1)
                act.wait_ge(n_app, k + 1)
                if name in ("mid", "final"):
                    return
                if name in MODULATED:
                    act.wait_ge(gain_ready, MODORD[name] + 1)
                for t in range(n):
                    if name in MODULATED:
                        act.activation(hh[:, t, :], TN[:, t, :], ACT.Identity, bias=shift(name, t),
                                       scale=gain(name, t)).then_inc(n_hi, 1)
                    else:
                        act.activation(hh[:, t, :], TN[:, t, :], ACT.Copy, scale=gain(name, t)).then_inc(n_hi, 1)

            def plain_hi(name):
                n, _ = NINFO[name]
                hh, _ = target(name)
                source_ready(name)
                for t in range(n):
                    act.activation(hh[:, t, :], Y[:, t, :], ACT.Copy).then_inc(n_hi, 1)

            def evacuate(dst, src, o, block_, func=ACT.Copy, scale=1.0, **kw):
                if block_ is not None:
                    hi_upto(block_ + 2)
                wait_full(act, o)
                act.activation(dst, src, func, scale=scale, **kw).then_inc(free[o % 4], 1)

            def mark():
                st["ev"] += 1
                act.copy(VS[:, 5:6], eps).then_inc(evac, 1)
                act.wait_ge(evac, st["ev"])

            def blk(stage, tiles):
                return (P0[stage] + tiles - 1) // TPB

            def attend(h0, n, o0, keys, single):
                nk = keys // P
                for a in range(n + 1):
                    if a < n:
                        h = h0 + a
                        act.wait_ge(max_ready, h + 1)
                        wait = h if single else h - 1
                        if wait > 0:
                            act.wait_ge(pt_full, wait)
                        for qt in range(2):
                            src = bank[qt][:, :] if single else bank[h % 2][:, qt * T:qt * T + T]
                            dst = PR[:, qt, :] if single else PR[:, h % 2, qt * T:qt * T + T]
                            c = 2 * (h % 2) + qt
                            last = act.activation(dst, src, ACT.Exp, bias=NM[:, c:c + 1], scale=1.0,
                                                  accum_out=SM[:, c:c + 1])
                        last.then_inc(exp_done, 1)
                    if a >= 1:
                        h, o = h0 + a - 1, o0 + a - 1
                        back = 1 if single else 2
                        if a - 1 >= back:
                            wait_full(act, o - back)
                        act.wait_ge(pt_full, h + 1)
                        if single:
                            for j in range(2):
                                last = act.activation(PT[:, 2 * j:2 * j + 2, :].rearrange("p a t -> p (a t)"),
                                                      bank[2 + j][:, :], ACT.Copy)
                        else:
                            last = act.activation(PT[:, 2 * (h % 2):2 * (h % 2) + 2, :].rearrange("p a t -> p (a t)"),
                                                  bank[2 + h % 2][:, :], ACT.Copy)
                        last.then_inc(pt_copied, 1)

            def ffn(name):
                f, b0 = FI[name], P0[name] // TPB
                conv = name in ("f0", "f1")
                hi_upto(b0 + 3)

                def group(g2, cnt, i, gs, n):
                    def at(m):
                        return cnt + m if i is None else i * 2 + (cnt + m)
                    act.wait_ge(w_used, n + 2 if i is None else i * PERIT + (n + 2))
                    gb, vb = bank[4 + 2 * g2], bank[5 + 2 * g2]
                    if conv:
                        if f or gs:
                            act.wait_ge(g_lo, at(0))
                        for part, (b, buf) in enumerate(((gb, A_CG), (vb, A_CV))):
                            for ft in range(2):
                                col = PCOL[f"conv{f}"] + 4 * (NF * part + ft) + 8 * gs
                                if i is None:
                                    w, bb = PAR[:, col + 1:col + 2], PAR[:, col + 3:col + 4]
                                else:
                                    w, bb = PAR[:, bass.ds(i * 16 + (col + 1), 1)], PAR[:, bass.ds(i * 16 + (col + 3), 1)]
                                last = act.activation(AR[:, buf + ft * T:buf + ft * T + T], b[:, ft * T:ft * T + T],
                                                      ACT.Identity, bias=bb, scale=w)
                        last.then_inc(affine, 1)
                    else:
                        act.wait_ge(up_free, at(1))
                        act.activation(AR[:, A_CG:A_CG + 512], gb[:, :], ACT.Silu).then_inc(silu_done, 1)

                def group_end(g2, cnt, i):
                    def at(m):
                        return cnt + m if i is None else i * 2 + (cnt + m)
                    if conv:
                        act.wait_ge(up_free, at(2))
                        act.activation(AR[:, A_CG:A_CG + 512], AR[:, A_CG:A_CG + 512], ACT.Silu).then_inc(silu_done, 1)
                        act.wait_ge(gate_out, at(1))
                    else:
                        act.wait_ge(up_free, at(2))
                    act.activation(Gh[:, 2 * g2:2 * g2 + 2, :].rearrange("p a t -> p (a t)"), AR[:, A_CV:A_CV + 512],
                                   ACT.Copy).then_inc(g_hi, 1)

                group(0, NG * f, None, 0, b0)
                group_end(0, NG * f, None)
                assert st["hi"] == b0 + 4
                with act.Fori(0, LOOPS) as i:
                    for c in range(2):
                        n0 = b0 + 2 + 3 * c
                        split_hi(n0 + 2, i)
                        split_hi(n0 + 3, i)
                        group((1 + c) % 2, NG * f + 1 + c, i, 1 + c, n0)
                        split_hi(n0 + 4, i)
                        group_end((1 + c) % 2, NG * f + 1 + c, i)
                st["hi"] = b0 + 34
                hi_upto(b0 + 35)
                act.wait_ge(down_read, f + 1)

            act.wait_ge(c_in, 32)
            act.activation(cb[:, :, :], cb[:, :, :], ACT.Silu).then_inc(c_silu, 1)
            act.wait_ge(const_in, 16)
            act.wait_ge(par_in, 16)
            act.wait_ge(x_in, 16)
            hi_upto(2)
            for l in range(DEPTH):
                QM, KM, VM, QB, VB = ar(A_QM, 6), ar(A_KM, 6), ar(A_VM, 2, 384), ar(A_QB, 4), ar(A_VB, 2, 128)
                C, KP, GV, U, VV = ar(A_C, 3), ar(A_KP, 1), ar(A_GV, 1), ar(A_U, 2), ar(A_VV, 2)
                norm(f"mix{l}")
                o, s = O0[f"in{l}"], f"in{l}"
                for m in range(3):
                    evacuate(C[:, m, :], obank(o + m)[:, 0:T], o + m, blk(s, 8 * m + 8))
                evacuate(KP[:, 0, :], obank(o + 3)[:, 0:T], o + 3, blk(s, 32))
                mark()
                norm_square(f"c{l}")
                for m in range(3):
                    evacuate(QB[:, m, :], obank(o + 4 + m)[:, 0:T], o + 4 + m, blk(s, 8 * m + 40))
                norm_rest(f"c{l}")
                evacuate(QB[:, 3, :], obank(o + 7)[:, 0:T], o + 7, blk(s, 64))
                evacuate(GV[:, 0, :], obank(o + 8)[:, 0:T], o + 8, blk(s, 72))
                for m in range(2):
                    evacuate(U[:, m, :], obank(o + 9 + m)[:, 0:T], o + 9 + m, blk(s, 80 + 8 * m), ACT.Gelu_apprx_tanh)
                for tt in range(2):
                    o = O0[f"vv{l}"] + tt
                    evacuate(VV[:, tt, :], obank(o)[:, 0:T], o, blk(f"vv{l}", 16), ACT.Gelu_apprx_tanh)
                mark()
                for tt in range(2):
                    act.activation(TN[:, 6 + tt, :], VV[:, tt, :], ACT.Square, accum_out=VS[:, tt:tt + 1])
                act.activation(SQ[:, 4:8, :], QB[:, 0:4, :], ACT.Square).then_inc(qk_sq, 1)
                act.wait_ge(qk_sq, l + 1)
                act.activation(VS[:, 2:4], VS[:, 0:2], ACT.Sqrt, bias=eps, scale=1.0 / 256).then_inc(vv_std, 1)
                act.wait_ge(qk_sum, l + 1)
                act.wait_ge(n_lo, NTILES[f"c{l}"] + 3)
                for j in range(2):
                    last = act.activation(STD[:, 2 * j:2 * j + 2, :].rearrange("p a t -> p (a t)"), bank[2 + j][:, :],
                                          ACT.Sqrt, bias=eps, scale=1.0 / 64)
                last.then_inc(qk_std, 1)
                o = O0[f"gvt{l}"]
                evacuate(VB[:, :, :].rearrange("p a t -> p (a t)"), obank(o)[:, 0:T], o, None)
                for m in range(6):
                    o = O0[f"uq{l}"] + m
                    evacuate(QM[:, m, :], obank(o)[:, 0:T], o, blk(f"uq{l}", 2 * m + 2), scale=96.0 ** -0.5)
                mark()
                for m in range(3):
                    o = O0[f"nope{l}"] + m
                    hi_upto(blk(f"nope{l}", m + 1) + 2)
                    wait_full(act, o)
                    act.activation(KM[0:64, 2 * m, :], obank(o)[0:64, 0:T], ACT.Copy)
                    act.activation(KM[64:128, 2 * m + 1, :], obank(o)[64:128, 0:T], ACT.Copy).then_inc(free[o % 4], 1)
                for tt in range(2):
                    o = O0[f"va{l}"] + tt
                    evacuate(VM[:, tt, :], obank(o)[:, 0:384], o, blk(f"va{l}", 3))
                mark()
                hi_upto(blk(f"pad{l}", 6) + 3)
                attend(16 * l, 12, O0[f"att{l}"], T, False)
                norm(f"y{l}")
                for m in range(8):
                    hi_upto(blk(f"out{l}", 8 * m + 8) + 2)
                hi_upto(blk(f"out{l}", 64) + 3)
                if l == 0:
                    act.wait_ge(mem_in, 16)
                norm(f"mem{l}")
                MK, MV, MQ = ar(A_MK, 4), ar(A_MV, 2, 512), ar(A_MQ, 4)
                for m in range(4):
                    o = O0[f"mk{l}"] + m
                    evacuate(MK[:, m, :], obank(o)[:, 0:T], o, blk(f"mk{l}", 8 * m + 8))
                for j in range(4):
                    o = O0[f"mv{l}"] + j
                    evacuate(MV[:, j % 2, T * (j // 2):T * (j // 2) + T], obank(o)[:, 0:T], o, blk(f"mv{l}", 16 * (j // 2) + 16))
                hi_upto(blk(f"mv{l}", 32) + 3)
                norm(f"memx{l}")
                for m in range(4):
                    o = O0[f"mq{l}"] + m
                    evacuate(MQ[:, m, :], obank(o)[:, 0:T], o, blk(f"mq{l}", 8 * m + 8), scale=128.0 ** -0.5)
                mark()
                hi_upto(blk(f"mq{l}", 32) + 3)
                attend(16 * l + 12, 4, O0[f"matt{l}"], T, False)
                norm(f"my{l}")
                hi_upto(blk(f"mo{l}", 16) + 2)
                hi_upto(blk(f"mo{l}", 32) + 3)
                norm(f"f{l}")
                ffn(f"f{l}")
            norm("mid")
            act.wait_ge(ctx_in, 16)
            norm("ctx")
            ffn("ctx")
            norm("x0a")
            ffn("x0a")
            norm("cn")
            Q, KL, KC, VL, VC, UT = ar(A_Q, 4), ar(A_KL, 4), ar(A_KC, 4), ar(A_VL, 2, 512), ar(A_VC, 2, 512), ar(A_UT, 2, 512)

            def feat(stage, buf, scale=1.0, order=lambda v: v):
                for m in range(4):
                    o = O0[stage] + m
                    src = obank(o)[:, 0:T] if order is not backwards else obank(o)[:, 0:T].rearrange("p (r c) -> p r c", r=4)
                    evacuate(order(buf[:, m, :]), src, o, blk(stage, 8 * m + 8), scale=scale)

            def tok(stage, buf):
                for j in range(4):
                    o = O0[stage] + j
                    evacuate(buf[:, j % 2, T * (j // 2):T * (j // 2) + T], obank(o)[:, 0:T], o, blk(stage, 16 * (j // 2) + 16))

            feat("ck", KC)
            tok("cv", VC)
            hi_upto(blk("cv", 32) + 3)
            norm("xn")
            feat("eq", Q, 0.125, backwards)
            feat("ek", KL)
            tok("ev", VL)
            tok("eu", UT)
            mark()
            for g in range(4):
                o = O0["pooled"] + g
                wait_full(act, o)
                act.activation(Gh[:, g, :], obank(o)[:, 0:T], ACT.Copy).then_inc(g_hi, 1)
                hi_upto(blk("pool", 4) + 2)
            for g in range(4):
                o = O0["pool"] + g
                wait_full(act, o)
                act.activation(Y[:, 4 + g, :], obank(o)[:, 0:T], ACT.Copy, scale=par("ps", g)).then_inc(free[o % 4], 1)
            mark()
            hi_upto(blk("padp", 12) + 3)
            attend(32, 8, O0["natt"], 512, True)
            norm("ey")
            for m in range(8):
                hi_upto(blk("eo", 8 * m + 8) + 2)
            hi_upto(blk("eo", 64) + 3)
            norm("x0b")
            ffn("x0b")
            norm("x1a")
            ffn("x1a")
            norm("x1n")
            for t in range(KT):
                o = O0["cin"] + 3 * t + 1
                if t:
                    act.wait_ge(y_half, YV("cin", t - 1))
                hi_upto(blk("cin", 24 * t + 16) + 2)
                wait_full(act, o)
                act.activation(AR[:, A_CG:A_CG + T], obank(o)[:, 0:T], ACT.Copy).then_inc(z_copy, 1)
                hi_upto(blk("cin", 24 * t + 24) + 2)
            hi_upto(blk("cin", 192) + 3)
            norm("oy")
            for m in range(8):
                hi_upto(blk("co", 8 * m + 8) + 2)
            hi_upto(blk("co", 64) + 3)
            norm("x1b")
            ffn("x1b")
            norm("final")

        @block.vector
        def _(dve):
            chain = Chain(dve, dve_step)
            link = chain.link
            st = {"lo": 0, "y": 0}
            fl = lambda v: v.rearrange("p a t -> p (a t)")

            def split_lo(n, i=None):
                dve.wait_ge(hi_ready, n + 1 if i is None else i * PERIT + (n + 1))
                dve.tensor_tensor(wlo[:, n % RING, :], wraw[:, n % RAW, :], whi[:, n % RING, :].bitcast(F32),
                                  ALU.subtract).then_inc(lo_ready, 1)

            def lo_upto(n):
                while st["lo"] <= min(n, NBLK):
                    split_lo(st["lo"])
                    st["lo"] += 1

            def blk(stage, tiles):
                return (P0[stage] + tiles - 1) // TPB

            def norm(name):
                n, groups = NINFO[name]
                src, (hh, hl) = source(name), target(name)
                k = NSUMS[name]
                if groups:
                    if name in MODULATED:
                        modulated_gain(name)
                    dve.wait_ge(n_std, k + 1)
                    ng = len(groups)
                    link(dve.reciprocal(STD[:, 0:ng, :], STD[:, 0:ng, :]))
                    for g, (a, b, _) in enumerate(groups):
                        last = dve.tensor_tensor(TN[:, a:b, :], src[:, a:b, :],
                                                 STD[:, g:g + 1, :].to_broadcast([P, b - a, T]), ALU.mult)
                    last.then_inc(n_app, 1)
                    dve.wait_ge(n_app, k + 1)
                    if name == "mid":
                        for t in range(n):
                            last = dve.tensor_scalar(X[:, t, :], TN[:, t, :], gain(name, t), None, ALU.mult)
                        link(last)
                        return
                    for t in range(n):
                        if name in MODULATED:
                            last = dve.tensor_scalar(SQ[:, t, :], TN[:, t, :], gain(name, t), shift(name, t), ALU.mult, ALU.add)
                        else:
                            last = dve.tensor_scalar(SQ[:, t, :], TN[:, t, :], gain(name, t), None, ALU.mult)
                    if name == "final":
                        last.then_inc(out_ready, 1)
                        return
                    link(last)
                    exact = SQ
                else:
                    exact = Y
                for t in range(n):
                    dve.wait_ge(n_hi, NTILES[name] + t + 1)
                    dve.tensor_tensor(hl[:, t, :], exact[:, t, :], hh[:, t, :].bitcast(F32), ALU.subtract).then_inc(n_lo, 1)

            def modulated_gain(name):
                m, base, j, g = MODULATED[name]
                link(dve.scalar_tensor_tensor(GS[:, :], m[:, base + 8 * (j + 1):base + 8 * (j + 2)], 1.0, par(g, 0, 8),
                                              ALU.add, ALU.mult))
                dve.tensor_scalar(HG[:, :], m[:, base + 8 * (j + 2):base + 8 * (j + 3)] if name != "cn" else GS[:, :],
                                  1.0 if j == 3 else 0.5, None, ALU.mult).then_inc(gain_ready, 1)

            def attend(h0, n, o0, keys, single, put, bias=None):
                for a in range(n + 2):
                    if a < n:
                        h = h0 + a
                        dve.wait_ge(s_full, h + 1)
                        c = 2 * (h % 2)
                        if bias is not None:
                            for qt in range(2):
                                last = dve.tensor_tensor(bank[qt][:, 0:T], bank[qt][:, 0:T], bias(a, qt), ALU.add)
                            link(last)
                        if h >= 2:
                            dve.wait_ge(exp_done, h - 1)
                        if single:
                            for qt in range(2):
                                last = dve.tensor_reduce(NM[:, c + qt:c + qt + 1], bank[qt][:, :], AXX, ALU.max, negate=True)
                            last.then_inc(max_ready, 1)
                        else:
                            dve.tensor_reduce(NM[:, c:c + 2], bank[h % 2][:, :].rearrange("p (q k) -> p q k", q=2), AXX,
                                              ALU.max, negate=True).then_inc(max_ready, 1)
                        dve.wait_ge(exp_done, h + 1)
                        link(dve.reciprocal(RI[:, c:c + 2], SM[:, c:c + 2]))
                        for qt in range(2):
                            p = PR[:, qt, :] if single else PR[:, h % 2, qt * T:qt * T + T]
                            last = dve.tensor_scalar(p, p, RI[:, c + qt:c + qt + 1], None, ALU.mult)
                        last.then_inc(prob_ready, 1)
                    if a >= 2:
                        o = o0 + a - 2
                        wait_full(dve, o)
                        dst, rows = put(a - 2)
                        src = obank(o)[rows, 0:T]
                        if single:
                            dst, src = backwards(dst), src.rearrange("p (r c) -> p r c", r=4)
                        dve.tensor_copy(dst, src).then_inc(free[o % 4], 1)
                done()

            def done():
                st["y"] += 1
                dve.tensor_copy(VS[:, 4:5], eps).then_inc(y_half, 1)
                dve.wait_ge(y_half, st["y"])

            def ffn(name):
                f, b0 = FI[name], P0[name] // TPB
                conv = name in ("f0", "f1")
                l = 0 if name == "f0" else 1
                per = MODS_PER_IT.get(name, 0)
                lo_upto(b0 + 3)

                def group(g2, cnt, i, gs):
                    def at(m):
                        return cnt + m if i is None else i * 2 + (cnt + m)
                    gb, vb = bank[4 + 2 * g2], bank[5 + 2 * g2]
                    if conv:
                        dve.wait_ge(affine, at(1))
                        for tap, (d0, s0) in ((0, (1, 0)), (2, (0, 1))):
                            for part, (b, buf) in enumerate(((gb, A_CG), (vb, A_CV))):
                                for ft in range(2):
                                    col = PCOL[f"conv{l}"] + 4 * (NF * part + ft) + tap + 8 * gs
                                    w = PAR[:, col:col + 1] if i is None else PAR[:, bass.ds(i * 16 + col, 1)]
                                    dst = AR[:, buf + ft * T + d0:buf + ft * T + d0 + T - 1]
                                    last = dve.scalar_tensor_tensor(dst, b[:, ft * T + s0:ft * T + s0 + T - 1], w, dst,
                                                                    ALU.mult, ALU.add)
                            if tap == 0:
                                link(last)
                        last.then_inc(up_free, 1)

                def product(g2, cnt, i, gs):
                    def at(m):
                        return cnt + m if i is None else i * 2 + (cnt + m)
                    vb = bank[5 + 2 * g2]
                    dve.wait_ge(silu_done, at(1))
                    if conv:
                        dve.tensor_tensor(AR[:, A_CV:A_CV + 512], AR[:, A_CG:A_CG + 512], AR[:, A_CV:A_CV + 512],
                                          ALU.mult).then_inc(gate_out, 1)
                    else:
                        dve.wait_ge(g_lo, at(0))
                        dve.tensor_tensor(AR[:, A_CV:A_CV + 512], AR[:, A_CG:A_CG + 512], vb[:, :],
                                          ALU.mult).then_inc(up_free, 1)

                def low(g2, cnt, i):
                    dve.wait_ge(g_hi, GX(name) + cnt + 1 if i is None else i * 2 + (GX(name) + cnt + 1))
                    dve.tensor_tensor(fl(Gl[:, 2 * g2:2 * g2 + 2, :]), AR[:, A_CV:A_CV + 512],
                                      fl(Gh[:, 2 * g2:2 * g2 + 2, :]).bitcast(F32), ALU.subtract).then_inc(g_lo, 1)

                def mods(u, count, i):
                    for k in range(count):
                        uu = u + k
                        ld = 16 * (uu // MODRING + 1)
                        dve.wait_ge(mod_loaded[uu % MODRING], ld if i is None else i * (16 * per // MODRING) + ld)
                        slot = modw[:, uu % MODRING, :]
                        sc = PR[:, :, :].rearrange("p a k -> p (a k)")
                        if name == "f0":
                            dve.wait_ge(mod_used, uu + MODRING if i is None else i * per + (uu + MODRING))
                            dve.tensor_tensor_reduce(sc, slot, cb[:, 1, :], 1.0, 0.0, ALU.mult, ALU.add, MSC[:, 1, k:k + 1])
                        dve.tensor_tensor_reduce(slot, slot, cb[:, 0, :], 1.0, 0.0, ALU.mult, ALU.add,
                                                 MSC[:, 0, k:k + 1]).then_inc(mod_used, 1)
                    dve.wait_ge(mod_used, u + count + MODRING if i is None else i * per + (u + count + MODRING))
                    if i is None:
                        link(dve.tensor_copy(MODL[:, u:u + count], MSC[:, 0, 0:count]))
                    else:
                        if name == "f0":
                            dve.tensor_copy(MODC[:, bass.ds(i * per + u, count)], MSC[:, 1, 0:count])
                        link(dve.tensor_copy(MODL[:, bass.ds(i * per + u, count)], MSC[:, 0, 0:count]))

                group(0, NG * f, None, 0)
                product(0, NG * f, None, 0)
                low(0, NG * f, None)
                with dve.Fori(0, LOOPS) as i:
                    chain.enter(i, (2 if conv else 0) + (2 if per else 0))
                    for c in range(2):
                        n0 = b0 + 2 + 3 * c
                        g2 = (1 + c) % 2
                        split_lo(n0 + 2, i)
                        split_lo(n0 + 3, i)
                        group(g2, NG * f + 1 + c, i, 1 + c)
                        if not conv:
                            product(g2, NG * f + 1 + c, i, 1 + c)
                        split_lo(n0 + 4, i)
                        if conv:
                            product(g2, NG * f + 1 + c, i, 1 + c)
                        low(g2, NG * f + 1 + c, i)
                        if per:
                            mods(MOD_START[name] + per // 2 * c, per // 2, i)
                    chain.leave(LOOPS)
                st["lo"] = b0 + 34
                if name in MODS_AFTER:
                    mods(MOD_START[name] + per * LOOPS, MODS_AFTER[name], None)
                if name == "f1":
                    dve.tensor_tensor(MODC[:, :], MODC[:, :], par("mb0", 0, NMODC), ALU.add)
                    link(dve.tensor_tensor(MODL[:, 0:NMOD], MODL[:, 0:NMOD], par("mb0", 0, NMOD), ALU.add))
                if name == "x0b":
                    link(dve.tensor_tensor(MODL[:, NMOD:2 * NMOD], MODL[:, NMOD:2 * NMOD], par("mb1", 0, NMOD), ALU.add))
                lo_upto(b0 + 35)
                res = CX if name == "ctx" else X
                dve.wait_ge(w_used, b0 + 33)
                for m in range(KT):
                    b = bank[m // 2][:, T * (m % 2):T * (m % 2) + T]
                    if conv:
                        last = dve.tensor_tensor(res[:, m, :], res[:, m, :], b, ALU.add)
                    else:
                        last = dve.scalar_tensor_tensor(res[:, m, :], b, HG[:, m:m + 1], res[:, m, :], ALU.mult, ALU.add)
                last.then_inc(down_read, 1)
                dve.wait_ge(down_read, f + 1)

            def residual(stage, kt, gated=False):
                for m in range(KT):
                    o = O0[stage] + m
                    lo_upto(blk(stage, kt * m + kt) + 2)
                    wait_full(dve, o)
                    b = obank(o)[:, 0:T]
                    if gated:
                        dve.scalar_tensor_tensor(X[:, m, :], b, HG[:, m:m + 1], X[:, m, :], ALU.mult,
                                                 ALU.add).then_inc(free[o % 4], 1)
                    else:
                        dve.tensor_tensor(X[:, m, :], X[:, m, :], b, ALU.add).then_inc(free[o % 4], 1)
                lo_upto(blk(stage, kt * KT) + 3)
                done()

            dve.memset(VS[:, 0:1], 0.0).then_inc(up_free, 1)
            for j in range(MODRING):
                dve.memset(VS[:, 1 + j:2 + j], 0.0).then_inc(mod_used, 1)
            dve.memset(ZB[:, :], 0.0).then_inc(zeros_ready, 1)
            dve.wait_ge(const_in, 16)
            dve.wait_ge(par_in, 16)
            dve.wait_ge(c_silu, 1)
            dve.wait_ge(x_in, 16)
            lo_upto(2)
            for l in range(DEPTH):
                QM, KM, QB = ar(A_QM, 6), ar(A_KM, 6), ar(A_QB, 4)
                KP, U, VV, RT = ar(A_KP, 1), ar(A_U, 2), ar(A_VV, 2), ar(A_RT, 2)
                norm(f"mix{l}")
                lo_upto(blk(f"in{l}", 56) + 2)
                norm(f"c{l}")
                lo_upto(blk(f"in{l}", 88) + 2)
                lo_upto(blk(f"vv{l}", 16) + 2)
                dve.wait_ge(vv_std, l + 1)
                link(dve.reciprocal(VS[:, 2:4], VS[:, 2:4]))
                dve.wait_ge(sw_in, 96 * (l + 1))
                for tt in range(2):
                    last = dve.scalar_tensor_tensor(VV[:, tt, :], VV[:, tt, :], VS[:, 2 + tt:3 + tt], SW[:, 512:768],
                                                    ALU.mult, ALU.mult)
                last.then_inc(vv_ready, 1)
                o = O0[f"krot{l}"]
                wait_full(dve, o)
                link(dve.tensor_tensor(RT[:, 0, :], obank(o)[:, 0:T], con("sk", T), ALU.mult))
                dve.nop().then_inc(free[o % 4], 1)
                link(dve.tensor_tensor(KP[:, 0, :], KP[:, 0, :], con("ck", T), ALU.mult))
                for par_, r in ((0, slice(64, 128)), (1, slice(0, 64))):
                    last = dve.tensor_tensor(KM[r, par_:6:2, :], KP[r, 0:1, :].to_broadcast([64, 3, T]),
                                             RT[r, 0:1, :].to_broadcast([64, 3, T]), ALU.add)
                link(last)
                dve.wait_ge(qk_std, l + 1)
                link(dve.reciprocal(STD[:, :, :], STD[:, :, :]))
                link(dve.tensor_tensor(QB[:, :, :], QB[:, :, :], STD[:, :, :], ALU.mult))
                dve.tensor_scalar(QB[:, 0:3, :], QB[:, 0:3, :], par(f"gq{l}"), 0.125, ALU.mult, ALU.mult)
                dve.tensor_scalar(QB[:, 3, :], QB[:, 3, :], par(f"gk{l}"), None, ALU.mult).then_inc(qk_norm, 1)
                o = O0[f"mix{l}"]
                wait_full(dve, o)
                MX = obank(o)[:, :].rearrange("p (g n t) -> p g n t", g=2, n=2)
                YC = Y[:, 6:8, :].rearrange("p g (n t) -> p g n t", n=2)
                BS = SW[:, 768:1024].rearrange("p (g t) -> p g t", g=2)
                for n in range(2):
                    last = dve.tensor_tensor(YC[:, :, n, :], MX[:, :, n, :], BS, ALU.add)
                link(last)
                dve.nop().then_inc(free[o % 4], 1)
                dve.tensor_tensor(Y[:, 6:8, :], Y[:, 6:8, :], U[:, :, :], ALU.mult).then_inc(mixed_done, 1)
                lo_upto(blk(f"uq{l}", 12) + 2)
                lo_upto(blk(f"pad{l}", 6) + 2)
                dve.wait_ge(mixed_done, l + 1)
                dve.wait_ge(qk_norm, l + 1)
                for j in range(2):
                    o = O0[f"gqrot{l}"] + j
                    wait_full(dve, o)
                    link(dve.tensor_tensor(RT[:, :, :], obank(o)[:, :].rearrange("p (a t) -> p a t", a=2),
                                           con("sg", T)[:, None, :].to_broadcast([P, 2, T]), ALU.mult))
                    dve.nop().then_inc(free[o % 4], 1)
                    q = QB[:, 2 * j:2 * j + 2, :]
                    link(dve.tensor_tensor(q, q, con("cg", T)[:, None, :].to_broadcast([P, 2, T]), ALU.mult))
                    link(dve.tensor_tensor(q, q, RT[:, :, :], ALU.add))
                for j in range(3):
                    o = O0[f"qrot{l}"] + j
                    wait_full(dve, o)
                    for e, r in ((0, slice(64, 128)), (1, slice(0, 64))):
                        last = dve.tensor_tensor(RT[r, e, :], obank(o)[r, e * T:e * T + T], con("sk", T)[r, :], ALU.mult)
                    link(last)
                    dve.nop().then_inc(free[o % 4], 1)
                    for e, r in ((0, slice(64, 128)), (1, slice(0, 64))):
                        last = dve.tensor_tensor(QM[r, 2 * j + e, :], QM[r, 2 * j + e, :], con("ck", T)[r, :], ALU.mult)
                    link(last)
                    for e, r in ((0, slice(64, 128)), (1, slice(0, 64))):
                        last = dve.tensor_tensor(QM[r, 2 * j + e, :], QM[r, 2 * j + e, :], RT[r, e, :], ALU.add)
                    link(last)
                dve.nop().then_inc(rope_in, 1)
                lo_upto(blk(f"pad{l}", 6) + 3)

                def put(a):
                    if a < 6:
                        r = slice(64 * (a % 2), 64 * (a % 2) + 64)
                        return Y[r, a // 2, :], r
                    b = a - 6
                    r = slice(64 * (b // 3), 64 * (b // 3) + 64)
                    return Y[r, 3 + b % 3, :], r

                attend(16 * l, 12, O0[f"att{l}"], T, False, put)
                norm(f"y{l}")
                residual(f"out{l}", 8)
                norm(f"mem{l}")
                lo_upto(blk(f"mk{l}", 32) + 2)
                lo_upto(blk(f"mv{l}", 32) + 3)
                norm(f"memx{l}")
                lo_upto(blk(f"mq{l}", 32) + 3)
                attend(16 * l + 12, 4, O0[f"matt{l}"], T, False, lambda a: (Y[:, a, :], slice(0, P)))
                norm(f"my{l}")
                residual(f"mo{l}", 4)
                norm(f"f{l}")
                ffn(f"f{l}")
            norm("mid")
            dve.wait_ge(ctx_in, 16)
            norm("ctx")
            ffn("ctx")
            norm("x0a")
            ffn("x0a")
            norm("cn")
            lo_upto(blk("ck", 32) + 2)
            lo_upto(blk("cv", 32) + 3)
            norm("xn")
            for s in ("eq", "ek", "ev", "eu"):
                lo_upto(blk(s, 32) + 2)
            for g in range(4):
                o = O0["pooled"] + g
                dve.wait_ge(g_hi, NG * 4 + g + 1)
                dve.tensor_tensor(Gl[:, g, :], obank(o)[:, 0:T], Gh[:, g, :].bitcast(F32), ALU.subtract).then_inc(free[o % 4], 1)
                done()
            lo_upto(blk("pool", 4) + 2)
            dve.wait_ge(bias_in, 16 * 32)
            link(dve.tensor_tensor(NS[:, :, :, :].rearrange("p a k (r c) -> p (a k r) c", c=64),
                                   NS[:, :, :, :].rearrange("p a k (r c) -> p (a k r) c", c=64),
                                   con("mask", 64)[:, None, :].to_broadcast([P, 64, 64]), ALU.add))
            lo_upto(blk("padp", 12) + 3)
            BI = NS[:, :, :, :].rearrange("p a k t -> p (a k) t")
            attend(32, 8, O0["natt"], 512, True,
                   lambda a: (Y[64 * (a % 2):64 * (a % 2) + 64, a // 2, :], slice(64 * (a % 2), 64 * (a % 2) + 64)),
                   bias=lambda a, qt: BI[:, 2 * a + qt, :])
            dve.wait_ge(evac, EV(2, "ps"))
            norm("ey")
            residual("eo", 8, gated=True)
            norm("x0b")
            ffn("x0b")
            norm("x1a")
            ffn("x1a")
            norm("x1n")
            for t in range(KT):
                ob, oc, ox = (O0["cin"] + 3 * t + j for j in range(3))
                lo_upto(blk("cin", 24 * t + 24) + 2)
                dve.wait_ge(z_copy, t + 1)
                dve.nop().then_inc(free[oc % 4], 1)
                wait_full(dve, ox)
                z, zc, cg = AR[:, 512:512 + T], AR[:, 1024:1024 + T], AR[:, A_CG:A_CG + T]
                link(dve.tensor_tensor(z, cg, obank(ox)[:, 0:T], ALU.mult))
                dve.nop().then_inc(free[ox % 4], 1)
                link(dve.tensor_scalar(zc, z, par("cw", 8 + t), None, ALU.mult))
                link(dve.scalar_tensor_tensor(zc[:, 1:T], z[:, 0:T - 1], par("cw", t), zc[:, 1:T], ALU.mult, ALU.add))
                link(dve.scalar_tensor_tensor(zc[:, 0:T - 1], z[:, 1:T], par("cw", 16 + t), zc[:, 0:T - 1], ALU.mult, ALU.add))
                wait_full(dve, ob)
                link(dve.tensor_tensor(Y[:, t, :], zc, obank(ob)[:, 0:T], ALU.mult))
                dve.nop().then_inc(free[ob % 4], 1)
                done()
            lo_upto(blk("cin", 192) + 3)
            norm("oy")
            residual("co", 8, gated=True)
            norm("x1b")
            ffn("x1b")
            norm("final")


def weight_blocks(a):
    stream = np.zeros((NBLK + 1, P, TPB, P), np.float32)
    tiles = stream.transpose(0, 2, 1, 3)

    def put(p, rows, cols=slice(0, P)):
        tiles[p // TPB, p % TPB][:, cols] = rows

    def feature(stage, w, cols, p=None):
        p = P0[stage] if p is None else p
        for c in cols:
            for k in range(w.shape[0] // P):
                put(p, w[k * P:k * P + P, c])
                p += 1
        return p

    def wide(stage, w, cols):
        p = P0[stage]
        for k in range(w.shape[0] // P):
            for c in cols:
                put(p, w[k * P:k * P + P, c])
                p += 1

    def span(n, off=0):
        return [slice(off + m * P, off + m * P + P) for m in range(n)]

    def ffn(stage, up, down):
        b0 = P0[stage] // TPB
        for g in range(NG):
            n = b0 if g == 0 else b0 + 2 + 3 * (g - 1)
            d = b0 + 4 + 3 * g if g < NG - 1 else b0 + 32
            feature(None, up, span(2, 2 * g * P), n * TPB)
            feature(None, up, span(2, DFF + 2 * g * P), (n + 1) * TPB)
            for ft in range(2):
                r = (2 * g + ft) * P
                for m in range(KT):
                    put(d * TPB + ft * KT + m, down[r:r + P, m * P:m * P + P])

    for l in range(DEPTH):
        w = a["w_in"][l]
        q0, kr, gq, gk, gv, gm = 0, 384, 416, 800, 928, 1056
        pair = np.arange(64)
        p = feature(f"in{l}", w, [slice(256, 384), slice(0, 128), slice(128, 256)])
        for k in range(KT):
            put(p, w[k * P:k * P + P, kr:kr + 32], slice(32, 64))
            put(p, w[k * P:k * P + P, kr:kr + 32], slice(64, 96))
            p += 1
        p = feature(None, w, [np.concatenate([gq + 64 * t + pair, gq + 64 * (3 + t) + pair]) for t in range(3)], p)
        p = feature(None, w, [slice(gk, gk + P), slice(gv, gv + P), slice(gm, gm + P), slice(gm + P, gm + 2 * P)], p)
        wide(f"vv{l}", w, span(2, gm + 256))
        p = P0[f"uq{l}"]
        for h in range(6):
            for k in range(2):
                u = a["mla_w_uq"][l][k * P:k * P + P, h * 96:h * 96 + 96]
                put(p, u[:, 0:64], slice(64 * (h % 2), 64 * (h % 2) + 64))
                put(p, u[:, 64:96], slice(64, 96) if h % 2 == 0 else slice(32, 64))
                p += 1
        u = a["mla_w_ukv"][l]
        for m in range(3):
            for e in range(2):
                h = 2 * m + e
                put(P0[f"nope{l}"] + m, u[:, h * P:h * P + 64], slice(64 * e, 64 * e + 64))
                put(P0[f"va{l}"] + m, u[:, h * P + 64:h * P + P], slice(64 * e, 64 * e + 64))
        feature(f"out{l}", a["w_out"][l][mixed_order()], span(8))
        feature(f"mk{l}", a["mem_w_kv"][l], span(4))
        wide(f"mv{l}", a["mem_w_kv"][l], span(2, 512))
        p = P0[f"mv{l}"] + 16
        for k in range(KT):
            for c in span(2, 768):
                put(p, a["mem_w_kv"][l][k * P:k * P + P, c])
                p += 1
        feature(f"mq{l}", a["mem_w_q"][l], span(4))
        feature(f"mo{l}", a["mem_w_o"][l], span(8))
        ffn(f"f{l}", a["ffn_w_up"][l], a["ffn_w_down"][l])
    w13, w2, ein = a["ffn_w13_2"], a["ffn_w2_2"], a["even_w_in_2"][0]
    for name, i, j in (("ctx", 0, 0), ("x0a", 0, 0), ("x0b", 0, 1), ("x1a", 1, 0), ("x1b", 1, 1)):
        ffn(name, w13[i, j], w2[i, j])

    def halves(stage, w, off):
        for half in range(2):
            p = P0[stage] + 16 * half
            for k in range(KT):
                for c in span(2, off + 256 * half):
                    put(p, w[k * P:k * P + P, c])
                    p += 1

    feature("ck", ein, span(4, 512))
    halves("cv", ein, 1024)
    feature("eq", ein, span(4))
    feature("ek", ein, span(4, 512))
    halves("ev", ein, 1024)
    halves("eu", ein, 1536)
    for g in range(4):
        put(P0["pool"] + g, a["pool_w_2"][0, g])
    feature("eo", a["even_w_out_2"][0], span(8))
    cin = a["conv_w_in_2"][0]
    feature("cin", cin, [slice(j * D + t * P, j * D + t * P + P) for t in range(KT) for j in range(3)])
    feature("co", a["conv_w_out_2"][0], span(8))
    return stream.reshape(NBLK + 1, P, TPB * P)


def mixed_order():
    order = list(range(384))
    for t in range(3):
        order += list(range(384 + 64 * t, 384 + 64 * t + 64)) + list(range(384 + 64 * (3 + t), 384 + 64 * (3 + t) + 64))
    return np.array(order + list(range(768, 1024)))


def param_columns(a):
    out = np.zeros((P, NPAR), np.float32)

    def put(name, v):
        v = np.asarray(v).reshape(-1, P)
        out[:, PCOL[name]:PCOL[name] + v.shape[0]] = v.T

    for l in range(DEPTH):
        put(f"mix{l}", a["mix_norm"][l])
        put(f"c{l}", np.concatenate([a["mla_kv_norm"][l], a["mla_q_norm"][l]]))
        put(f"gq{l}", np.concatenate([a["gqa_q_norm"][l]] * 2))
        put(f"gk{l}", np.concatenate([a["gqa_k_norm"][l]] * 2))
        put(f"y{l}", a["out_norm"][l][mixed_order()])
        put(f"mem{l}", a["mem_kv_norm"][l])
        put(f"memx{l}", a["mem_x_norm"][l])
        put(f"f{l}", a["ffn_norm"][l])
        conv = out[:, PCOL[f"conv{l}"]:PCOL[f"conv{l}"] + 8 * NF].reshape(P, 2 * NF, 4)
        for tap in range(3):
            conv[:, :, tap] = a["ffn_conv_w"][l, tap].reshape(2 * NF, P).T
        conv[:, :, 3] = a["ffn_conv_b"][l].reshape(2 * NF, P).T
        out[:, PCOL[f"conv{l}"]:PCOL[f"conv{l}"] + 8 * NF] = conv.reshape(P, 8 * NF)
    for i in range(DEPTH):
        for j in range(3):
            put(f"ng{i}{j}", a["norm_g_2"][i, j])
        put(f"mb{i}", a["mod_b_2"][i])
    put("ps", a["pool_scale_2"][0])
    put("cw", a["conv_w_2"][0])
    put("mid", a["final_norm"])
    put("final", a["final_g_2"])
    return out


def rotary(d):
    n = d // 4
    inv = (np.float32(10000.0) ** (-np.arange(n, dtype=np.float32) / np.float32(n))).astype(np.float32)
    t = np.arange(T)
    ang = np.concatenate([(t // 64).astype(np.float32)[:, None] * inv, (t % 64).astype(np.float32)[:, None] * inv], axis=-1)
    ang = np.repeat(ang.T, 2, axis=0).astype(np.float32)
    return np.cos(ang), np.sin(ang)


def shape_constants():
    con = np.zeros((P, NCON), np.float32)

    def put(name, v):
        con[:, CCOL[name]:CCOL[name] + v.shape[1]] = v

    i = np.arange(P)
    put("ident", np.eye(P))
    put("ones", np.ones((P, P)))
    put("bd", (i[:, None] // 64 == i[None, :] // 64).astype(np.float32))
    rot = np.zeros((P, P))
    rot[i[1::2], i[0::2]] = -1.0
    rot[i[0::2], i[1::2]] = 1.0
    put("rot", rot)
    c, s = rotary(32)
    ck, sk = np.zeros((P, T)), np.zeros((P, T))
    for r in (32, 64):
        ck[r:r + 32], sk[r:r + 32] = c, s
    put("ck", ck)
    put("sk", sk)
    c, s = rotary(64)
    put("cg", np.concatenate([c, c]))
    put("sg", np.concatenate([s, s]))
    put("eps", np.full((P, 1), 1e-6))
    q = 63 - (i % 64)[:, None]
    start = np.clip(q - 8, 0, 48)
    kc = np.arange(64)[None, :]
    put("mask", np.where((kc >= start) & (kc < start + 16), 0.0, -1e30))
    pool = np.zeros((4, T, T))
    for g, w in enumerate((2, 4, 8, 16)):
        for t in range(T):
            lo, hi = max(t - w // 2, 0), min(t - w // 2 + w, T)
            pool[g, lo:hi, t] = 1.0 / (hi - lo)
            pool[g, t, t] -= 1.0
    bp = pool.reshape(4, 2, P, T).transpose(2, 0, 1, 3).reshape(P, 2048).astype(np.float32)
    return con, np.ascontiguousarray(bp)


def feature_major(x):
    return np.ascontiguousarray(np.asarray(x).reshape(T, KT, P).transpose(2, 1, 0))


def kernel(**inputs):
    import concourse.bacc as bacc
    from concourse.bass_utils import run_bass_kernel_spmd

    a = {k: np.asarray(v) for k, v in inputs.items()}
    con, bp = shape_constants()
    rpb = np.zeros((8, 15, 128), np.float32)
    rpb[:, :, 48:79] = a["na_rpb_2"][0]
    mod = a["mod_w_2"].transpose(0, 2, 1).reshape(DEPTH * NMOD, P, D)
    arrays = {
        "stream": weight_blocks(a), "modstream": np.ascontiguousarray(mod),
        "x": feature_major(a["x"][0]), "mem": feature_major(a["mem"][0]), "ctxin": feature_major(a["ctx_2"][0]),
        "crow": np.ascontiguousarray(a["c_2"][0]), "ccrow": np.ascontiguousarray(a["c_ctx_2"]),
        "params": param_columns(a), "consts": con,
        "smallw": np.ascontiguousarray(a["gmlp_w_s"].transpose(0, 3, 1, 2).reshape(DEPTH, P, 512)),
        "smallb": np.ascontiguousarray(a["gmlp_b_s"]), "smallg": np.ascontiguousarray(a["gmlp_v_norm"]),
        "bpool": bp, "rpb": rpb,
    }
    nc = bacc.Bacc("TRN2", target_bir_lowering=False, num_devices=1)
    args = [nc.dram_tensor(k, v.shape, mybir.dt.from_np(v.dtype), kind="ExternalInput").ap() for k, v in arrays.items()]
    res = nc.dram_tensor("result", (P, KT, T), F32, kind="ExternalOutput").ap()
    two_blocks(nc, *args, res)
    r = run_bass_kernel_spmd(nc, [arrays], core_ids=[0])
    return np.ascontiguousarray(r.results[0]["result"].transpose(2, 1, 0)).reshape(1, T, D)
```

```python
from contextlib import ExitStack

import numpy as np

import concourse.bass as bass
from concourse import mybir

F32 = mybir.dt.float32
F32R = mybir.dt.float32r
BF16 = mybir.dt.bfloat16
ALU = mybir.AluOpType
ACT = mybir.ActivationFunctionType
AXX = mybir.AxisListType.X

P, T, D, DEPTH = 128, 256, 1024, 2
KT = D // P
DFF = 2816
NF = DFF // P
NG = NF // 2
TPB = 16
RAW, RING, MODRING = 3, 3, 2
LOOPS = (NG - 1) // 2
PERIT = 6
NMOD = 9 * KT
FFNS = ["f0", "f1", "ctx", "x0a", "x0b", "x1a", "x1b"]
MODS_PER_IT = {"f0": 2, "f1": 2, "ctx": 4, "x0a": 6, "x0b": 6, "x1a": 6}
MODS_AFTER = {"f0": 2, "f1": 2, "ctx": 4, "x0a": 2, "x0b": 2, "x1a": 2}
MOD_START = {"f0": 0, "f1": 12, "ctx": 24, "x0a": 48, "x0b": 80, "x1a": 112}
MOD_BOTH = ("f0", "f1", "ctx")
NMODC = 6 * KT



def stage_sizes():
    out = []
    for l in range(DEPTH):
        out += [(f"in{l}", 88), (f"vv{l}", 16), (f"uq{l}", 12), (f"nope{l}", 3), (f"va{l}", 3), (f"pad{l}", 6),
                (f"out{l}", 64), (f"mk{l}", 32), (f"mv{l}", 32), (f"mq{l}", 32), (f"mo{l}", 32), (f"f{l}", 33 * TPB)]
    out += [("ctx", 33 * TPB), ("x0a", 33 * TPB), ("ck", 32), ("cv", 64 - 32), ("eq", 32), ("ek", 32), ("ev", 32), ("eu", 32),
            ("pool", 4), ("padp", 12), ("eo", 64), ("x0b", 33 * TPB), ("x1a", 33 * TPB),
            ("cin", 192), ("co", 64), ("x1b", 33 * TPB)]
    return out


P0, _p = {}, 0
for _name, _n in stage_sizes():
    P0[_name] = _p
    _p += _n
assert _p % TPB == 0
NBLK = _p // TPB



def output_counts():
    out = []
    for l in range(DEPTH):
        out += [(f"in{l}", 11), (f"vv{l}", 2), (f"gvt{l}", 1), (f"krot{l}", 1), (f"mix{l}", 1), (f"uq{l}", 6), (f"nope{l}", 3),
                (f"va{l}", 2), (f"gqrot{l}", 2), (f"qrot{l}", 3), (f"att{l}", 12), (f"out{l}", 8), (f"mk{l}", 4),
                (f"mv{l}", 4), (f"mq{l}", 4), (f"matt{l}", 4), (f"mo{l}", 8)]
    out += [("ck", 4), ("cv", 4), ("eq", 4), ("ek", 4), ("ev", 4), ("eu", 4), ("pooled", 4), ("pool", 4), ("natt", 8),
            ("eo", 8), ("cin", 24), ("co", 8)]
    return out


O0, _o = {}, 0
for _name, _n in output_counts():
    O0[_name] = _o
    _o += _n

BLOCK_END, FULL_COUNT = {}, {}
_full = [0] * 4
for _name, _n in output_counts():
    _stage = _name.rstrip("01") if _name[-1] in "01" else _name
    for _j in range(_n):
        _end = None
        if _stage in ("mv", "cv", "ev", "eu"):
            _end = P0[_name] + 16 * (_j // 2 + 1) if _j % 2 else None
        elif _stage in ("in", "out", "mk", "mq", "ck", "eq", "ek", "eo", "cin", "co"):
            _end = P0[_name] + KT * (_j + 1)
        elif _stage == "uq":
            _end = P0[_name] + 2 * (_j + 1)
        elif _stage == "mo":
            _end = P0[_name] + 4 * (_j + 1)
        if _end is not None and _end % TPB == 0:
            BLOCK_END[O0[_name] + _j] = _end // TPB
        else:
            _full[(O0[_name] + _j) % 4] += 1
            FULL_COUNT[O0[_name] + _j] = _full[(O0[_name] + _j) % 4]

NORMS = []
for _l in range(DEPTH):
    NORMS += [(f"mix{_l}", 8, ((0, 8, D),)), (f"c{_l}", 3, ((0, 1, 128), (1, 3, 256))),
              (f"y{_l}", 8, ((0, 3, 384), (3, 6, 384), (6, 8, 256))),
              (f"mem{_l}", 8, ((0, 8, D),)), (f"memx{_l}", 8, ((0, 8, D),)), (f"my{_l}", 4, None), (f"f{_l}", 8, ((0, 8, D),))]
NORMS += [("mid", 8, ((0, 8, D),)), ("ctx", 8, ((0, 8, D),)), ("x0a", 8, ((0, 8, D),)), ("cn", 8, ((0, 8, D),)), ("xn", 8, ((0, 8, D),)),
          ("ey", 8, None), ("x0b", 8, ((0, 8, D),)), ("x1a", 8, ((0, 8, D),)), ("x1n", 8, ((0, 8, D),)), ("oy", 8, None),
          ("x1b", 8, ((0, 8, D),)), ("final", 8, ((0, 8, D),))]
NSUMS, NTILES, NSQ = {}, {}, {}
_k = _s = _t = 0
for _name, _n, _g in NORMS:
    NSUMS[_name], NTILES[_name], NSQ[_name] = _s, _t, _k
    _k, _s, _t = _k + (_n if _g else 0), _s + (_g is not None), _t + (0 if _name == "mid" else _n)

PCOL, _c = {}, 0
for _name, _n in ([(f"{a}{l}", n) for l in range(DEPTH) for a, n in (
        ("mix", 8), ("c", 3), ("gq", 1), ("gk", 1), ("y", 8), ("mem", 8), ("memx", 8), ("f", 8), ("conv", 4 * 2 * NF))]
        + [(f"ng{i}{j}", 8) for i in range(DEPTH) for j in range(3)]
        + [("ps", 4), ("cw", 24), ("mid", 8), ("final", 8), ("mb0", NMOD), ("mb1", NMOD)]):
    PCOL[_name] = _c
    _c += _n
NPAR = _c

CCOL, _c = {}, 0
for _name, _n in (("ones", 128), ("eps", 1), ("ident", 128), ("bd", 128), ("rot", 128), ("ck", 256), ("sk", 256),
                  ("cg", 256), ("sg", 256), ("mask", 64)):
    CCOL[_name] = _c
    _c += _n
CFIRST = 129
NCON = _c

A_QM, A_KM, A_VM, A_QB, A_VB, A_C, A_KP, A_GV, A_U, A_VV, A_RT = 0, 1536, 3072, 3840, 4864, 5120, 5888, 6144, 6400, 6912, 7424
A_MK, A_MV, A_MQ = 0, 1024, 2048
A_Q, A_KL, A_KC, A_VL, A_VC, A_UT, A_BP = 0, 1024, 2048, 3072, 4096, 5120, 6144
A_PR1, A_PT1 = A_BP, A_BP + 1024
A_CG, A_CV, A_BG = 0, 512, 1536
A_Z, A_ZC = 0, 256
NAR = 8192




AFTER_FFN = ("mix1", "mid", "ctx", "x0a", "cn", "x1a", "x1n", "final")


def SUM_BANK(name, g):
    return (4 if name in AFTER_FFN else 0) + g // 2


def NAPP(name):
    return NSQ[name] - (KT if NSQ[name] > NSQ["mid"] else 0)


LAG = 1
NAV = 5


def EV(l, what):
    return NAV * l + {"c": 1, "gv": 2, "uq": 3, "va": 4, "mq": 5, "eu": 1, "ps": 2}[what]


def YV(what, j=0):
    return 2 * DEPTH + {"pool_lo": j + 1, "natt": 5, "cin": 6 + j}[what]


def GX(ffn):
    return 4 if ffn in ("x0b", "x1a", "x1b") else 0


class Chain:

    def __init__(self, eng, sem):
        self.eng, self.sem, self.n, self.i, self.per = eng, sem, 0, None, 0

    def value(self):
        return self.n if self.i is None else self.n + self.i * self.per

    def link(self, ins):
        self.n += 1
        ins.then_inc(self.sem, 1)
        self.eng.wait_ge(self.sem, self.value())

    def enter(self, i, per):
        self.i, self.per, self.start = i, per, self.n

    def leave(self, trips):
        assert self.n - self.start == self.per, (self.n - self.start, self.per)
        self.n = self.start + self.per * trips
        self.i = None


def two_blocks(nc, stream, modstream, x, mem, ctxin, crow, ccrow, params, consts, smallw, smallb, smallg, bpool, rpb, out):
    es = ExitStack()
    with es:
        def sb(name, shape, dt=F32):
            return es.enter_context(nc.sbuf_tensor(name, shape, dt))

        def sem(name):
            return es.enter_context(nc.semaphore(name))

        wraw = sb("wraw", [P, RAW, 2048])
        whi = sb("whi", [P, RING, 2048], F32R)
        wlo = sb("wlo", [P, RING, 2048], F32R)
        modw = sb("modw", [P, MODRING, D])
        cb = sb("cb", [P, 2, D])
        X = sb("X", [P, KT, T])
        CX = sb("CX", [P, KT, T])
        Hh = sb("Hh", [P, KT, T], F32R)
        Hl = sb("Hl", [P, KT, T], F32R)
        NS = sb("NS", [P, 2, KT, T])
        SQ, TN = NS[:, 0], NS[:, 1]
        Gh = sb("Gh", [P, 4, T], F32R)
        Gl = sb("Gl", [P, 4, T], F32R)
        Y = sb("Y", [P, KT, T])
        PR = sb("PR", [P, 2, 512])
        PT = sb("PT", [P, 4, T])
        STD = PT
        AR = sb("AR", [P, NAR])
        SW = sb("SW", [P, 1024])
        CON = sb("CON", [P, NCON])
        PAR = sb("PAR", [P, NPAR])
        ZB = sb("ZB", [P, 512], BF16)
        GS = sb("GS", [P, 8])
        HG = sb("HG", [P, 8])
        MODL = sb("MODL", [P, DEPTH * NMOD])
        MODC = sb("MODC", [P, NMODC])
        MSC = sb("MSC", [P, 2, 8])
        NM = sb("NM", [P, 4])
        SM = sb("SM", [P, 4])
        RI = sb("RI", [P, 4])
        VS = sb("VS", [P, 6])
        WARM = sb("WARM", [P, 1])

        bank = [es.enter_context(nc.psum_tensor(f"bank{b}", [P, 512], F32)) for b in range(8)]

        raw_loaded = [sem(f"raw_loaded{s}") for s in range(RAW)]
        mod_loaded = [sem(f"mod_loaded{s}") for s in range(MODRING)]
        hi_ready, lo_ready, w_used, mod_used = sem("hi_ready"), sem("lo_ready"), sem("w_used"), sem("mod_used")
        full = [sem(f"psum_full{b}") for b in range(4)]
        free = [sem(f"psum_free{b}") for b in range(4)]
        act_step, dve_step = sem("act_step"), sem("dve_step")
        n_sq, n_sum, n_std, n_app, n_hi, n_lo = (sem(s) for s in (
            "norm_squared", "norm_summed", "norm_deviation", "norm_applied", "norm_hi", "norm_lo"))
        gain_ready = sem("gain_ready")
        up_free, affine, silu_done, gate_out, g_hi, g_lo = (sem(s) for s in (
            "up_read", "conv_centre", "silu_done", "gate_out", "g_hi", "g_lo"))
        res_tile, down_full = sem("residual_tile"), sem("down_bank_full")
        s_full, max_ready, exp_done, prob_ready, pt_full, pt_copied = (sem(s) for s in (
            "scores_full", "max_ready", "exp_done", "prob_ready", "pt_full", "pt_copied"))
        const_in, par_in, x_in, mem_in, ctx_in, c_in, sw_in, bp_in, bias_in, out_done = (sem(s) for s in (
            "const_in", "par_in", "x_in", "mem_in", "ctx_in", "c_in", "sw_in", "bp_in", "bias_in", "out_done"))
        const_rest, par_rest = sem("const_rest"), sem("par_rest")
        c_silu, zeros_ready = sem("c_silu"), sem("zeros_ready")
        evac, qk_std, vv_std, vv_ready, kp_raw, y_half, qk_norm, rope_in = (sem(s) for s in (
            "act_evacuated", "qk_deviation", "vv_deviation", "vv_normed", "kp_raw", "dve_evacuated", "qk_normed", "roped"))
        qk_sq, qk_sum, cx_free, mixed_done, ubuf, out_ready, z_copy, mask_done = (sem(s) for s in (
            "qk_squared", "qk_summed", "context_buffer_free", "spatial_mixed", "u_read", "result_ready", "cg_copied",
            "bias_masked"))

        def con(name, n=128):
            return CON[:, CCOL[name]:CCOL[name] + n]

        def par(name, j=0, n=1):
            return PAR[:, PCOL[name] + j:PCOL[name] + j + n]

        def ar(off, n, w=T):
            return AR[:, off:off + n * w].rearrange("p (n w) -> p n w", w=w)

        def backwards(v):
            return v.rearrange("p (r c) -> p r c", r=4)[:, :, ::-1]

        def probs(h, wide_):
            if not wide_:
                return PR[:, h % 2, :].rearrange("p (q k) -> p q k", q=2)
            return PR[:, :, :] if h % 2 == 0 else ar(A_PR1, 2, 512)

        def probs_t(h, wide_):
            if not wide_:
                return PT[:, 2 * (h % 2):2 * (h % 2) + 2, :]
            return PT[:, :, :] if h % 2 == 0 else ar(A_PT1, 4)

        def obank(o):
            return bank[4 + o % 4]

        def wait_full(eng, o):
            if o in BLOCK_END:
                eng.wait_ge(w_used, BLOCK_END[o])
            else:
                eng.wait_ge(full[o % 4], FULL_COUNT[o])

        ident, ones, bdiag, rot = con("ident"), con("ones"), con("bd"), con("rot")
        eps = con("eps", 1)
        KBUF = {"h": (Hh, Hl), "g": (Gh, Gl)}

        def gain(name, t):
            if name in MODULATED:
                return GS[:, t:t + 1]
            return par(name, t)

        MODULATED = {"ctx": (MODC, 0, 0, "ng00"), "x0a": (MODL, 0, 0, "ng00"), "cn": (MODC, 0, 3, "ng01"),
                     "xn": (MODL, 0, 3, "ng01"), "x0b": (MODL, 0, 6, "ng02"), "x1a": (MODL, NMOD, 0, "ng10"),
                     "x1n": (MODL, NMOD, 3, "ng11"), "x1b": (MODL, NMOD, 6, "ng12")}
        MODORD = {n: i for i, n in enumerate(["ctx", "x0a", "cn", "xn", "x0b", "x1a", "x1n", "x1b"])}

        def shift(name, t):
            m, base, j, _ = MODULATED[name]
            return m[:, base + j * 8 + t:base + j * 8 + t + 1]

        def source(name):
            if name.startswith("c") and name[1:].isdigit():
                return ar(A_C, 3)
            if name.startswith("y") or name.startswith("my") or name in ("ey", "oy"):
                return Y[:, :, :]
            if (name.startswith("mem") and not name.startswith("memx")) or name in ("ctx", "cn"):
                return CX[:, :, :]
            return X[:, :, :]

        def target(name):
            return KBUF["g"] if name.startswith("c") and name[1:].isdigit() else KBUF["h"]

        NINFO = {n: (t, g) for n, t, g in NORMS}
        UPDATES = ["out0", "mo0", "f0", "out1", "mo1", "f1", "mid", "ctx", "x0a", "eo", "x0b", "x1a", "co", "x1b"]
        UPDATED = {"memx0": "out0", "f0": "mo0", "mix1": "f0", "memx1": "out1", "f1": "mo1", "mid": "f1", "x0a": "mid",
                   "cn": "ctx", "xn": "x0a", "x0b": "eo", "x1a": "x0b", "x1n": "x1a", "x1b": "co", "final": "x1b"}
        FI = {n: i for i, n in enumerate(FFNS)}

        block = es.enter_context(nc.Block())

        @block.sync
        def _(sp):
            sp.dma_start(X[:, 0:4, :], x[:, 0:4, :]).then_inc(x_in, 16)
            sp.dma_start(X[:, 4:8, :], x[:, 4:8, :]).then_inc(x_in, 16)
            sp.dma_start(CON[:, 0:CFIRST], consts[:, 0:CFIRST]).then_inc(const_in, 16)
            sp.dma_start(PAR[:, 0:KT], params[:, 0:KT]).then_inc(par_in, 16)
            loaded = 0

            def load(n, i=None, step=0):
                if n >= RAW or i is not None:
                    sp.wait_ge(lo_ready, n - RAW + 1 if i is None else i * PERIT + (n - RAW + 1))
                src = stream[n] if i is None else stream[bass.ds(i * PERIT + n, 1)].rearrange("o p f -> (o p) f")
                sp.dma_start(wraw[:, n % RAW, :], src).then_inc(raw_loaded[n % RAW], 16)

            def load_mod(u, i=None, per=0):
                sp.wait_ge(mod_used, u + 1 if i is None else i * per + (u + 1))
                src = modstream[u] if i is None else modstream[bass.ds(i * per + u, 1)].rearrange("o p f -> (o p) f")
                sp.dma_start(modw[:, u % MODRING, :], src).then_inc(mod_loaded[u % MODRING], 16)

            for f in FFNS:
                b0 = P0[f] // TPB
                for n in range(loaded, b0 + 4):
                    load(n)
                per = MODS_PER_IT.get(f, 0)
                with sp.Fori(0, LOOPS) as i:
                    for c in range(2):
                        for k in range(3):
                            load(b0 + 4 + 3 * c + k, i)
                            if k < per // 2:
                                load_mod(MOD_START[f] + per // 2 * c + k, i, per)
                if b0 + 34 < NBLK + 1:
                    load(b0 + 34)
                for k in range(MODS_AFTER.get(f, 0)):
                    load_mod(MOD_START[f] + per * LOOPS + k)
                loaded = b0 + 35
            sp.wait_ge(n_app, NAPP("final") + KT)
            sp.dma_start(out, SQ).then_inc(out_done, 16)
            sp.wait_ge(out_done, 16)

        @block.gpsimd
        def _(pool):
            pool.wait_ge(hi_ready, 1)
            pool.dma_start(CON[:, CFIRST:], consts[:, CFIRST:]).then_inc(const_rest, 16)
            pool.dma_start(PAR[:, KT:], params[:, KT:]).then_inc(par_rest, 16)
            pool.dma_start(CX[:, :, :], mem).then_inc(mem_in, 16)
            pool.dma_start(cb[:, 0, :], crow.partition_broadcast(P)).then_inc(c_in, 16)
            pool.dma_start(cb[:, 1, :], ccrow.partition_broadcast(P)).then_inc(c_in, 16)
            for l in range(DEPTH):
                if l:
                    pool.wait_ge(mixed_done, l)
                pool.dma_start(SW[:, 0:512], smallw[l]).then_inc(sw_in, 16)
                pool.dma_start(SW[:, 512:768], smallg[l].partition_broadcast(P)).then_inc(sw_in, 16)
                for g in range(4):
                    r = 64 * (g % 2)
                    pool.dma_start(SW[r:r + 64, 768 + 128 * (g // 2):896 + 128 * (g // 2)],
                                   smallb[l, g].partition_broadcast(64)).then_inc(sw_in, 16)
            pool.wait_ge(n_hi, NTILES["mem1"] + 8)
            pool.wait_ge(n_app, NAPP("mem1") + 8)
            pool.dma_start(CX[:, :, :], ctxin).then_inc(ctx_in, 16)
            pool.wait_ge(n_lo, NTILES["f1"] + 8)
            pool.dma_start(AR[:, A_BP:A_BP + 2048], bpool).then_inc(bp_in, 16)
            pool.wait_ge(n_lo, NTILES["xn"] + 8)
            pool.wait_ge(n_hi, NTILES["xn"] + 8)
            for t in range(2):
                for r in range(2):
                    for h in range(8):
                        src = bass.AP(tensor=rpb.tensor, offset=h * 15 * 128 + (7 - (2 * t + r)) * 128,
                                      ap=[[1, 64], [128, 4], [1, 64]])
                        dst = NS[64 * r:64 * r + 64].rearrange("p a k t -> p (a k) t")[:, 2 * h + t, :] \
                            .rearrange("p (a b) -> p a b", a=4)
                        pool.dma_start(dst, src).then_inc(bias_in, 16)

        @block.tensor
        def _(pe):
            state = {"block": -1}

            def open_block(n, i=None):
                pe.wait_ge(lo_ready, n + 1 if i is None else i * PERIT + (n + 1))

            def tile_at(p, w=1):
                c = (p % TPB) * P
                return whi[:, (p // TPB) % RING, c:c + w * P], wlo[:, (p // TPB) % RING, c:c + w * P]

            def need(p):
                if p // TPB != state["block"]:
                    assert p // TPB == state["block"] + 1
                    state["block"] = p // TPB
                    open_block(p // TPB)

            def three(outp, whl, ahl, start, stop, flip=False, skip=False):
                last = None
                for j, (a, b) in enumerate(((0, 0), (0, 1), (1, 0))):
                    st, en = start and j == 0, stop and j == 2
                    lhs, rhs = (ahl[b], whl[a]) if flip else (whl[a], ahl[b])
                    last = pe.matmul(outp, lhs, rhs, start=st, stop=en, skip_group_check=skip)
                return last

            def claim(o):
                if o // 4 > 0:
                    pe.wait_ge(free[o % 4], o // 4)

            def wait_h(name, k):
                pe.wait_ge(n_lo, NTILES[name] + k + 1)

            def feature(stage, name, outs, kt, src="h", k0=0, first=0, p=None, o=None):
                hh, hl = KBUF[src]
                p = P0[stage] if p is None else p
                o = O0[stage] if o is None else o
                for m in range(outs):
                    claim(o)
                    for k in range(kt):
                        need(p)
                        if m == 0 and name:
                            wait_h(name, k0 + k)
                        last = three(obank(o)[:, 0:T], tile_at(p), (hh[:, k0 + k, :], hl[:, k0 + k, :]), k == 0, k == kt - 1)
                        p += 1
                        if p % TPB == 0 and k < kt - 1:
                            last.then_inc(w_used, 1)
                    last.then_inc(w_used if p % TPB == 0 else full[o % 4], 1)
                    o += 1

            def tokens(stage, name, kt, w, src="h", k0=0, p=None, o=None):
                hh, hl = KBUF[src]
                p = P0[stage] if p is None else p
                o = O0[stage] if o is None else o
                for tt in range(2):
                    claim(o + tt)
                for k in range(kt):
                    need(p)
                    if name:
                        wait_h(name, k0 + k)
                    for tt in range(2):
                        s = slice(tt * P, tt * P + P)
                        last = three(obank(o + tt)[:, 0:w * P], tile_at(p, w),
                                     (hh[:, k0 + k, s], hl[:, k0 + k, s]), k == 0, k == kt - 1, flip=True)
                        if k == kt - 1 and tt == 0:
                            last.then_inc(full[(o + tt) % 4], 1)
                    p += w
                    if p % TPB == 0 and k < kt - 1:
                        last.then_inc(w_used, 1)
                last.then_inc(w_used if p % TPB == 0 else full[(o + 1) % 4], 1)

            def norm_sum(name):
                n, groups = NINFO[name]
                for g, (a, b, _) in enumerate(groups):
                    for t in range(a, b):
                        pe.wait_ge(n_sq, NSQ[name] + t + 1)
                        last = pe.matmul(bank[SUM_BANK(name, g)][:, T * (g % 2):T * (g % 2) + T], ones, SQ[:, t, :],
                                         start=(t == a), stop=(t == b - 1))
                last.then_inc(n_sum, 1)

            def skip_pad(p):
                last = pe.matmul(bank[0][:, 0:P], ZB[:, 0:P], ZB[:, 0:P], start=True, stop=True)
                last.then_inc(w_used, 1)

            def attention(h0, n, o0, keys, single, q_of, k_of, v_of, place):
                nk = keys // P

                def scores(a):
                    h = h0 + a
                    wait = h if single else h - 1
                    if wait > 0:
                        pe.wait_ge(exp_done, wait)
                    for qt in range(2):
                        for kk in range(keys // T):
                            b = bank[qt][:, kk * T:kk * T + T] if single else bank[h % 2][:, qt * T:qt * T + T]
                            last = pe.matmul(b, q_of(a)[:, qt * P:qt * P + P], k_of(a, kk), start=True, stop=True)
                    last.then_inc(s_full, 1)

                def transposes(a):
                    h = h0 + a
                    pe.wait_ge(prob_ready, h + 1)
                    wait = h if single else h - 1
                    if wait > 0:
                        pe.wait_ge(pt_copied, wait)
                    for qt in range(2):
                        for k in range(nk):
                            b = bank[2 + k // 2][:, (k % 2) * T + qt * P:(k % 2) * T + qt * P + P] if single else \
                                bank[2 + h % 2][:, k * T + qt * P:k * T + qt * P + P]
                            src = probs(h, single)[:, qt, k * P:k * P + P]
                            last = pe.transpose(b, src, ident)
                    last.then_inc(pt_full, 1)

                def values(a):
                    h, o = h0 + a, o0 + a
                    pe.wait_ge(pt_copied, h + 1)
                    claim(o)
                    r0, r1 = place(a)
                    for k in range(nk):
                        last = pe.matmul(obank(o)[r0:r1, 0:T], v_of(a, k), probs_t(h, single)[:, k, :], start=(k == 0), stop=(k == nk - 1))
                    last.then_inc(full[o % 4], 1)

                for a in range(n + 3):
                    if a < n:
                        scores(a)
                    if 2 <= a <= n + 1:
                        transposes(a - 2)
                    if a >= 3:
                        values(a - 3)

            def ffn(name):
                f, b0 = FI[name], P0[name] // TPB
                pe.wait_ge(n_std, NSUMS[name] + 1)
                if name == "x0a":
                    pe.wait_ge(res_tile, KT * (UPDATES.index("ctx") + 1))
                for b in range(4):
                    pe.matmul(bank[b][:, :], ZB[:, 0:P], ZB[:, :], start=True, stop=False, skip_group_check=True)

                def up(g2, n, i, gval):
                    pe.wait_ge(up_free, gval)
                    for half in range(2):
                        open_block(n + half, i)
                        for ft in range(2):
                            for k in range(KT):
                                if i is None and half == 0 and ft == 0:
                                    wait_h(name, k)
                                last = three(bank[4 + 2 * g2 + half][:, ft * T:ft * T + T],
                                             tile_at((n + half) * TPB + ft * KT + k), (Hh[:, k, :], Hl[:, k, :]),
                                             k == 0, k == KT - 1)
                        last.then_inc(w_used, 1)

                def down(g2, n, i, gval, final=False):
                    open_block(n, i)
                    pe.wait_ge(g_lo, gval)
                    order = [(ft, m) for m in range(KT) for ft in range(2)] if final else \
                        [(ft, m) for ft in range(2) for m in range(KT)]
                    for ft, m in order:
                        last = three(bank[m // 2][:, T * (m % 2):T * (m % 2) + T], tile_at(n * TPB + ft * KT + m),
                                     (Gh[:, 2 * g2 + ft, :], Gl[:, 2 * g2 + ft, :]), False, final and ft == 1, skip=True)
                        if final and ft == 1 and m % 2 and m < KT - 1:
                            last.then_inc(down_full, 1)
                    last.then_inc(w_used, 1)

                up(0, b0, None, NG * f + 1)
                with pe.Fori(0, LOOPS) as i:
                    for c in range(2):
                        n = b0 + 2 + 3 * c
                        up((1 + c) % 2, n, i, i * 2 + (NG * f + c + 1))
                        down(c % 2, n + 2, i, i * 2 + (NG * f + c + 1))
                down(0, b0 + 32, None, NG * f + NG, final=True)
                state["block"] = b0 + 32

            pe.wait_ge(const_in, 16)
            pe.wait_ge(zeros_ready, 1)
            for l in range(DEPTH):
                QM, KM, VM = ar(A_QM, 6), ar(A_KM, 6), ar(A_VM, 2, 384)
                QB, VB, GV, VV, KP = ar(A_QB, 4), ar(A_VB, 2, 128), ar(A_GV, 1), ar(A_VV, 2), ar(A_KP, 1)
                norm_sum(f"mix{l}")
                feature(f"in{l}", f"mix{l}", 7, KT)
                norm_sum(f"c{l}")
                feature(f"in{l}", None, 4, KT, p=P0[f"in{l}"] + 56, o=O0[f"in{l}"] + 7)
                tokens(f"vv{l}", None, KT, 2)
                if l == 0:
                    pe.wait_ge(const_rest, 16)
                o = O0[f"gvt{l}"]
                claim(o)
                pe.wait_ge(evac, EV(l, "gv"))
                for tt in range(2):
                    last = pe.transpose(obank(o)[:, tt * P:tt * P + P], GV[:, 0, tt * P:tt * P + P], ident)
                last.then_inc(full[o % 4], 1)
                o = O0[f"krot{l}"]
                claim(o)
                pe.matmul(obank(o)[:, 0:T], rot, KP[:, 0, :], start=True, stop=True).then_inc(full[o % 4], 1)
                pe.wait_ge(qk_sq, l + 1)
                for j in range(2):
                    last = pe.matmul(bank[2 + j][:, :], bdiag,
                                     SQ[:, 4 + 2 * j:6 + 2 * j, :].rearrange("p a t -> p (a t)"), start=True, stop=True)
                last.then_inc(qk_sum, 1)
                o = O0[f"mix{l}"]
                claim(o)
                pe.wait_ge(vv_ready, l + 1)
                pe.wait_ge(sw_in, 96 * (l + 1))
                for n in range(2):
                    for g in range(4):
                        last = pe.matmul(obank(o)[64 * (g % 2):64 * (g % 2) + 64, (g // 2) * T + n * P:(g // 2) * T + n * P + P],
                                         VV[:, n, g * 64:g * 64 + 64], SW[:, g * P:g * P + P], start=True, stop=True)
                last.then_inc(full[o % 4], 1)
                feature(f"uq{l}", f"c{l}", 6, 2, src="g", k0=1)
                feature(f"nope{l}", f"c{l}", 3, 1, src="g", k0=0)
                tokens(f"va{l}", None, 1, 3, src="g", k0=0)
                skip_pad(None)
                pe.wait_ge(qk_norm, l + 1)
                for j in range(2):
                    o = O0[f"gqrot{l}"] + j
                    claim(o)
                    pe.matmul(obank(o)[:, :], rot, QB[:, 2 * j:2 * j + 2, :].rearrange("p a t -> p (a t)"),
                              start=True, stop=True).then_inc(full[o % 4], 1)
                pe.wait_ge(evac, EV(l, "uq"))
                for j in range(3):
                    o = O0[f"qrot{l}"] + j
                    claim(o)
                    pe.matmul(obank(o)[:, :], rot, QM[:, 2 * j:2 * j + 2, :].rearrange("p a t -> p (a t)"),
                              start=True, stop=True).then_inc(full[o % 4], 1)
                pe.wait_ge(rope_in, l + 1)
                pe.wait_ge(evac, EV(l, "va"))

                def qh(a):
                    if a < 6:
                        return QM[:, a, :]
                    b = a - 6
                    return QB[64 * (b // 3):64 * (b // 3) + 64, b % 3, :]

                def kh(a, kk):
                    if a < 6:
                        return KM[:, a, :]
                    b = a - 6
                    return QB[64 * (b // 3):64 * (b // 3) + 64, 3, :]

                def vh(a, k):
                    if a < 6:
                        return VM[:, k, 64 * a:64 * a + 64]
                    b = a - 6
                    return VB[:, k, 64 * (b // 3):64 * (b // 3) + 64]

                def row(a):
                    r = 64 * (a % 2) if a < 6 else 64 * ((a - 6) // 3)
                    return r, r + 64

                attention(16 * l, 12, O0[f"att{l}"], T, False, qh, kh, vh, row)
                norm_sum(f"y{l}")
                feature(f"out{l}", f"y{l}", 8, KT)
                norm_sum(f"mem{l}")
                feature(f"mk{l}", f"mem{l}", 4, KT)
                tokens(f"mv{l}", None, KT, 2)
                tokens(f"mv{l}", None, KT, 2, p=P0[f"mv{l}"] + 16, o=O0[f"mv{l}"] + 2)
                norm_sum(f"memx{l}")
                feature(f"mq{l}", f"memx{l}", 4, KT)
                pe.wait_ge(evac, EV(l, "mq"))
                MK, MV, MQ = ar(A_MK, 4), ar(A_MV, 2, 512), ar(A_MQ, 4)
                attention(16 * l + 12, 4, O0[f"matt{l}"], T, False, lambda a: MQ[:, a, :], lambda a, kk: MK[:, a, :],
                          lambda a, k: MV[:, k, P * a:P * a + P], lambda a: (0, P))
                feature(f"mo{l}", f"my{l}", 8, 4)
                norm_sum(f"f{l}")
                ffn(f"f{l}")
            norm_sum("mid")
            for name in ("ctx", "x0a"):
                norm_sum(name)
                ffn(name)
            norm_sum("cn")
            feature("ck", "cn", 4, KT)
            tokens("cv", None, KT, 2)
            tokens("cv", None, KT, 2, p=P0["cv"] + 16, o=O0["cv"] + 2)
            norm_sum("xn")
            feature("eq", "xn", 4, KT)
            feature("ek", None, 4, KT)
            for s in ("ev", "eu"):
                tokens(s, None, KT, 2)
                tokens(s, None, KT, 2, p=P0[s] + 16, o=O0[s] + 2)
            pe.wait_ge(evac, EV(2, "eu"))
            pe.wait_ge(bp_in, 16)
            UT, BP = ar(A_UT, 2, 512), AR[:, A_BP:A_BP + 2048].rearrange("p (g s t) -> p g s t", g=4, s=2)
            for g in range(4):
                o = O0["pooled"] + g
                claim(o)
                for s in range(2):
                    last = pe.matmul(obank(o)[:, 0:T], UT[:, s, g * P:g * P + P], BP[:, g, s, :], start=(s == 0), stop=(s == 1))
                last.then_inc(full[o % 4], 1)
            p = P0["pool"]
            for g in range(4):
                o = O0["pool"] + g
                claim(o)
                need(p)
                pe.wait_ge(y_half, YV("pool_lo", g))
                three(obank(o)[:, 0:T], tile_at(p), (Gh[:, g, :], Gl[:, g, :]), True, True).then_inc(full[o % 4], 1)
                p += 1
            skip_pad(None)
            Q, KL, KC = ar(A_Q, 4), ar(A_KL, 4), ar(A_KC, 4)
            VL, VC = ar(A_VL, 2, 512), ar(A_VC, 2, 512)

            def half(a):
                return slice(64 * (a % 2), 64 * (a % 2) + 64)

            attention(32, 8, O0["natt"], 512, True, lambda a: Q[half(a), a // 2, :],
                      lambda a, kk: (KL if kk == 0 else KC)[half(a), a // 2, :],
                      lambda a, k: (VL if k < 2 else VC)[:, k % 2, 64 * a:64 * a + 64],
                      lambda a: (64 * (a % 2), 64 * (a % 2) + 64))
            feature("eo", "ey", 8, KT)
            norm_sum("x0b")
            ffn("x0b")
            norm_sum("x1a")
            ffn("x1a")
            norm_sum("x1n")
            feature("cin", "x1n", 24, KT)
            feature("co", "oy", 8, KT)
            norm_sum("x1b")
            ffn("x1b")
            norm_sum("final")

        @block.scalar
        def _(act):
            chain = Chain(act, act_step)
            st = {"hi": 0, "ev": 0}

            def split_hi(n, i=None):
                slot = n % RAW
                loads = 16 * (n // RAW + 1)
                act.wait_ge(raw_loaded[slot], loads if i is None else i * (16 * PERIT // RAW) + loads)
                if n >= RING:
                    act.wait_ge(w_used, n - RING + 1 if i is None else i * PERIT + (n - RING + 1))
                act.activation(whi[:, n % RING, :], wraw[:, slot, :], ACT.Copy).then_inc(hi_ready, 1)

            def hi_upto(n):
                while st["hi"] <= min(n, NBLK):
                    split_hi(st["hi"])
                    st["hi"] += 1

            def table(func):
                act.activation(WARM[:, :], eps, func)

            def source_ready(name):
                marks = {"ey": YV("natt"), "oy": YV("cin", KT - 1)}
                for l in range(DEPTH):
                    marks.update({f"y{l}": 2 * l + 1, f"my{l}": 2 * l + 2})
                if name in marks:
                    act.wait_ge(y_half, marks[name])

            def norm(name):
                n, groups = NINFO[name]
                if groups:
                    norm_square(name)
                    norm_rest(name)
                else:
                    plain_hi(name)

            def norm_square(name):
                n, groups = NINFO[name]
                src = source(name)
                source_ready(name)
                if NSUMS[name]:
                    act.wait_ge(n_sum, NSUMS[name])
                if name not in AFTER_FFN:
                    table(ACT.Sqrt)
                for t in range(n):
                    if name == "mix0" and t % 4 == 0:
                        act.wait_ge(x_in, 4 * t + 16)
                    if name in UPDATED:
                        act.wait_ge(res_tile, KT * UPDATES.index(UPDATED[name]) + t + 1)
                    act.activation(SQ[:, t, :], src[:, t, :], ACT.Square).then_inc(n_sq, 1)

            def norm_rest(name):
                n, groups = NINFO[name]
                hh, _ = target(name)
                k = NSUMS[name]
                act.wait_ge(n_sum, k + 1)
                if name == "ctx":
                    act.wait_ge(res_tile, KT * (UPDATES.index("mid") + 1))
                for g, (a, b, width) in enumerate(groups):
                    last = act.activation(STD[:, g, :], bank[SUM_BANK(name, g)][:, T * (g % 2):T * (g % 2) + T], ACT.Sqrt,
                                          bias=eps, scale=1.0 / width)
                last.then_inc(n_std, 1)
                if name in ("mid", "final"):
                    return
                if name == "mix0":
                    hi_upto(0)
                if name in MODULATED:
                    act.wait_ge(gain_ready, MODORD[name] + 1)
                for t in range(n):
                    act.wait_ge(n_app, NAPP(name) + t + 1)
                    if name in MODULATED:
                        act.activation(hh[:, t, :], TN[:, t, :], ACT.Identity, bias=shift(name, t)).then_inc(n_hi, 1)
                    else:
                        act.activation(hh[:, t, :], TN[:, t, :], ACT.Copy).then_inc(n_hi, 1)

            def plain_hi(name):
                n, _ = NINFO[name]
                hh, _ = target(name)
                source_ready(name)
                for t in range(n):
                    act.activation(hh[:, t, :], Y[:, t, :], ACT.Copy).then_inc(n_hi, 1)

            def evacuate(dst, src, o, block_, func=ACT.Copy, scale=1.0, **kw):
                if block_ is not None:
                    hi_upto(block_ + 2)
                wait_full(act, o)
                act.activation(dst, src, func, scale=scale, **kw).then_inc(free[o % 4], 1)

            def mark():
                st["ev"] += 1
                act.copy(VS[:, 5:6], eps).then_inc(evac, 1)
                act.wait_ge(evac, st["ev"])

            def blk(stage, tiles):
                return (P0[stage] + tiles - 1) // TPB

            def attend(h0, n, o0, keys, single):
                table(ACT.Exp)
                for a in range(n + 2):
                    if a < n:
                        h = h0 + a
                        act.wait_ge(max_ready, h + 1)
                        if h >= 2:
                            act.wait_ge(pt_full, h - 1)
                        for qt in range(2):
                            src = bank[qt][:, :] if single else bank[h % 2][:, qt * T:qt * T + T]
                            c = 2 * (h % 2) + qt
                            last = act.activation(probs(h, single)[:, qt, :], src, ACT.Exp, bias=NM[:, c:c + 1], scale=1.0,
                                                  accum_out=SM[:, c:c + 1])
                        last.then_inc(exp_done, 1)
                    if a >= 2:
                        h, o = h0 + a - 2, o0 + a - 2
                        if a >= 4:
                            wait_full(act, o - 2)
                        act.wait_ge(pt_full, h + 1)
                        for j in range(keys // T):
                            last = act.activation(probs_t(h, single)[:, 2 * j:2 * j + 2, :],
                                                  bank[2 + (j if single else h % 2)][:, :].rearrange("p (a t) -> p a t", a=2),
                                                  ACT.Copy)
                        last.then_inc(pt_copied, 1)

            def ffn(name):
                f, b0 = FI[name], P0[name] // TPB
                conv = name in ("f0", "f1")
                table(ACT.Silu)
                hi_upto(b0 + 3)

                def group(g2, cnt, i, gs, n):
                    def at(m):
                        return cnt + m if i is None else i * 2 + (cnt + m)
                    act.wait_ge(w_used, n + 2 if i is None else i * PERIT + (n + 2))
                    gb, vb = bank[4 + 2 * g2], bank[5 + 2 * g2]
                    if conv:
                        if f or gs:
                            act.wait_ge(g_lo, at(0))
                        for part, (b, buf) in enumerate(((gb, A_CG), (vb, A_CV))):
                            for ft in range(2):
                                col = PCOL[f"conv{f}"] + 4 * (NF * part + ft) + 8 * gs
                                if i is None:
                                    w, bb = PAR[:, col + 1:col + 2], PAR[:, col + 3:col + 4]
                                else:
                                    w, bb = PAR[:, bass.ds(i * 16 + (col + 1), 1)], PAR[:, bass.ds(i * 16 + (col + 3), 1)]
                                last = act.activation(AR[:, buf + ft * T:buf + ft * T + T], b[:, ft * T:ft * T + T],
                                                      ACT.Identity, bias=bb, scale=w)
                        last.then_inc(affine, 1)
                    else:
                        act.wait_ge(up_free, at(1))
                        act.activation(AR[:, A_CG:A_CG + 512], gb[:, :], ACT.Silu).then_inc(silu_done, 1)

                def group_end(g2, cnt, i):
                    def at(m):
                        return cnt + m if i is None else i * 2 + (cnt + m)
                    if conv:
                        act.wait_ge(up_free, at(2))
                        act.activation(AR[:, A_CG:A_CG + 512], AR[:, A_CG:A_CG + 512], ACT.Silu).then_inc(silu_done, 1)
                        act.wait_ge(gate_out, at(1))
                    else:
                        act.wait_ge(up_free, at(2))
                    act.activation(Gh[:, 2 * g2:2 * g2 + 2, :].rearrange("p a t -> p (a t)"), AR[:, A_CV:A_CV + 512],
                                   ACT.Copy).then_inc(g_hi, 1)

                group(0, NG * f, None, 0, b0)
                group_end(0, NG * f, None)
                assert st["hi"] == b0 + 4
                with act.Fori(0, LOOPS) as i:
                    for c in range(2):
                        n0 = b0 + 2 + 3 * c
                        split_hi(n0 + 2, i)
                        split_hi(n0 + 3, i)
                        group((1 + c) % 2, NG * f + 1 + c, i, 1 + c, n0)
                        split_hi(n0 + 4, i)
                        group_end((1 + c) % 2, NG * f + 1 + c, i)
                st["hi"] = b0 + 34
                table(ACT.Sqrt)
                hi_upto(b0 + 34)

            act.wait_ge(const_in, 16)
            for l in range(DEPTH):
                QM, KM, VM, QB, VB = ar(A_QM, 6), ar(A_KM, 6), ar(A_VM, 2, 384), ar(A_QB, 4), ar(A_VB, 2, 128)
                C, KP, GV, U, VV = ar(A_C, 3), ar(A_KP, 1), ar(A_GV, 1), ar(A_U, 2), ar(A_VV, 2)
                norm(f"mix{l}")
                hi_upto(P0[f"in{l}"] // TPB + 2)
                if l == 0:
                    act.wait_ge(const_rest, 16)
                    act.wait_ge(par_rest, 16)
                o, s = O0[f"in{l}"], f"in{l}"
                for m in range(3):
                    evacuate(C[:, m, :], obank(o + m)[:, 0:T], o + m, blk(s, 8 * m + 8))
                evacuate(KP[:, 0, :], obank(o + 3)[:, 0:T], o + 3, blk(s, 32))
                mark()
                norm_square(f"c{l}")
                for m in range(3):
                    evacuate(QB[:, m, :], obank(o + 4 + m)[:, 0:T], o + 4 + m, blk(s, 8 * m + 40))
                norm_rest(f"c{l}")
                evacuate(QB[:, 3, :], obank(o + 7)[:, 0:T], o + 7, blk(s, 64))
                evacuate(GV[:, 0, :], obank(o + 8)[:, 0:T], o + 8, blk(s, 72))
                for m in range(2):
                    evacuate(U[:, m, :], obank(o + 9 + m)[:, 0:T], o + 9 + m, blk(s, 80 + 8 * m), ACT.Gelu_apprx_tanh)
                for tt in range(2):
                    o = O0[f"vv{l}"] + tt
                    evacuate(VV[:, tt, :], obank(o)[:, 0:T], o, blk(f"vv{l}", 16), ACT.Gelu_apprx_tanh)
                mark()
                for tt in range(2):
                    act.activation(TN[:, 6 + tt, :], VV[:, tt, :], ACT.Square, accum_out=VS[:, tt:tt + 1])
                act.activation(SQ[:, 4:8, :], QB[:, 0:4, :], ACT.Square).then_inc(qk_sq, 1)
                act.wait_ge(qk_sq, l + 1)
                act.activation(VS[:, 2:4], VS[:, 0:2], ACT.Sqrt, bias=eps, scale=1.0 / 256).then_inc(vv_std, 1)
                act.wait_ge(qk_sum, l + 1)
                act.wait_ge(n_lo, NTILES[f"c{l}"] + 3)
                for j in range(2):
                    last = act.activation(STD[:, 2 * j:2 * j + 2, :].rearrange("p a t -> p (a t)"), bank[2 + j][:, :],
                                          ACT.Sqrt, bias=eps, scale=1.0 / 64)
                last.then_inc(qk_std, 1)
                o = O0[f"gvt{l}"]
                evacuate(VB[:, :, :].rearrange("p a t -> p (a t)"), obank(o)[:, 0:T], o, None)
                for m in range(6):
                    o = O0[f"uq{l}"] + m
                    evacuate(QM[:, m, :], obank(o)[:, 0:T], o, blk(f"uq{l}", 2 * m + 2), scale=96.0 ** -0.5)
                mark()
                for m in range(3):
                    o = O0[f"nope{l}"] + m
                    hi_upto(blk(f"nope{l}", m + 1) + 2)
                    wait_full(act, o)
                    act.activation(KM[0:64, 2 * m, :], obank(o)[0:64, 0:T], ACT.Copy)
                    act.activation(KM[64:128, 2 * m + 1, :], obank(o)[64:128, 0:T], ACT.Copy).then_inc(free[o % 4], 1)
                for tt in range(2):
                    o = O0[f"va{l}"] + tt
                    evacuate(VM[:, tt, :], obank(o)[:, 0:384], o, blk(f"va{l}", 3))
                mark()
                hi_upto(blk(f"pad{l}", 6) + 3)
                attend(16 * l, 12, O0[f"att{l}"], T, False)
                norm(f"y{l}")
                for m in range(8):
                    hi_upto(blk(f"out{l}", 8 * m + 8) + 2)
                if l == 0:
                    act.wait_ge(mem_in, 16)
                norm(f"mem{l}")
                MK, MV, MQ = ar(A_MK, 4), ar(A_MV, 2, 512), ar(A_MQ, 4)
                for m in range(4):
                    o = O0[f"mk{l}"] + m
                    evacuate(MK[:, m, :], obank(o)[:, 0:T], o, blk(f"mk{l}", 8 * m + 8))
                for j in range(4):
                    o = O0[f"mv{l}"] + j
                    evacuate(MV[:, j % 2, T * (j // 2):T * (j // 2) + T], obank(o)[:, 0:T], o, blk(f"mv{l}", 16 * (j // 2) + 16))
                norm(f"memx{l}")
                for m in range(4):
                    o = O0[f"mq{l}"] + m
                    evacuate(MQ[:, m, :], obank(o)[:, 0:T], o, blk(f"mq{l}", 8 * m + 8), scale=128.0 ** -0.5)
                mark()
                hi_upto(blk(f"mq{l}", 32) + 3)
                attend(16 * l + 12, 4, O0[f"matt{l}"], T, False)
                norm(f"my{l}")
                if l == 0:
                    act.wait_ge(c_in, 32)
                    act.activation(cb[:, :, :], cb[:, :, :], ACT.Silu).then_inc(c_silu, 1)
                hi_upto(blk(f"mo{l}", 16) + 2)
                hi_upto(blk(f"mo{l}", 32) + 2)
                norm(f"f{l}")
                ffn(f"f{l}")
            norm("mid")
            act.wait_ge(ctx_in, 16)
            norm("ctx")
            ffn("ctx")
            norm("x0a")
            ffn("x0a")
            norm("cn")
            Q, KL, KC, VL, VC, UT = ar(A_Q, 4), ar(A_KL, 4), ar(A_KC, 4), ar(A_VL, 2, 512), ar(A_VC, 2, 512), ar(A_UT, 2, 512)

            def feat(stage, buf, scale=1.0, order=lambda v: v):
                for m in range(4):
                    o = O0[stage] + m
                    src = obank(o)[:, 0:T] if order is not backwards else obank(o)[:, 0:T].rearrange("p (r c) -> p r c", r=4)
                    evacuate(order(buf[:, m, :]), src, o, blk(stage, 8 * m + 8), scale=scale)

            def tok(stage, buf):
                for j in range(4):
                    o = O0[stage] + j
                    evacuate(buf[:, j % 2, T * (j // 2):T * (j // 2) + T], obank(o)[:, 0:T], o, blk(stage, 16 * (j // 2) + 16))

            feat("ck", KC)
            tok("cv", VC)
            norm("xn")
            feat("eq", Q, 0.125, backwards)
            feat("ek", KL)
            tok("ev", VL)
            tok("eu", UT)
            mark()
            for g in range(4):
                o = O0["pooled"] + g
                wait_full(act, o)
                act.activation(Gh[:, g, :], obank(o)[:, 0:T], ACT.Copy).then_inc(g_hi, 1)
                hi_upto(blk("pool", 4) + 2)
            for g in range(4):
                o = O0["pool"] + g
                wait_full(act, o)
                act.activation(Y[:, 4 + g, :], obank(o)[:, 0:T], ACT.Copy, scale=par("ps", g)).then_inc(free[o % 4], 1)
            mark()
            hi_upto(blk("padp", 12) + 3)
            attend(32, 8, O0["natt"], 512, True)
            norm("ey")
            for m in range(8):
                hi_upto(blk("eo", 8 * m + 8) + 2)
            norm("x0b")
            ffn("x0b")
            norm("x1a")
            ffn("x1a")
            norm("x1n")
            for t in range(KT):
                o = O0["cin"] + 3 * t + 1
                if t >= 2:
                    act.wait_ge(y_half, YV("cin", t - 2))
                hi_upto(blk("cin", 24 * t + 8) + 2)
                wait_full(act, o - 1)
                act.activation(AR[:, A_BG + T * (t % 2):A_BG + T * (t % 2) + T], obank(o - 1)[:, 0:T],
                               ACT.Copy).then_inc(free[(o - 1) % 4], 1)
                hi_upto(blk("cin", 24 * t + 16) + 2)
                wait_full(act, o)
                act.activation(AR[:, A_CG + T * (t % 2):A_CG + T * (t % 2) + T], obank(o)[:, 0:T],
                               ACT.Copy).then_inc(z_copy, 1)
                hi_upto(blk("cin", 24 * t + 24) + 2)
            norm("oy")
            for m in range(8):
                hi_upto(blk("co", 8 * m + 8) + 2)
            norm("x1b")
            ffn("x1b")
            norm("final")

        @block.vector
        def _(dve):
            chain = Chain(dve, dve_step)
            link = chain.link
            st = {"lo": 0, "y": 0}
            fl = lambda v: v.rearrange("p a t -> p (a t)")

            def split_lo(n, i=None):
                dve.wait_ge(hi_ready, n + 1 if i is None else i * PERIT + (n + 1))
                dve.tensor_tensor(wlo[:, n % RING, :], wraw[:, n % RAW, :], whi[:, n % RING, :].bitcast(F32),
                                  ALU.subtract).then_inc(lo_ready, 1)

            def lo_upto(n):
                while st["lo"] <= min(n, NBLK):
                    split_lo(st["lo"])
                    st["lo"] += 1

            def blk(stage, tiles):
                return (P0[stage] + tiles - 1) // TPB

            def norm(name):
                n, groups = NINFO[name]
                src, (hh, hl) = source(name), target(name)
                k = NSUMS[name]
                if groups:
                    if name in MODULATED:
                        modulated_gain(name)
                    dve.wait_ge(n_std, k + 1)
                    if NTILES[name]:
                        dve.wait_ge(n_lo, NTILES[name])
                    group_of = {t: g for g, (a, b, _) in enumerate(groups) for t in range(a, b)}

                    if name == "mix0":
                        lo_upto(0)

                    def apply(t):
                        rstd = STD[:, group_of[t], :]
                        if t == groups[group_of[t]][0]:
                            link(dve.reciprocal(rstd, rstd))
                        if name in ("mid", "final"):
                            dst, done_ = (X, res_tile) if name == "mid" else (SQ, n_app)
                        else:
                            dst, done_ = TN, n_app
                        dve.scalar_tensor_tensor(dst[:, t, :], src[:, t, :], gain(name, t), rstd, ALU.mult,
                                                 ALU.mult).then_inc(done_, 1)

                    def low(t):
                        dve.wait_ge(n_hi, NTILES[name] + t + 1)
                        if name in MODULATED:
                            dve.scalar_tensor_tensor(hl[:, t, :], TN[:, t, :], shift(name, t), hh[:, t, :].bitcast(F32),
                                                     ALU.add, ALU.subtract).then_inc(n_lo, 1)
                        else:
                            dve.tensor_tensor(hl[:, t, :], TN[:, t, :], hh[:, t, :].bitcast(F32),
                                              ALU.subtract).then_inc(n_lo, 1)

                    if name in ("mid", "final"):
                        for t in range(n):
                            apply(t)
                        return
                    for t in range(n + LAG):
                        if t < n:
                            apply(t)
                        if t >= LAG:
                            low(t - LAG)
                    return
                for t in range(n):
                    dve.wait_ge(n_hi, NTILES[name] + t + 1)
                    dve.tensor_tensor(hl[:, t, :], Y[:, t, :], hh[:, t, :].bitcast(F32), ALU.subtract).then_inc(n_lo, 1)

            def modulated_gain(name):
                m, base, j, g = MODULATED[name]
                if name in UPDATED:
                    dve.wait_ge(res_tile, KT * (UPDATES.index(UPDATED[name]) + 1))
                link(dve.scalar_tensor_tensor(GS[:, :], m[:, base + 8 * (j + 1):base + 8 * (j + 2)], 1.0, par(g, 0, 8),
                                              ALU.add, ALU.mult))
                dve.tensor_scalar(HG[:, :], m[:, base + 8 * (j + 2):base + 8 * (j + 3)] if name != "cn" else GS[:, :],
                                  1.0 if j == 3 else 0.5, None, ALU.mult).then_inc(gain_ready, 1)

            def attend(h0, n, o0, keys, single, put, bias=None):
                for a in range(n + 3):
                    if a < n:
                        h = h0 + a
                        dve.wait_ge(s_full, h + 1)
                        c = 2 * (h % 2)
                        if bias is not None:
                            for qt in range(2):
                                last = dve.tensor_tensor(bank[qt][:, 0:T], bank[qt][:, 0:T], bias(a, qt), ALU.add)
                            link(last)
                        if h >= 2:
                            dve.wait_ge(exp_done, h - 1)
                        if single:
                            for qt in range(2):
                                last = dve.tensor_reduce(NM[:, c + qt:c + qt + 1], bank[qt][:, :], AXX, ALU.max, negate=True)
                            last.then_inc(max_ready, 1)
                        else:
                            dve.tensor_reduce(NM[:, c:c + 2], bank[h % 2][:, :].rearrange("p (q k) -> p q k", q=2), AXX,
                                              ALU.max, negate=True).then_inc(max_ready, 1)
                    if 1 <= a <= n:
                        h = h0 + a - 1
                        c = 2 * (h % 2)
                        dve.wait_ge(exp_done, h + 1)
                        link(dve.reciprocal(RI[:, c:c + 2], SM[:, c:c + 2]))
                        for qt in range(2):
                            p = probs(h, single)[:, qt, :]
                            last = dve.tensor_scalar(p, p, RI[:, c + qt:c + qt + 1], None, ALU.mult)
                        last.then_inc(prob_ready, 1)
                    if a >= 3:
                        o = o0 + a - 3
                        wait_full(dve, o)
                        dst, rows = put(a - 3)
                        src = obank(o)[rows, 0:T]
                        if single:
                            dst, src = backwards(dst), src.rearrange("p (r c) -> p r c", r=4)
                        dve.tensor_copy(dst, src).then_inc(free[o % 4], 1)
                done()

            def done():
                st["y"] += 1
                dve.tensor_copy(VS[:, 4:5], eps).then_inc(y_half, 1)
                dve.wait_ge(y_half, st["y"])

            def ffn(name):
                f, b0 = FI[name], P0[name] // TPB
                conv = name in ("f0", "f1")
                l = 0 if name == "f0" else 1
                per = MODS_PER_IT.get(name, 0)
                if name == "f0":
                    dve.wait_ge(c_silu, 1)
                lo_upto(b0 + 3)

                def group(g2, cnt, i, gs):
                    def at(m):
                        return cnt + m if i is None else i * 2 + (cnt + m)
                    gb, vb = bank[4 + 2 * g2], bank[5 + 2 * g2]
                    if conv:
                        dve.wait_ge(affine, at(1))
                        for tap, (d0, s0) in ((0, (1, 0)), (2, (0, 1))):
                            for part, (b, buf) in enumerate(((gb, A_CG), (vb, A_CV))):
                                for ft in range(2):
                                    col = PCOL[f"conv{l}"] + 4 * (NF * part + ft) + tap + 8 * gs
                                    w = PAR[:, col:col + 1] if i is None else PAR[:, bass.ds(i * 16 + col, 1)]
                                    dst = AR[:, buf + ft * T + d0:buf + ft * T + d0 + T - 1]
                                    last = dve.scalar_tensor_tensor(dst, b[:, ft * T + s0:ft * T + s0 + T - 1], w, dst,
                                                                    ALU.mult, ALU.add)
                            if tap == 0:
                                link(last)
                        last.then_inc(up_free, 1)

                def product(g2, cnt, i, gs):
                    def at(m):
                        return cnt + m if i is None else i * 2 + (cnt + m)
                    vb = bank[5 + 2 * g2]
                    dve.wait_ge(silu_done, at(1))
                    if conv:
                        dve.tensor_tensor(AR[:, A_CV:A_CV + 512], AR[:, A_CG:A_CG + 512], AR[:, A_CV:A_CV + 512],
                                          ALU.mult).then_inc(gate_out, 1)
                    else:
                        dve.wait_ge(g_lo, at(0))
                        dve.tensor_tensor(AR[:, A_CV:A_CV + 512], AR[:, A_CG:A_CG + 512], vb[:, :],
                                          ALU.mult).then_inc(up_free, 1)

                def low(g2, cnt, i):
                    dve.wait_ge(g_hi, GX(name) + cnt + 1 if i is None else i * 2 + (GX(name) + cnt + 1))
                    dve.tensor_tensor(fl(Gl[:, 2 * g2:2 * g2 + 2, :]), AR[:, A_CV:A_CV + 512],
                                      fl(Gh[:, 2 * g2:2 * g2 + 2, :]).bitcast(F32), ALU.subtract).then_inc(g_lo, 1)

                def mods(u, count, i):
                    for k in range(count):
                        mod(u + k, k, i)
                    mod_columns(u, count, i)

                def mod(uu, k, i):
                    if True:
                        ld = 16 * (uu // MODRING + 1)
                        dve.wait_ge(mod_loaded[uu % MODRING], ld if i is None else i * (16 * per // MODRING) + ld)
                        slot = modw[:, uu % MODRING, :]
                        sc = PR[:, :, :].rearrange("p a k -> p (a k)")
                        if name in MOD_BOTH:
                            dve.wait_ge(mod_used, uu + MODRING if i is None else i * per + (uu + MODRING))
                            dve.tensor_tensor_reduce(sc, slot, cb[:, 1, :], 1.0, 0.0, ALU.mult, ALU.add, MSC[:, 1, k:k + 1])
                        dve.tensor_tensor_reduce(slot, slot, cb[:, 0, :], 1.0, 0.0, ALU.mult, ALU.add,
                                                 MSC[:, 0, k:k + 1]).then_inc(mod_used, 1)

                def mod_columns(u, count, i):
                    dve.wait_ge(mod_used, u + count + MODRING if i is None else i * per + (u + count + MODRING))
                    if i is None:
                        if name in MOD_BOTH:
                            dve.tensor_copy(MODC[:, u:u + count], MSC[:, 1, 0:count])
                        link(dve.tensor_copy(MODL[:, u:u + count], MSC[:, 0, 0:count]))
                    else:
                        if name in MOD_BOTH:
                            dve.tensor_copy(MODC[:, bass.ds(i * per + u, count)], MSC[:, 1, 0:count])
                        link(dve.tensor_copy(MODL[:, bass.ds(i * per + u, count)], MSC[:, 0, 0:count]))

                group(0, NG * f, None, 0)
                product(0, NG * f, None, 0)
                low(0, NG * f, None)
                with dve.Fori(0, LOOPS) as i:
                    chain.enter(i, (2 if conv else 0) + (2 if per else 0))
                    for c in range(2):
                        n0 = b0 + 2 + 3 * c
                        g2 = (1 + c) % 2
                        u0 = MOD_START.get(name, 0) + per // 2 * c
                        split_lo(n0 + 2, i)
                        if per > 2:
                            mod(u0, 0, i)
                        split_lo(n0 + 3, i)
                        if per > 4:
                            mod(u0 + 1, 1, i)
                        group(g2, NG * f + 1 + c, i, 1 + c)
                        if not conv:
                            product(g2, NG * f + 1 + c, i, 1 + c)
                        split_lo(n0 + 4, i)
                        if conv:
                            product(g2, NG * f + 1 + c, i, 1 + c)
                        low(g2, NG * f + 1 + c, i)
                        if per:
                            mod(u0 + per // 2 - 1, per // 2 - 1, i)
                            mod_columns(u0, per // 2, i)
                    chain.leave(LOOPS)
                st["lo"] = b0 + 34
                if name in MODS_AFTER:
                    mods(MOD_START[name] + per * LOOPS, MODS_AFTER[name], None)
                res = CX if name == "ctx" else X
                for m in range(KT):
                    if m % 2 == 0:
                        if m < KT - 2:
                            dve.wait_ge(down_full, 3 * f + m // 2 + 1)
                        else:
                            dve.wait_ge(w_used, b0 + 33)
                    b = bank[m // 2][:, T * (m % 2):T * (m % 2) + T]
                    if conv:
                        dve.tensor_tensor(res[:, m, :], res[:, m, :], b, ALU.add).then_inc(res_tile, 1)
                    else:
                        dve.scalar_tensor_tensor(res[:, m, :], b, HG[:, m:m + 1], res[:, m, :], ALU.mult,
                                                 ALU.add).then_inc(res_tile, 1)
                if name in ("f1", "ctx", "x0a", "x0b", "x1a"):
                    u = 0 if name == "f1" else MOD_START[name]
                    e = MOD_START[name] + per * LOOPS + MODS_AFTER[name]
                    if name in MOD_BOTH:
                        dve.tensor_tensor(MODC[:, u:e], MODC[:, u:e], par("mb0", u, e - u), ALU.add)
                    link(dve.tensor_tensor(MODL[:, u:e], MODL[:, u:e], par("mb0", u, e - u), ALU.add))

            def residual(stage, kt, gated=False):
                for m in range(KT):
                    o = O0[stage] + m
                    lo_upto(blk(stage, kt * m + kt) + 2)
                    wait_full(dve, o)
                    b = obank(o)[:, 0:T]
                    if gated:
                        dve.scalar_tensor_tensor(X[:, m, :], b, HG[:, m:m + 1], X[:, m, :], ALU.mult,
                                                 ALU.add).then_inc(res_tile, 1)
                    else:
                        dve.tensor_tensor(X[:, m, :], X[:, m, :], b, ALU.add).then_inc(res_tile, 1)
                    if m < KT - 4:
                        dve.wait_ge(res_tile, KT * UPDATES.index(stage) + m + 1)
                        dve.nop().then_inc(free[o % 4], 1)
                dve.wait_ge(res_tile, KT * UPDATES.index(stage) + KT)
                for m in range(KT - 4, KT):
                    dve.nop().then_inc(free[(O0[stage] + m) % 4], 1)

            dve.memset(VS[:, 0:1], 0.0).then_inc(up_free, 1)
            for j in range(MODRING):
                dve.memset(VS[:, 1 + j:2 + j], 0.0).then_inc(mod_used, 1)
            dve.memset(ZB[:, :], 0.0).then_inc(zeros_ready, 1)
            dve.wait_ge(par_in, 16)
            dve.wait_ge(x_in, 32)
            for l in range(DEPTH):
                QM, KM, QB = ar(A_QM, 6), ar(A_KM, 6), ar(A_QB, 4)
                KP, U, VV, RT = ar(A_KP, 1), ar(A_U, 2), ar(A_VV, 2), ar(A_RT, 2)
                norm(f"mix{l}")
                lo_upto(P0[f"in{l}"] // TPB + 2)
                if l == 0:
                    dve.wait_ge(const_rest, 16)
                    dve.wait_ge(par_rest, 16)
                lo_upto(blk(f"in{l}", 56) + 2)
                norm(f"c{l}")
                lo_upto(blk(f"in{l}", 88) + 2)
                lo_upto(blk(f"vv{l}", 16) + 2)
                dve.wait_ge(vv_std, l + 1)
                link(dve.reciprocal(VS[:, 2:4], VS[:, 2:4]))
                dve.wait_ge(sw_in, 96 * (l + 1))
                for tt in range(2):
                    last = dve.scalar_tensor_tensor(VV[:, tt, :], VV[:, tt, :], VS[:, 2 + tt:3 + tt], SW[:, 512:768],
                                                    ALU.mult, ALU.mult)
                last.then_inc(vv_ready, 1)
                o = O0[f"krot{l}"]
                wait_full(dve, o)
                link(dve.tensor_tensor(RT[:, 0, :], obank(o)[:, 0:T], con("sk", T), ALU.mult))
                dve.nop().then_inc(free[o % 4], 1)
                link(dve.tensor_tensor(KP[:, 0, :], KP[:, 0, :], con("ck", T), ALU.mult))
                for par_, r in ((0, slice(64, 128)), (1, slice(0, 64))):
                    last = dve.tensor_tensor(KM[r, par_:6:2, :], KP[r, 0:1, :].to_broadcast([64, 3, T]),
                                             RT[r, 0:1, :].to_broadcast([64, 3, T]), ALU.add)
                link(last)
                dve.wait_ge(qk_std, l + 1)
                link(dve.reciprocal(STD[:, :, :], STD[:, :, :]))
                link(dve.tensor_tensor(QB[:, :, :], QB[:, :, :], STD[:, :, :], ALU.mult))
                dve.tensor_scalar(QB[:, 0:3, :], QB[:, 0:3, :], par(f"gq{l}"), 0.125, ALU.mult, ALU.mult)
                dve.tensor_scalar(QB[:, 3, :], QB[:, 3, :], par(f"gk{l}"), None, ALU.mult).then_inc(qk_norm, 1)
                o = O0[f"mix{l}"]
                wait_full(dve, o)
                MX = obank(o)[:, :].rearrange("p (g n t) -> p g n t", g=2, n=2)
                YC = Y[:, 6:8, :].rearrange("p g (n t) -> p g n t", n=2)
                BS = SW[:, 768:1024].rearrange("p (g t) -> p g t", g=2)
                for n in range(2):
                    last = dve.tensor_tensor(YC[:, :, n, :], MX[:, :, n, :], BS, ALU.add)
                link(last)
                dve.nop().then_inc(free[o % 4], 1)
                dve.tensor_tensor(Y[:, 6:8, :], Y[:, 6:8, :], U[:, :, :], ALU.mult).then_inc(mixed_done, 1)
                lo_upto(blk(f"uq{l}", 12) + 2)
                lo_upto(blk(f"pad{l}", 6) + 2)
                dve.wait_ge(mixed_done, l + 1)
                dve.wait_ge(qk_norm, l + 1)
                for j in range(2):
                    o = O0[f"gqrot{l}"] + j
                    wait_full(dve, o)
                    link(dve.tensor_tensor(RT[:, :, :], obank(o)[:, :].rearrange("p (a t) -> p a t", a=2),
                                           con("sg", T)[:, None, :].to_broadcast([P, 2, T]), ALU.mult))
                    dve.nop().then_inc(free[o % 4], 1)
                    q = QB[:, 2 * j:2 * j + 2, :]
                    link(dve.tensor_tensor(q, q, con("cg", T)[:, None, :].to_broadcast([P, 2, T]), ALU.mult))
                    link(dve.tensor_tensor(q, q, RT[:, :, :], ALU.add))
                for j in range(3):
                    o = O0[f"qrot{l}"] + j
                    wait_full(dve, o)
                    for e, r in ((0, slice(64, 128)), (1, slice(0, 64))):
                        last = dve.tensor_tensor(RT[r, e, :], obank(o)[r, e * T:e * T + T], con("sk", T)[r, :], ALU.mult)
                    link(last)
                    dve.nop().then_inc(free[o % 4], 1)
                    for e, r in ((0, slice(64, 128)), (1, slice(0, 64))):
                        last = dve.tensor_tensor(QM[r, 2 * j + e, :], QM[r, 2 * j + e, :], con("ck", T)[r, :], ALU.mult)
                    link(last)
                    for e, r in ((0, slice(64, 128)), (1, slice(0, 64))):
                        last = dve.tensor_tensor(QM[r, 2 * j + e, :], QM[r, 2 * j + e, :], RT[r, e, :], ALU.add)
                    link(last)
                dve.nop().then_inc(rope_in, 1)
                lo_upto(blk(f"pad{l}", 6) + 3)

                def put(a):
                    if a < 6:
                        r = slice(64 * (a % 2), 64 * (a % 2) + 64)
                        return Y[r, a // 2, :], r
                    b = a - 6
                    r = slice(64 * (b // 3), 64 * (b // 3) + 64)
                    return Y[r, 3 + b % 3, :], r

                attend(16 * l, 12, O0[f"att{l}"], T, False, put)
                norm(f"y{l}")
                residual(f"out{l}", 8)
                norm(f"mem{l}")
                lo_upto(blk(f"mk{l}", 32) + 2)
                lo_upto(blk(f"mv{l}", 32) + 2)
                norm(f"memx{l}")
                lo_upto(blk(f"mq{l}", 32) + 3)
                attend(16 * l + 12, 4, O0[f"matt{l}"], T, False, lambda a: (Y[:, a, :], slice(0, P)))
                norm(f"my{l}")
                residual(f"mo{l}", 4)
                norm(f"f{l}")
                ffn(f"f{l}")
            norm("mid")
            dve.wait_ge(ctx_in, 16)
            norm("ctx")
            ffn("ctx")
            norm("x0a")
            ffn("x0a")
            norm("cn")
            lo_upto(blk("ck", 32) + 2)
            lo_upto(blk("cv", 32) + 2)
            norm("xn")
            for s in ("eq", "ek", "ev", "eu"):
                lo_upto(blk(s, 32) + 2)
            for g in range(4):
                o = O0["pooled"] + g
                dve.wait_ge(g_hi, NG * 4 + g + 1)
                dve.tensor_tensor(Gl[:, g, :], obank(o)[:, 0:T], Gh[:, g, :].bitcast(F32), ALU.subtract).then_inc(free[o % 4], 1)
                done()
            lo_upto(blk("pool", 4) + 2)
            dve.wait_ge(bias_in, 16 * 32)
            link(dve.tensor_tensor(NS[:, :, :, :].rearrange("p a k (r c) -> p (a k r) c", c=64),
                                   NS[:, :, :, :].rearrange("p a k (r c) -> p (a k r) c", c=64),
                                   con("mask", 64)[:, None, :].to_broadcast([P, 64, 64]), ALU.add))
            lo_upto(blk("padp", 12) + 3)
            BI = NS[:, :, :, :].rearrange("p a k t -> p (a k) t")
            attend(32, 8, O0["natt"], 512, True,
                   lambda a: (Y[64 * (a % 2):64 * (a % 2) + 64, a // 2, :], slice(64 * (a % 2), 64 * (a % 2) + 64)),
                   bias=lambda a, qt: BI[:, 2 * a + qt, :])
            dve.wait_ge(evac, EV(2, "ps"))
            norm("ey")
            residual("eo", 8, gated=True)
            norm("x0b")
            ffn("x0b")
            norm("x1a")
            ffn("x1a")
            norm("x1n")
            for t in range(KT):
                oc, ox = (O0["cin"] + 3 * t + j for j in (1, 2))
                lo_upto(blk("cin", 24 * t + 24) + 2)
                dve.wait_ge(z_copy, t + 1)
                dve.nop().then_inc(free[oc % 4], 1)
                wait_full(dve, ox)
                z, zc, cg = AR[:, 512:512 + T], AR[:, 1024:1024 + T], AR[:, A_CG + T * (t % 2):A_CG + T * (t % 2) + T]
                link(dve.tensor_tensor(z, cg, obank(ox)[:, 0:T], ALU.mult))
                dve.nop().then_inc(free[ox % 4], 1)
                link(dve.tensor_scalar(zc, z, par("cw", 8 + t), None, ALU.mult))
                link(dve.scalar_tensor_tensor(zc[:, 1:T], z[:, 0:T - 1], par("cw", t), zc[:, 1:T], ALU.mult, ALU.add))
                link(dve.scalar_tensor_tensor(zc[:, 0:T - 1], z[:, 1:T], par("cw", 16 + t), zc[:, 0:T - 1], ALU.mult, ALU.add))
                link(dve.tensor_tensor(Y[:, t, :], zc, AR[:, A_BG + T * (t % 2):A_BG + T * (t % 2) + T], ALU.mult))
                done()
            norm("oy")
            residual("co", 8, gated=True)
            norm("x1b")
            ffn("x1b")
            norm("final")


def weight_blocks(a):
    stream = np.zeros((NBLK + 1, P, TPB, P), np.float32)
    tiles = stream.transpose(0, 2, 1, 3)

    def put(p, rows, cols=slice(0, P)):
        tiles[p // TPB, p % TPB][:, cols] = rows

    def feature(stage, w, cols, p=None):
        p = P0[stage] if p is None else p
        for c in cols:
            for k in range(w.shape[0] // P):
                put(p, w[k * P:k * P + P, c])
                p += 1
        return p

    def wide(stage, w, cols):
        p = P0[stage]
        for k in range(w.shape[0] // P):
            for c in cols:
                put(p, w[k * P:k * P + P, c])
                p += 1

    def span(n, off=0):
        return [slice(off + m * P, off + m * P + P) for m in range(n)]

    def ffn(stage, up, down):
        b0 = P0[stage] // TPB
        for g in range(NG):
            n = b0 if g == 0 else b0 + 2 + 3 * (g - 1)
            d = b0 + 4 + 3 * g if g < NG - 1 else b0 + 32
            feature(None, up, span(2, 2 * g * P), n * TPB)
            feature(None, up, span(2, DFF + 2 * g * P), (n + 1) * TPB)
            for ft in range(2):
                r = (2 * g + ft) * P
                for m in range(KT):
                    put(d * TPB + ft * KT + m, down[r:r + P, m * P:m * P + P])

    for l in range(DEPTH):
        w = a["w_in"][l]
        q0, kr, gq, gk, gv, gm = 0, 384, 416, 800, 928, 1056
        pair = np.arange(64)
        p = feature(f"in{l}", w, [slice(256, 384), slice(0, 128), slice(128, 256)])
        for k in range(KT):
            put(p, w[k * P:k * P + P, kr:kr + 32], slice(32, 64))
            put(p, w[k * P:k * P + P, kr:kr + 32], slice(64, 96))
            p += 1
        p = feature(None, w, [np.concatenate([gq + 64 * t + pair, gq + 64 * (3 + t) + pair]) for t in range(3)], p)
        p = feature(None, w, [slice(gk, gk + P), slice(gv, gv + P), slice(gm, gm + P), slice(gm + P, gm + 2 * P)], p)
        wide(f"vv{l}", w, span(2, gm + 256))
        p = P0[f"uq{l}"]
        for h in range(6):
            for k in range(2):
                u = a["mla_w_uq"][l][k * P:k * P + P, h * 96:h * 96 + 96]
                put(p, u[:, 0:64], slice(64 * (h % 2), 64 * (h % 2) + 64))
                put(p, u[:, 64:96], slice(64, 96) if h % 2 == 0 else slice(32, 64))
                p += 1
        u = a["mla_w_ukv"][l]
        for m in range(3):
            for e in range(2):
                h = 2 * m + e
                put(P0[f"nope{l}"] + m, u[:, h * P:h * P + 64], slice(64 * e, 64 * e + 64))
                put(P0[f"va{l}"] + m, u[:, h * P + 64:h * P + P], slice(64 * e, 64 * e + 64))
        feature(f"out{l}", a["w_out"][l][mixed_order()], span(8))
        feature(f"mk{l}", a["mem_w_kv"][l], span(4))
        wide(f"mv{l}", a["mem_w_kv"][l], span(2, 512))
        p = P0[f"mv{l}"] + 16
        for k in range(KT):
            for c in span(2, 768):
                put(p, a["mem_w_kv"][l][k * P:k * P + P, c])
                p += 1
        feature(f"mq{l}", a["mem_w_q"][l], span(4))
        feature(f"mo{l}", a["mem_w_o"][l], span(8))
        ffn(f"f{l}", a["ffn_w_up"][l], a["ffn_w_down"][l])
    w13, w2, ein = a["ffn_w13_2"], a["ffn_w2_2"], a["even_w_in_2"][0]
    for name, i, j in (("ctx", 0, 0), ("x0a", 0, 0), ("x0b", 0, 1), ("x1a", 1, 0), ("x1b", 1, 1)):
        ffn(name, w13[i, j], w2[i, j])

    def halves(stage, w, off):
        for half in range(2):
            p = P0[stage] + 16 * half
            for k in range(KT):
                for c in span(2, off + 256 * half):
                    put(p, w[k * P:k * P + P, c])
                    p += 1

    feature("ck", ein, span(4, 512))
    halves("cv", ein, 1024)
    feature("eq", ein, span(4))
    feature("ek", ein, span(4, 512))
    halves("ev", ein, 1024)
    halves("eu", ein, 1536)
    for g in range(4):
        put(P0["pool"] + g, a["pool_w_2"][0, g])
    feature("eo", a["even_w_out_2"][0], span(8))
    cin = a["conv_w_in_2"][0]
    feature("cin", cin, [slice(j * D + t * P, j * D + t * P + P) for t in range(KT) for j in range(3)])
    feature("co", a["conv_w_out_2"][0], span(8))
    return stream.reshape(NBLK + 1, P, TPB * P)


def mixed_order():
    order = list(range(384))
    for t in range(3):
        order += list(range(384 + 64 * t, 384 + 64 * t + 64)) + list(range(384 + 64 * (3 + t), 384 + 64 * (3 + t) + 64))
    return np.array(order + list(range(768, 1024)))


def param_columns(a):
    out = np.zeros((P, NPAR), np.float32)

    def put(name, v):
        v = np.asarray(v).reshape(-1, P)
        out[:, PCOL[name]:PCOL[name] + v.shape[0]] = v.T

    for l in range(DEPTH):
        put(f"mix{l}", a["mix_norm"][l])
        put(f"c{l}", np.concatenate([a["mla_kv_norm"][l], a["mla_q_norm"][l]]))
        put(f"gq{l}", np.concatenate([a["gqa_q_norm"][l]] * 2))
        put(f"gk{l}", np.concatenate([a["gqa_k_norm"][l]] * 2))
        put(f"y{l}", a["out_norm"][l][mixed_order()])
        put(f"mem{l}", a["mem_kv_norm"][l])
        put(f"memx{l}", a["mem_x_norm"][l])
        put(f"f{l}", a["ffn_norm"][l])
        conv = out[:, PCOL[f"conv{l}"]:PCOL[f"conv{l}"] + 8 * NF].reshape(P, 2 * NF, 4)
        for tap in range(3):
            conv[:, :, tap] = a["ffn_conv_w"][l, tap].reshape(2 * NF, P).T
        conv[:, :, 3] = a["ffn_conv_b"][l].reshape(2 * NF, P).T
        out[:, PCOL[f"conv{l}"]:PCOL[f"conv{l}"] + 8 * NF] = conv.reshape(P, 8 * NF)
    for i in range(DEPTH):
        for j in range(3):
            put(f"ng{i}{j}", a["norm_g_2"][i, j])
        put(f"mb{i}", a["mod_b_2"][i])
    put("ps", a["pool_scale_2"][0])
    put("cw", a["conv_w_2"][0])
    put("mid", a["final_norm"])
    put("final", a["final_g_2"])
    return out


def rotary(d):
    n = d // 4
    inv = (np.float32(10000.0) ** (-np.arange(n, dtype=np.float32) / np.float32(n))).astype(np.float32)
    t = np.arange(T)
    ang = np.concatenate([(t // 64).astype(np.float32)[:, None] * inv, (t % 64).astype(np.float32)[:, None] * inv], axis=-1)
    ang = np.repeat(ang.T, 2, axis=0).astype(np.float32)
    return np.cos(ang), np.sin(ang)


def shape_constants():
    con = np.zeros((P, NCON), np.float32)

    def put(name, v):
        con[:, CCOL[name]:CCOL[name] + v.shape[1]] = v

    i = np.arange(P)
    put("ident", np.eye(P))
    put("ones", np.ones((P, P)))
    put("bd", (i[:, None] // 64 == i[None, :] // 64).astype(np.float32))
    rot = np.zeros((P, P))
    rot[i[1::2], i[0::2]] = -1.0
    rot[i[0::2], i[1::2]] = 1.0
    put("rot", rot)
    c, s = rotary(32)
    ck, sk = np.zeros((P, T)), np.zeros((P, T))
    for r in (32, 64):
        ck[r:r + 32], sk[r:r + 32] = c, s
    put("ck", ck)
    put("sk", sk)
    c, s = rotary(64)
    put("cg", np.concatenate([c, c]))
    put("sg", np.concatenate([s, s]))
    put("eps", np.full((P, 1), 1e-6))
    q = 63 - (i % 64)[:, None]
    start = np.clip(q - 8, 0, 48)
    kc = np.arange(64)[None, :]
    put("mask", np.where((kc >= start) & (kc < start + 16), 0.0, -1e30))
    pool = np.zeros((4, T, T))
    for g, w in enumerate((2, 4, 8, 16)):
        for t in range(T):
            lo, hi = max(t - w // 2, 0), min(t - w // 2 + w, T)
            pool[g, lo:hi, t] = 1.0 / (hi - lo)
            pool[g, t, t] -= 1.0
    bp = pool.reshape(4, 2, P, T).transpose(2, 0, 1, 3).reshape(P, 2048).astype(np.float32)
    return con, np.ascontiguousarray(bp)


def feature_major(x):
    return np.ascontiguousarray(np.asarray(x).reshape(T, KT, P).transpose(2, 1, 0))


def kernel(**inputs):
    import concourse.bacc as bacc
    from concourse.bass_utils import run_bass_kernel_spmd

    a = {k: np.asarray(v) for k, v in inputs.items()}
    con, bp = shape_constants()
    rpb = np.zeros((8, 15, 128), np.float32)
    rpb[:, :, 48:79] = a["na_rpb_2"][0]
    mod = a["mod_w_2"].transpose(0, 2, 1).reshape(DEPTH * NMOD, P, D)
    arrays = {
        "stream": weight_blocks(a), "modstream": np.ascontiguousarray(mod),
        "x": feature_major(a["x"][0]), "mem": feature_major(a["mem"][0]), "ctxin": feature_major(a["ctx_2"][0]),
        "crow": np.ascontiguousarray(a["c_2"][0]), "ccrow": np.ascontiguousarray(a["c_ctx_2"]),
        "params": param_columns(a), "consts": con,
        "smallw": np.ascontiguousarray(a["gmlp_w_s"].transpose(0, 3, 1, 2).reshape(DEPTH, P, 512)),
        "smallb": np.ascontiguousarray(a["gmlp_b_s"]), "smallg": np.ascontiguousarray(a["gmlp_v_norm"]),
        "bpool": bp, "rpb": rpb,
    }
    nc = bacc.Bacc("TRN2", target_bir_lowering=False, num_devices=1)
    args = [nc.dram_tensor(k, v.shape, mybir.dt.from_np(v.dtype), kind="ExternalInput").ap() for k, v in arrays.items()]
    res = nc.dram_tensor("result", (P, KT, T), F32, kind="ExternalOutput").ap()
    two_blocks(nc, *args, res)
    r = run_bass_kernel_spmd(nc, [arrays], core_ids=[0])
    return np.ascontiguousarray(r.results[0]["result"].transpose(2, 1, 0)).reshape(1, T, D)
```

```python
from contextlib import ExitStack

import numpy as np

import concourse.bass as bass
from concourse import mybir

F32 = mybir.dt.float32
F32R = mybir.dt.float32r
BF16 = mybir.dt.bfloat16
ALU = mybir.AluOpType
ACT = mybir.ActivationFunctionType
AXX = mybir.AxisListType.X

P, T, D, DEPTH = 128, 256, 1024, 2
KT = D // P
DFF = 2816
NF = DFF // P
NG = NF // 2
TPB = 16
RAW, RING, MODRING = 3, 3, 2
LOOPS = (NG - 1) // 2
PERIT = 6
NMOD = 9 * KT
FFNS = ["f0", "f1", "ctx", "x0a", "x0b", "x1a", "x1b"]
MODS_PER_IT = {"f0": 2, "f1": 2, "ctx": 4, "x0a": 6, "x0b": 6, "x1a": 6}
MODS_FIRST = {"f0": 2, "f1": 2, "x0a": 4, "x0b": 4, "x1a": 2}
MOD_START = {"f0": 0, "f1": 12, "ctx": 24, "x0a": 44, "x0b": 78, "x1a": 112}
MOD_BOTH = ("f0", "f1", "ctx")
NMODC = 44



def stage_sizes():
    out = []
    for l in range(DEPTH):
        out += [(f"in{l}", 88), (f"vv{l}", 16), (f"mk{l}", 32), (f"uq{l}", 12), (f"nope{l}", 3), (f"va{l}", 3),
                (f"pad{l}", 6), (f"mv{l}", 32), (f"out{l}", 64), (f"mq{l}", 32), (f"mo{l}", 32), (f"f{l}", 33 * TPB)]
    out += [("ctx", 33 * TPB), ("x0a", 33 * TPB), ("ck", 32), ("cv", 64 - 32), ("eq", 32), ("ek", 32), ("ev", 32), ("eu", 32),
            ("pool", 4), ("padp", 12), ("eo", 64), ("x0b", 33 * TPB), ("x1a", 33 * TPB),
            ("cin", 192), ("co", 64), ("x1b", 33 * TPB)]
    return out


P0, _p = {}, 0
for _name, _n in stage_sizes():
    P0[_name] = _p
    _p += _n
assert _p % TPB == 0
NBLK = _p // TPB



def output_counts():
    out = []
    for l in range(DEPTH):
        out += [(f"in{l}", 11), (f"vv{l}", 2), (f"gvt{l}", 1), (f"krot{l}", 1), (f"mix{l}", 1), (f"mk{l}", 4), (f"uq{l}", 6),
                (f"nope{l}", 3), (f"va{l}", 2), (f"qrot{l}", 1), (f"mv{l}", 4), (f"att{l}", 12), (f"out{l}", 8),
                (f"mq{l}", 4), (f"matt{l}", 4), (f"mo{l}", 8)]
    out += [("ck", 4), ("cv", 4), ("eq", 4), ("ek", 4), ("ev", 4), ("eu", 4), ("pooled", 4), ("pool", 4), ("natt", 16),
            ("eo", 8), ("cin", 24), ("co", 8)]
    return out


O0, _o = {}, 0
for _name, _n in output_counts():
    O0[_name] = _o
    _o += _n

BLOCK_END, FULL_COUNT = {}, {}
_full = [0] * 4
for _name, _n in output_counts():
    _stage = _name.rstrip("01") if _name[-1] in "01" else _name
    for _j in range(_n):
        _end = None
        if _stage in ("mv", "cv", "ev", "eu"):
            _end = P0[_name] + 16 * (_j // 2 + 1) if _j % 2 else None
        elif _stage in ("in", "out", "mk", "mq", "ck", "eq", "ek", "eo", "cin", "co"):
            _end = P0[_name] + KT * (_j + 1)
        elif _stage == "uq":
            _end = P0[_name] + 2 * (_j + 1)
        elif _stage == "mo":
            _end = P0[_name] + 4 * (_j + 1)
        if _stage == "qrot" or _name == "natt" and (O0[_name] + _j) % 4 < 2:
            continue
        if _end is not None and _end % TPB == 0:
            BLOCK_END[O0[_name] + _j] = _end // TPB
        else:
            _full[(O0[_name] + _j) % 4] += 1
            FULL_COUNT[O0[_name] + _j] = _full[(O0[_name] + _j) % 4]



def natt_output(a):
    return [o for o in range(O0["natt"], O0["natt"] + 16) if o % 4 >= 2][a]


NORMS = []
for _l in range(DEPTH):
    NORMS += [(f"mix{_l}", 8, ((0, 8, D),)), (f"c{_l}", 3, ((0, 1, 128), (1, 3, 256)))]
    if _l == 0:
        NORMS.append(("memory", 8, ((0, 8, D),)))
    NORMS += [(f"mem{_l}", 8, None),
              (f"y{_l}", 8, ((0, 3, 384), (3, 6, 384), (6, 8, 256))),
              (f"memx{_l}", 8, ((0, 8, D),)), (f"my{_l}", 4, None), (f"f{_l}", 8, ((0, 8, D),))]
NORMS += [("ctx", 8, ((0, 8, D),)), ("mid", 8, ((0, 8, D),)), ("x0a", 8, ((0, 8, D),)), ("cn", 8, ((0, 8, D),)), ("xn", 8, ((0, 8, D),)),
          ("ey", 8, None), ("x0b", 8, ((0, 8, D),)), ("x1a", 8, ((0, 8, D),)), ("x1n", 8, ((0, 8, D),)), ("oy", 8, None),
          ("x1b", 8, ((0, 8, D),)), ("final", 8, ((0, 8, D),))]
NSUMS, NTILES, NSQ = {}, {}, {}
IN_PLACE = ("memory", "mid")
_k = _s = _t = 0
for _name, _n, _g in NORMS:
    NSUMS[_name], NTILES[_name], NSQ[_name] = _s, _t, _k
    _k, _s, _t = _k + (_n if _g else 0), _s + (_g is not None), _t + (0 if _name in IN_PLACE else _n)

PCOL, _c = {}, 0
for _name, _n in ([(f"{a}{l}", n) for l in range(DEPTH) for a, n in (
        ("mix", 8), ("c", 3), ("gq", 1), ("gk", 1), ("y", 8), ("mem", 8), ("memx", 8), ("f", 8), ("conv", 4 * 2 * NF))]
        + [(f"ng{i}{j}", 8) for i in range(DEPTH) for j in range(3)]
        + [("ps", 4), ("cw", 24), ("mid", 8), ("final", 8), ("mb0", NMOD), ("mb1", NMOD)]):
    PCOL[_name] = _c
    _c += _n
NPAR = _c

CCOL, _c = {}, 0
for _name, _n in (("ones", 128), ("eps", 1), ("ident", 128), ("bd", 128), ("rot", 128), ("ck", 256), ("sk", 256),
                  ("cg", 256), ("sg", 256), ("mask", 64)):
    CCOL[_name] = _c
    _c += _n
CFIRST = 129
NCON = _c

A_QM, A_KM, A_VM, A_QB, A_VB, A_C, A_KP, A_GV, A_U, A_VV, A_RT = 0, 1536, 3072, 3840, 4864, 5120, 5888, 6144, 6400, 6912, 7424
A_MK, A_MV, A_MQ = A_C, A_GV, 0
A_Q, A_KL, A_KC, A_VL, A_VC, A_UT, A_BP = 0, 1024, 2048, 3072, 4096, 5120, 6144
A_PR1, A_PT1 = A_BP, A_BP + 1024
A_CG, A_CV, A_BG = 0, 512, 1536
A_Z, A_ZC = 0, 256
NAR = 8192




AFTER_FFN = ("mix1", "ctx", "x0a", "cn", "x1a", "x1n", "final")


def SUM_BANK(name, g):
    return (6 if name in AFTER_FFN else 0) + g // 2


EARLY = {"f1": "ctx", "ctx": "x0a", "x0a": "cn"}


def NAPP(name):
    return NSQ[name] - KT * sum(NSQ[name] > NSQ[p] for p in IN_PLACE)


NAV = 5


def EV(l, what):
    return NAV * l + {"c": 1, "gv": 2, "uq": 3, "va": 4, "mq": 5, "eu": 1, "ps": 2}[what]


def YV(what, j=0):
    return 2 * DEPTH + {"pool_lo": j + 1, "natt": 5, "cin": 6 + j}[what]


def GX(ffn):
    return 4 if ffn in ("x0b", "x1a", "x1b") else 0


class Chain:

    def __init__(self, eng, sem):
        self.eng, self.sem, self.n, self.i, self.per = eng, sem, 0, None, 0

    def value(self):
        return self.n if self.i is None else self.n + self.i * self.per

    def link(self, ins):
        self.n += 1
        ins.then_inc(self.sem, 1)
        self.eng.wait_ge(self.sem, self.value())

    def enter(self, i, per):
        self.i, self.per, self.start = i, per, self.n

    def leave(self, trips):
        assert self.n - self.start == self.per, (self.n - self.start, self.per)
        self.n = self.start + self.per * trips
        self.i = None


def two_blocks(nc, stream, modstream, x, mem, ctxin, crow, ccrow, params, consts, smallw, smallb, smallg, bpool, rpb, out):
    es = ExitStack()
    with es:
        def sb(name, shape, dt=F32):
            return es.enter_context(nc.sbuf_tensor(name, shape, dt))

        def sem(name):
            return es.enter_context(nc.semaphore(name))

        wraw = sb("wraw", [P, RAW, 2048])
        whi = sb("whi", [P, RING, 2048], F32R)
        wlo = sb("wlo", [P, RING, 2048], F32R)
        modw = sb("modw", [P, MODRING, D])
        cb = sb("cb", [P, 2, D])
        X = sb("X", [P, KT, T])
        CX = sb("CX", [P, KT, T])
        Hh = sb("Hh", [P, KT, T], F32R)
        Hl = sb("Hl", [P, KT, T], F32R)
        NS = sb("NS", [P, 2, KT, T])
        SQ, TN = NS[:, 0], NS[:, 1]
        Gh = sb("Gh", [P, 4, T], F32R)
        Gl = sb("Gl", [P, 4, T], F32R)
        Y = sb("Y", [P, KT, T])
        PR = sb("PR", [P, 2, 512])
        PT = sb("PT", [P, 4, T])
        STD = PT
        AR = sb("AR", [P, NAR])
        SW = sb("SW", [P, 1024])
        CON = sb("CON", [P, NCON])
        PAR = sb("PAR", [P, NPAR])
        ZB = sb("ZB", [P, 512], BF16)
        GS = sb("GS", [P, 8])
        HG = sb("HG", [P, 8])
        MODL = sb("MODL", [P, DEPTH * NMOD])
        MODC = sb("MODC", [P, NMODC])
        MSC = sb("MSC", [P, 2, 8])
        NM = sb("NM", [P, 4])
        SM = sb("SM", [P, 4])
        RI = sb("RI", [P, 4])
        VS = sb("VS", [P, 6])
        WARM = sb("WARM", [P, 4])

        bank = [es.enter_context(nc.psum_tensor(f"bank{b}", [P, 512], F32)) for b in range(8)]

        raw_loaded = [sem(f"raw_loaded{s}") for s in range(RAW)]
        mod_loaded = [sem(f"mod_loaded{s}") for s in range(MODRING)]
        hi_ready, lo_ready, w_used, mod_used = sem("hi_ready"), sem("lo_ready"), sem("w_used"), sem("mod_used")
        full = [sem(f"psum_full{b}") for b in range(4)]
        free = [sem(f"psum_free{b}") for b in range(4)]
        act_step, dve_step = sem("act_step"), sem("dve_step")
        n_sq, n_sum, n_std, n_app, n_hi, n_lo = (sem(s) for s in (
            "norm_squared", "norm_summed", "norm_deviation", "norm_applied", "norm_hi", "norm_lo"))
        gain_ready, rope_full = sem("gain_ready"), sem("rotated_full")
        up_free, affine, silu_done, gate_out, g_hi, g_lo = (sem(s) for s in (
            "up_read", "conv_centre", "silu_done", "gate_out", "g_hi", "g_lo"))
        res_tile, down_full = sem("residual_tile"), sem("down_bank_full")
        s_full, max_ready, exp_done, prob_ready, pt_full, pt_copied = (sem(s) for s in (
            "scores_full", "max_ready", "exp_done", "prob_ready", "pt_full", "pt_copied"))
        const_in, par_in, x_in, mem_in, ctx_in, c_in, sw_in, bp_in, bias_in, out_done = (sem(s) for s in (
            "const_in", "par_in", "x_in", "mem_in", "ctx_in", "c_in", "sw_in", "bp_in", "bias_in", "out_done"))
        const_rest, par_rest, last_bias_in = sem("const_rest"), sem("par_rest"), sem("last_bias_in")
        c_silu, zeros_ready = sem("c_silu"), sem("zeros_ready")
        evac, qk_std, vv_std, vv_ready, y_half, qk_norm, rope_in = (sem(s) for s in (
            "act_evacuated", "qk_deviation", "vv_deviation", "vv_normed", "dve_evacuated", "qk_normed", "roped"))
        qk_sq, qk_sum, mixed_done, z_copy = (sem(s) for s in ("qk_squared", "qk_summed", "spatial_mixed", "cg_copied"))

        def con(name, n=128):
            return CON[:, CCOL[name]:CCOL[name] + n]

        def par(name, j=0, n=1):
            return PAR[:, PCOL[name] + j:PCOL[name] + j + n]

        def ar(off, n, w=T):
            return AR[:, off:off + n * w].rearrange("p (n w) -> p n w", w=w)

        def bias_table(h):
            if h < 5:
                return CX.rearrange("p k t -> p (k t)")[:, 384 * h:384 * h + 384]
            if h < 7:
                return SW[:, 384 * (h - 5):384 * (h - 5) + 384]
            return NS[:, 0].rearrange("p k t -> p (k t)")[:, 0:384]

        def backwards(v):
            return v.rearrange("p (r c) -> p r c", r=4)[:, :, ::-1]

        def probs(h, wide_):
            if not wide_:
                return PR[:, h % 2, :].rearrange("p (q k) -> p q k", q=2)
            return PR[:, :, :] if h % 2 == 0 else ar(A_PR1, 2, 512)

        def probs_t(h, wide_):
            if not wide_:
                return PT[:, 2 * (h % 2):2 * (h % 2) + 2, :]
            return PT[:, :, :] if h % 2 == 0 else ar(A_PT1, 4)

        def rope_bank(l, j):
            return bank[(2, 3, 0, 1)[j]] if j < 4 else obank(O0[f"qrot{l}"])

        def obank(o):
            return bank[4 + o % 4]

        def wait_full(eng, o):
            if o in BLOCK_END:
                eng.wait_ge(w_used, BLOCK_END[o])
            else:
                eng.wait_ge(full[o % 4], FULL_COUNT[o])

        ident, ones, bdiag, rot = con("ident"), con("ones"), con("bd"), con("rot")
        eps = con("eps", 1)
        OPERAND = {"h": (Hh, Hl), "g": (Gh, Gl)}

        def gain(name, t):
            if name in MODULATED:
                return GS[:, t:t + 1]
            return par(name, t)

        MODULATED = {"ctx": (MODC, 0, 0, "ng00"), "x0a": (MODL, 0, 0, "ng00"), "cn": (MODC, 0, 3, "ng01"),
                     "xn": (MODL, 0, 3, "ng01"), "x0b": (MODL, 0, 6, "ng02"), "x1a": (MODL, NMOD, 0, "ng10"),
                     "x1n": (MODL, NMOD, 3, "ng11"), "x1b": (MODL, NMOD, 6, "ng12")}
        MODORD = {n: i for i, n in enumerate(["ctx", "x0a", "cn", "xn", "x0b", "x1a", "x1n", "x1b"])}

        def shift(name, t):
            m, base, j, _ = MODULATED[name]
            return m[:, base + j * 8 + t:base + j * 8 + t + 1]

        def source(name):
            if name.startswith("c") and name[1:].isdigit():
                return ar(A_C, 3)
            if name.startswith("y") or name.startswith("my") or name in ("ey", "oy"):
                return Y[:, :, :]
            if name in ("memory", "mem0", "mem1", "ctx", "cn"):
                return CX[:, :, :]
            return X[:, :, :]

        def target(name):
            return OPERAND["g"] if name.startswith("c") and name[1:].isdigit() else OPERAND["h"]

        NINFO = {n: (t, g) for n, t, g in NORMS}
        UPDATES = ["memory", "out0", "mo0", "f0", "out1", "mo1", "f1", "mid", "ctx", "x0a", "eo", "x0b", "x1a", "co", "x1b"]
        UPDATED = {"memx0": "out0", "f0": "mo0", "mix1": "f0", "memx1": "out1", "f1": "mo1", "mid": "f1", "x0a": "mid",
                   "cn": "ctx", "xn": "x0a", "x0b": "eo", "x1a": "x0b", "x1n": "x1a", "x1b": "co", "final": "x1b"}
        FI = {n: i for i, n in enumerate(FFNS)}

        block = es.enter_context(nc.Block())

        @block.sync
        def _(sp):
            sp.dma_start(X[:, 0:4, :], x[:, 0:4, :]).then_inc(x_in, 16)
            sp.dma_start(X[:, 4:8, :], x[:, 4:8, :]).then_inc(x_in, 16)
            sp.dma_start(CON[:, 0:CFIRST], consts[:, 0:CFIRST]).then_inc(const_in, 16)
            sp.dma_start(PAR[:, 0:KT], params[:, 0:KT]).then_inc(par_in, 16)
            loaded = 0

            def load(n, i=None, step=0):
                if n >= RAW or i is not None:
                    sp.wait_ge(lo_ready, n - RAW + 1 if i is None else i * PERIT + (n - RAW + 1))
                src = stream[n] if i is None else stream[bass.ds(i * PERIT + n, 1)].rearrange("o p f -> (o p) f")
                sp.dma_start(wraw[:, n % RAW, :], src).then_inc(raw_loaded[n % RAW], 16)

            def load_mod(u, i=None, per=0):
                sp.wait_ge(mod_used, u + 1 if i is None else i * per + (u + 1))
                src = modstream[u] if i is None else modstream[bass.ds(i * per + u, 1)].rearrange("o p f -> (o p) f")
                sp.dma_start(modw[:, u % MODRING, :], src).then_inc(mod_loaded[u % MODRING], 16)

            for f in FFNS:
                b0 = P0[f] // TPB
                for n in range(loaded, b0 + 4):
                    load(n)
                per, first = MODS_PER_IT.get(f, 0), MODS_FIRST.get(f, 0)
                for k in range(first):
                    load_mod(MOD_START[f] + k)
                with sp.Fori(0, LOOPS) as i:
                    for c in range(2):
                        for k in range(3):
                            load(b0 + 4 + 3 * c + k, i)
                            if k < per // 2:
                                load_mod(MOD_START[f] + first + per // 2 * c + k, i, per)
                loaded = b0 + 34
            sp.wait_ge(n_app, NAPP("final") + KT)
            sp.dma_start(out, SQ).then_inc(out_done, 16)
            sp.wait_ge(out_done, 16)

        @block.gpsimd
        def _(pool):
            def load_bias(heads, signal):
                for h in heads:
                    for r in range(2):
                        src = bass.AP(tensor=rpb.tensor, offset=h * 15 * 128 + (5 - r) * 128,
                                      ap=[[1, 64], [128, 6], [1, 64]])
                        pool.dma_start(bias_table(h)[64 * r:64 * r + 64].rearrange("p (m k) -> p m k", m=6),
                                       src).then_inc(signal, 16)

            pool.wait_ge(hi_ready, 1)
            pool.dma_start(CON[:, CFIRST:], consts[:, CFIRST:]).then_inc(const_rest, 16)
            pool.dma_start(PAR[:, KT:], params[:, KT:]).then_inc(par_rest, 16)
            pool.dma_start(CX[:, :, :], mem).then_inc(mem_in, 16)
            pool.dma_start(cb[:, 0, :], crow.partition_broadcast(P)).then_inc(c_in, 16)
            pool.dma_start(cb[:, 1, :], ccrow.partition_broadcast(P)).then_inc(c_in, 16)
            for l in range(DEPTH):
                if l:
                    pool.wait_ge(mixed_done, l)
                pool.dma_start(SW[:, 0:512], smallw[l]).then_inc(sw_in, 16)
                pool.dma_start(SW[:, 512:768], smallg[l].partition_broadcast(P)).then_inc(sw_in, 16)
                for g in range(4):
                    r = 64 * (g % 2)
                    pool.dma_start(SW[r:r + 64, 768 + 128 * (g // 2):896 + 128 * (g // 2)],
                                   smallb[l, g].partition_broadcast(64)).then_inc(sw_in, 16)
            pool.wait_ge(n_hi, NTILES["mem1"] + 8)
            pool.wait_ge(n_lo, NTILES["mem1"] + 8)
            pool.dma_start(CX[:, :, :], ctxin).then_inc(ctx_in, 16)
            pool.wait_ge(mixed_done, DEPTH)
            load_bias((5, 6), bias_in)
            pool.wait_ge(n_lo, NTILES["f1"] + 8)
            pool.dma_start(AR[:, A_BP:A_BP + 2048], bpool).then_inc(bp_in, 16)
            pool.wait_ge(n_lo, NTILES["cn"] + 8)
            load_bias(range(5), bias_in)
            pool.wait_ge(n_lo, NTILES["xn"] + 8)
            pool.wait_ge(n_hi, NTILES["xn"] + 8)
            load_bias((7,), last_bias_in)

        @block.tensor
        def _(pe):
            state = {"block": -1}

            def open_block(n, i=None):
                pe.wait_ge(lo_ready, n + 1 if i is None else i * PERIT + (n + 1))

            def tile_at(p, w=1):
                c = (p % TPB) * P
                return whi[:, (p // TPB) % RING, c:c + w * P], wlo[:, (p // TPB) % RING, c:c + w * P]

            def need(p):
                if p // TPB != state["block"]:
                    assert p // TPB == state["block"] + 1
                    state["block"] = p // TPB
                    open_block(p // TPB)

            def three(outp, whl, ahl, start, stop, flip=False, skip=False):
                last = None
                for j, (a, b) in enumerate(((0, 0), (0, 1), (1, 0))):
                    st, en = start and j == 0, stop and j == 2
                    lhs, rhs = (ahl[b], whl[a]) if flip else (whl[a], ahl[b])
                    last = pe.matmul(outp, lhs, rhs, start=st, stop=en, skip_group_check=skip)
                return last

            def claim(o):
                if o // 4 > 0:
                    pe.wait_ge(free[o % 4], o // 4)

            def wait_h(name, k):
                pe.wait_ge(n_lo, NTILES[name] + k + 1)

            def feature(stage, name, outs, kt, src="h", k0=0, first=0, p=None, o=None):
                hh, hl = OPERAND[src]
                p = P0[stage] if p is None else p
                o = O0[stage] if o is None else o
                for m in range(outs):
                    claim(o)
                    for k in range(kt):
                        need(p)
                        if m == 0 and name:
                            wait_h(name, k0 + k)
                        last = three(obank(o)[:, 0:T], tile_at(p), (hh[:, k0 + k, :], hl[:, k0 + k, :]), k == 0, k == kt - 1)
                        p += 1
                        if p % TPB == 0 and k < kt - 1:
                            last.then_inc(w_used, 1)
                    last.then_inc(w_used if p % TPB == 0 else full[o % 4], 1)
                    o += 1

            def tokens(stage, name, kt, w, src="h", k0=0, p=None, o=None):
                hh, hl = OPERAND[src]
                p = P0[stage] if p is None else p
                o = O0[stage] if o is None else o
                for tt in range(2):
                    claim(o + tt)
                for k in range(kt):
                    need(p)
                    if name:
                        wait_h(name, k0 + k)
                    for tt in range(2):
                        s = slice(tt * P, tt * P + P)
                        last = three(obank(o + tt)[:, 0:w * P], tile_at(p, w),
                                     (hh[:, k0 + k, s], hl[:, k0 + k, s]), k == 0, k == kt - 1, flip=True)
                        if k == kt - 1 and tt == 0:
                            last.then_inc(full[(o + tt) % 4], 1)
                    p += w
                    if p % TPB == 0 and k < kt - 1:
                        last.then_inc(w_used, 1)
                last.then_inc(w_used if p % TPB == 0 else full[(o + 1) % 4], 1)

            def norm_sum(name):
                n, groups = NINFO[name]
                for g, (a, b, _) in enumerate(groups):
                    for t in range(a, b):
                        pe.wait_ge(n_sq, NSQ[name] + t + 1)
                        last = pe.matmul(bank[SUM_BANK(name, g)][:, T * (g % 2):T * (g % 2) + T], ones, SQ[:, t, :],
                                         start=(t == a), stop=(t == b - 1))
                last.then_inc(n_sum, 1)

            def skip_pad():
                last = pe.matmul(bank[0][:, 0:P], ZB[:, 0:P], ZB[:, 0:P], start=True, stop=True)
                last.then_inc(w_used, 1)

            def attention(h0, n, o0, keys, single, q_of, k_of, v_of, place):
                nk = keys // P

                def scores(a):
                    h = h0 + a
                    if h >= 2:
                        pe.wait_ge(exp_done, h - 1)
                    if single and a == 1:
                        for o in range(O0["natt"], O0["natt"] + 4):
                            if o % 4 < 2:
                                claim(o)
                    for qt in range(2):
                        for kk in range(keys // T):
                            b = bank[4 * (h % 2) + qt][:, kk * T:kk * T + T] if single else bank[h % 2][:, qt * T:qt * T + T]
                            last = pe.matmul(b, q_of(a)[:, qt * P:qt * P + P], k_of(a, kk), start=True, stop=True)
                    last.then_inc(s_full, 1)

                def transposes(a):
                    h = h0 + a
                    pe.wait_ge(prob_ready, h + 1)
                    wait = h if single else h - 1
                    if wait > 0:
                        pe.wait_ge(pt_copied, wait)
                    for qt in range(2):
                        for k in range(nk):
                            b = bank[2 + k // 2][:, (k % 2) * T + qt * P:(k % 2) * T + qt * P + P] if single else \
                                bank[2 + h % 2][:, k * T + qt * P:k * T + qt * P + P]
                            src = probs(h, single)[:, qt, k * P:k * P + P]
                            last = pe.transpose(b, src, ident)
                    last.then_inc(pt_full, 1)

                def values(a):
                    h, o = h0 + a, natt_output(a) if single else o0 + a
                    pe.wait_ge(pt_copied, h + 1)
                    claim(o)
                    r0, r1 = place(a)
                    for k in range(nk):
                        last = pe.matmul(obank(o)[r0:r1, 0:T], v_of(a, k), probs_t(h, single)[:, k, :], start=(k == 0), stop=(k == nk - 1))
                    last.then_inc(full[o % 4], 1)

                for a in range(n + 3):
                    if a < n:
                        scores(a)
                    if 2 <= a <= n + 1:
                        transposes(a - 2)
                    if a >= 3:
                        values(a - 3)

            def ffn(name):
                f, b0 = FI[name], P0[name] // TPB
                def up(g2, n, i, gval):
                    pe.wait_ge(up_free, gval)
                    for half in range(2):
                        open_block(n + half, i)
                        for ft in range(2):
                            for k in range(KT):
                                if i is None and half == 0 and ft == 0:
                                    wait_h(name, k)
                                last = three(bank[4 + 2 * g2 + half][:, ft * T:ft * T + T],
                                             tile_at((n + half) * TPB + ft * KT + k), (Hh[:, k, :], Hl[:, k, :]),
                                             k == 0, k == KT - 1)
                        last.then_inc(w_used, 1)

                def down(g2, n, i, gval, final=False):
                    open_block(n, i)
                    pe.wait_ge(g_lo, gval)
                    order = [(ft, m) for m in range(KT) for ft in range(2)] if final else \
                        [(ft, m) for ft in range(2) for m in range(KT)]
                    for ft, m in order:
                        last = three(bank[m // 2][:, T * (m % 2):T * (m % 2) + T], tile_at(n * TPB + ft * KT + m),
                                     (Gh[:, 2 * g2 + ft, :], Gl[:, 2 * g2 + ft, :]), False, final and ft == 1, skip=True)
                        if final and ft == 1 and m % 2 and m < KT - 1:
                            last.then_inc(down_full, 1)
                    last.then_inc(w_used, 1)

                up(0, b0, None, NG * f + 1)
                if name == "ctx":
                    pe.wait_ge(res_tile, KT * (UPDATES.index("f1") + 1))
                    norm_sum("mid")
                    pe.wait_ge(n_std, NSUMS["mid"] + 1)
                if name == "x0a":
                    pe.wait_ge(res_tile, KT * (UPDATES.index("ctx") + 1))
                for b in range(4):
                    pe.matmul(bank[b][:, :], ZB[:, 0:P], ZB[:, :], start=True, stop=False, skip_group_check=True)
                with pe.Fori(0, LOOPS) as i:
                    for c in range(2):
                        n = b0 + 2 + 3 * c
                        up((1 + c) % 2, n, i, i * 2 + (NG * f + c + 1))
                        down(c % 2, n + 2, i, i * 2 + (NG * f + c + 1))
                if name in EARLY:
                    norm_sum(EARLY[name])
                down(0, b0 + 32, None, NG * f + NG, final=True)
                state["block"] = b0 + 32

            pe.wait_ge(const_in, 16)
            pe.wait_ge(zeros_ready, 1)
            for l in range(DEPTH):
                QM, KM, VM = ar(A_QM, 6), ar(A_KM, 6), ar(A_VM, 2, 384)
                QB, VB, GV, VV, KP = ar(A_QB, 4), ar(A_VB, 2, 128), ar(A_GV, 1), ar(A_VV, 2), ar(A_KP, 1)
                norm_sum(f"mix{l}")
                feature(f"in{l}", f"mix{l}", 7, KT)
                norm_sum(f"c{l}")
                feature(f"in{l}", None, 4, KT, p=P0[f"in{l}"] + 56, o=O0[f"in{l}"] + 7)
                if l == 0:
                    norm_sum("memory")
                tokens(f"vv{l}", None, KT, 2)
                if l == 0:
                    pe.wait_ge(const_rest, 16)
                o = O0[f"gvt{l}"]
                claim(o)
                pe.wait_ge(evac, EV(l, "gv"))
                for tt in range(2):
                    last = pe.transpose(obank(o)[:, tt * P:tt * P + P], GV[:, 0, tt * P:tt * P + P], ident)
                last.then_inc(full[o % 4], 1)
                o = O0[f"krot{l}"]
                claim(o)
                pe.matmul(obank(o)[:, 0:T], rot, KP[:, 0, :], start=True, stop=True).then_inc(full[o % 4], 1)
                pe.wait_ge(qk_sq, l + 1)
                for j in range(2):
                    last = pe.matmul(bank[2 + j][:, :], bdiag,
                                     SQ[:, 4 + 2 * j:6 + 2 * j, :].rearrange("p a t -> p (a t)"), start=True, stop=True)
                last.then_inc(qk_sum, 1)
                o = O0[f"mix{l}"]
                claim(o)
                pe.wait_ge(vv_ready, l + 1)
                pe.wait_ge(sw_in, 96 * (l + 1))
                for n in range(2):
                    for g in range(4):
                        last = pe.matmul(obank(o)[64 * (g % 2):64 * (g % 2) + 64, (g // 2) * T + n * P:(g // 2) * T + n * P + P],
                                         VV[:, n, g * 64:g * 64 + 64], SW[:, g * P:g * P + P], start=True, stop=True)
                last.then_inc(full[o % 4], 1)
                feature(f"mk{l}", f"mem{l}", 4, KT)
                feature(f"uq{l}", f"c{l}", 6, 2, src="g", k0=1)
                feature(f"nope{l}", f"c{l}", 3, 1, src="g", k0=0)
                tokens(f"va{l}", None, 1, 3, src="g", k0=0)
                skip_pad()
                pe.wait_ge(qk_norm, l + 1)
                for j in range(2):
                    pe.matmul(rope_bank(l, j)[:, :], rot, QB[:, 2 * j:2 * j + 2, :].rearrange("p a t -> p (a t)"),
                              start=True, stop=True).then_inc(rope_full, 1)
                pe.wait_ge(evac, EV(l, "uq"))
                for j in range(3):
                    if j == 2:
                        claim(O0[f"qrot{l}"])
                    pe.matmul(rope_bank(l, 2 + j)[:, :], rot, QM[:, 2 * j:2 * j + 2, :].rearrange("p a t -> p (a t)"),
                              start=True, stop=True).then_inc(rope_full, 1)
                tokens(f"mv{l}", None, KT, 2)
                tokens(f"mv{l}", None, KT, 2, p=P0[f"mv{l}"] + 16, o=O0[f"mv{l}"] + 2)
                pe.wait_ge(rope_in, l + 1)
                pe.wait_ge(evac, EV(l, "va"))

                def qh(a):
                    if a < 6:
                        return QM[:, a, :]
                    b = a - 6
                    return QB[64 * (b // 3):64 * (b // 3) + 64, b % 3, :]

                def kh(a, kk):
                    if a < 6:
                        return KM[:, a, :]
                    b = a - 6
                    return QB[64 * (b // 3):64 * (b // 3) + 64, 3, :]

                def vh(a, k):
                    if a < 6:
                        return VM[:, k, 64 * a:64 * a + 64]
                    b = a - 6
                    return VB[:, k, 64 * (b // 3):64 * (b // 3) + 64]

                def row(a):
                    r = 64 * (a % 2) if a < 6 else 64 * ((a - 6) // 3)
                    return r, r + 64

                attention(16 * l, 12, O0[f"att{l}"], T, False, qh, kh, vh, row)
                norm_sum(f"y{l}")
                feature(f"out{l}", f"y{l}", 8, KT)
                norm_sum(f"memx{l}")
                feature(f"mq{l}", f"memx{l}", 4, KT)
                pe.wait_ge(evac, EV(l, "mq"))
                MK, MV, MQ = ar(A_MK, 4), ar(A_MV, 2, 512), ar(A_MQ, 4)
                attention(16 * l + 12, 4, O0[f"matt{l}"], T, False, lambda a: MQ[:, a, :], lambda a, kk: MK[:, a, :],
                          lambda a, k: MV[:, k, P * a:P * a + P], lambda a: (0, P))
                feature(f"mo{l}", f"my{l}", 8, 4)
                norm_sum(f"f{l}")
                ffn(f"f{l}")
            ffn("ctx")
            ffn("x0a")
            feature("ck", "cn", 4, KT)
            tokens("cv", None, KT, 2)
            tokens("cv", None, KT, 2, p=P0["cv"] + 16, o=O0["cv"] + 2)
            norm_sum("xn")
            feature("eq", "xn", 4, KT)
            feature("ek", None, 4, KT)
            for s in ("ev", "eu"):
                tokens(s, None, KT, 2)
                tokens(s, None, KT, 2, p=P0[s] + 16, o=O0[s] + 2)
            pe.wait_ge(evac, EV(2, "eu"))
            pe.wait_ge(bp_in, 16)
            UT, BP = ar(A_UT, 2, 512), AR[:, A_BP:A_BP + 2048].rearrange("p (g s t) -> p g s t", g=4, s=2)
            for g in range(4):
                o = O0["pooled"] + g
                claim(o)
                for s in range(2):
                    last = pe.matmul(obank(o)[:, 0:T], UT[:, s, g * P:g * P + P], BP[:, g, s, :], start=(s == 0), stop=(s == 1))
                last.then_inc(full[o % 4], 1)
            p = P0["pool"]
            for g in range(4):
                o = O0["pool"] + g
                claim(o)
                need(p)
                pe.wait_ge(y_half, YV("pool_lo", g))
                three(obank(o)[:, 0:T], tile_at(p), (Gh[:, g, :], Gl[:, g, :]), True, True).then_inc(full[o % 4], 1)
                p += 1
            skip_pad()
            Q, KL, KC = ar(A_Q, 4), ar(A_KL, 4), ar(A_KC, 4)
            VL, VC = ar(A_VL, 2, 512), ar(A_VC, 2, 512)

            def half(a):
                return slice(64 * (a % 2), 64 * (a % 2) + 64)

            attention(32, 8, O0["natt"], 512, True, lambda a: Q[half(a), a // 2, :],
                      lambda a, kk: (KL if kk == 0 else KC)[half(a), a // 2, :],
                      lambda a, k: (VL if k < 2 else VC)[:, k % 2, 64 * a:64 * a + 64],
                      lambda a: (64 * (a % 2), 64 * (a % 2) + 64))
            feature("eo", "ey", 8, KT)
            norm_sum("x0b")
            ffn("x0b")
            norm_sum("x1a")
            ffn("x1a")
            norm_sum("x1n")
            feature("cin", "x1n", 24, KT)
            feature("co", "oy", 8, KT)
            norm_sum("x1b")
            ffn("x1b")
            norm_sum("final")

        @block.scalar
        def _(act):
            chain = Chain(act, act_step)
            st = {"hi": 0, "ev": 0, "table": 0}

            def split_hi(n, i=None):
                slot = n % RAW
                loads = 16 * (n // RAW + 1)
                act.wait_ge(raw_loaded[slot], loads if i is None else i * (16 * PERIT // RAW) + loads)
                if n >= RING:
                    act.wait_ge(w_used, n - RING + 1 if i is None else i * PERIT + (n - RING + 1))
                act.activation(whi[:, n % RING, :], wraw[:, slot, :], ACT.Copy).then_inc(hi_ready, 1)

            def hi_upto(n):
                while st["hi"] <= min(n, NBLK):
                    split_hi(st["hi"])
                    st["hi"] += 1

            def table(func):
                st["table"] = (st["table"] + 1) % 4
                act.activation(WARM[:, st["table"]:st["table"] + 1], eps, func)

            def source_ready(name):
                marks = {"ey": YV("natt"), "oy": YV("cin", KT - 1)}
                for l in range(DEPTH):
                    marks.update({f"y{l}": 2 * l + 1, f"my{l}": 2 * l + 2})
                if name in marks:
                    act.wait_ge(y_half, marks[name])

            def norm(name):
                n, groups = NINFO[name]
                if groups:
                    norm_square(name)
                    norm_rest(name)
                else:
                    plain_hi(name)

            def norm_square(name, tiles=range(KT)):
                n, groups = NINFO[name]
                src = source(name)
                source_ready(name)
                if NSUMS[name]:
                    act.wait_ge(n_sum, NSUMS[name])
                if name not in AFTER_FFN and 0 in tiles:
                    table(ACT.Sqrt)
                for t in tiles[:n]:
                    if name == "mix0" and t % 4 == 0:
                        act.wait_ge(x_in, 4 * t + 16)
                    if name in UPDATED:
                        act.wait_ge(res_tile, KT * UPDATES.index(UPDATED[name]) + t + 1)
                    act.activation(SQ[:, t, :], src[:, t, :], ACT.Square).then_inc(n_sq, 1)

            def norm_rest(name):
                n, groups = NINFO[name]
                hh, _ = target(name)
                k = NSUMS[name]
                act.wait_ge(n_sum, k + 1)
                for g, (a, b, width) in enumerate(groups):
                    last = act.activation(STD[:, g, :], bank[SUM_BANK(name, g)][:, T * (g % 2):T * (g % 2) + T], ACT.Sqrt,
                                          bias=eps, scale=1.0 / width)
                last.then_inc(n_std, 1)
                if name in ("memory", "mid", "final"):
                    return
                if name == "mix0":
                    hi_upto(0)
                if name in MODULATED:
                    act.wait_ge(gain_ready, MODORD[name] + 1)
                for t in range(n):
                    act.wait_ge(n_app, NAPP(name) + t + 1)
                    if name in MODULATED:
                        act.activation(hh[:, t, :], TN[:, t, :], ACT.Identity, bias=shift(name, t)).then_inc(n_hi, 1)
                    else:
                        act.activation(hh[:, t, :], TN[:, t, :], ACT.Copy).then_inc(n_hi, 1)

            def plain_hi(name):
                n, _ = NINFO[name]
                hh, _ = target(name)
                source_ready(name)
                for t in range(n):
                    act.activation(hh[:, t, :], Y[:, t, :], ACT.Copy).then_inc(n_hi, 1)

            def memory_hi(l):
                act.wait_ge(res_tile, KT)
                for t in range(KT):
                    act.activation(Hh[:, t, :], CX[:, t, :], ACT.Copy, scale=par(f"mem{l}", t)).then_inc(n_hi, 1)

            def evacuate(dst, src, o, block_, func=ACT.Copy, scale=1.0, **kw):
                if block_ is not None:
                    hi_upto(block_ + 2)
                wait_full(act, o)
                act.activation(dst, src, func, scale=scale, **kw).then_inc(free[o % 4], 1)

            def mark():
                st["ev"] += 1
                act.copy(VS[:, 5:6], eps).then_inc(evac, 1)
                act.wait_ge(evac, st["ev"])

            def blk(stage, tiles):
                return (P0[stage] + tiles - 1) // TPB

            def attend(h0, n, o0, keys, single):
                table(ACT.Exp)
                for a in range(n + 2):
                    if a < n:
                        h = h0 + a
                        act.wait_ge(max_ready, h + 1)
                        if h >= 2:
                            act.wait_ge(pt_full, h - 1)
                        for qt in range(2):
                            src = bank[4 * (h % 2) + qt][:, :] if single else bank[h % 2][:, qt * T:qt * T + T]
                            c = 2 * (h % 2) + qt
                            last = act.activation(probs(h, single)[:, qt, :], src, ACT.Exp, bias=NM[:, c:c + 1], scale=1.0,
                                                  accum_out=SM[:, c:c + 1])
                        last.then_inc(exp_done, 1)
                    if a >= 2:
                        h, o = h0 + a - 2, o0 + a - 2
                        if a >= 4:
                            wait_full(act, natt_output(a - 4) if single else o - 2)
                        act.wait_ge(pt_full, h + 1)
                        for j in range(keys // T):
                            last = act.activation(probs_t(h, single)[:, 2 * j:2 * j + 2, :],
                                                  bank[2 + (j if single else h % 2)][:, :].rearrange("p (a t) -> p a t", a=2),
                                                  ACT.Copy)
                        last.then_inc(pt_copied, 1)

            def ffn(name):
                f, b0 = FI[name], P0[name] // TPB
                conv = name in ("f0", "f1")
                if name != "ctx":
                    table(ACT.Silu)
                hi_upto(b0 + 3)

                def group(g2, cnt, i, gs, n):
                    def at(m):
                        return cnt + m if i is None else i * 2 + (cnt + m)
                    act.wait_ge(w_used, n + 2 if i is None else i * PERIT + (n + 2))
                    gb, vb = bank[4 + 2 * g2], bank[5 + 2 * g2]
                    if conv:
                        if f or gs:
                            act.wait_ge(g_lo, at(0))
                        for part, (b, buf) in enumerate(((gb, A_CG), (vb, A_CV))):
                            for ft in range(2):
                                col = PCOL[f"conv{f}"] + 4 * (NF * part + ft) + 8 * gs
                                if i is None:
                                    w, bb = PAR[:, col + 1:col + 2], PAR[:, col + 3:col + 4]
                                else:
                                    w, bb = PAR[:, bass.ds(i * 16 + (col + 1), 1)], PAR[:, bass.ds(i * 16 + (col + 3), 1)]
                                last = act.activation(AR[:, buf + ft * T:buf + ft * T + T], b[:, ft * T:ft * T + T],
                                                      ACT.Identity, bias=bb, scale=w)
                        last.then_inc(affine, 1)
                    else:
                        act.wait_ge(up_free, at(1))
                        act.activation(AR[:, A_CG:A_CG + 512], gb[:, :], ACT.Silu).then_inc(silu_done, 1)

                def group_end(g2, cnt, i):
                    def at(m):
                        return cnt + m if i is None else i * 2 + (cnt + m)
                    if conv:
                        act.wait_ge(up_free, at(2))
                        act.activation(AR[:, A_CG:A_CG + 512], AR[:, A_CG:A_CG + 512], ACT.Silu).then_inc(silu_done, 1)
                        act.wait_ge(gate_out, at(1))
                    else:
                        act.wait_ge(up_free, at(2))
                    act.activation(Gh[:, 2 * g2:2 * g2 + 2, :].rearrange("p a t -> p (a t)"), AR[:, A_CV:A_CV + 512],
                                   ACT.Copy).then_inc(g_hi, 1)

                if name == "ctx":
                    norm("mid")
                    table(ACT.Silu)
                group(0, NG * f, None, 0, b0)
                group_end(0, NG * f, None)
                if name in EARLY:
                    if name == "f1":
                        act.wait_ge(ctx_in, 16)
                    norm_square(EARLY[name])
                assert st["hi"] == b0 + 4
                with act.Fori(0, LOOPS) as i:
                    for c in range(2):
                        n0 = b0 + 2 + 3 * c
                        split_hi(n0 + 2, i)
                        split_hi(n0 + 3, i)
                        group((1 + c) % 2, NG * f + 1 + c, i, 1 + c, n0)
                        split_hi(n0 + 4, i)
                        group_end((1 + c) % 2, NG * f + 1 + c, i)
                st["hi"] = b0 + 34
                table(ACT.Sqrt)
                if name in EARLY:
                    norm_rest(EARLY[name])
                hi_upto(b0 + 34)

            act.wait_ge(const_in, 16)
            for l in range(DEPTH):
                QM, KM, VM, QB, VB = ar(A_QM, 6), ar(A_KM, 6), ar(A_VM, 2, 384), ar(A_QB, 4), ar(A_VB, 2, 128)
                C, KP, GV, U, VV = ar(A_C, 3), ar(A_KP, 1), ar(A_GV, 1), ar(A_U, 2), ar(A_VV, 2)
                norm(f"mix{l}")
                hi_upto(P0[f"in{l}"] // TPB + 2)
                if l == 0:
                    act.wait_ge(const_rest, 16)
                    act.wait_ge(par_rest, 16)
                o, s = O0[f"in{l}"], f"in{l}"
                for m in range(3):
                    evacuate(C[:, m, :], obank(o + m)[:, 0:T], o + m, blk(s, 8 * m + 8))
                evacuate(KP[:, 0, :], obank(o + 3)[:, 0:T], o + 3, blk(s, 32))
                mark()
                norm_square(f"c{l}")
                for m in range(3):
                    evacuate(QB[:, m, :], obank(o + 4 + m)[:, 0:T], o + 4 + m, blk(s, 8 * m + 40))
                norm_rest(f"c{l}")
                if l == 0:
                    act.wait_ge(mem_in, 16)
                    norm_square("memory")
                evacuate(QB[:, 3, :], obank(o + 7)[:, 0:T], o + 7, blk(s, 64))
                evacuate(GV[:, 0, :], obank(o + 8)[:, 0:T], o + 8, blk(s, 72))
                for m in range(2):
                    evacuate(U[:, m, :], obank(o + 9 + m)[:, 0:T], o + 9 + m, blk(s, 80 + 8 * m), ACT.Gelu_apprx_tanh)
                if l == 0:
                    norm_rest("memory")
                    table(ACT.Gelu_apprx_tanh)
                for tt in range(2):
                    o = O0[f"vv{l}"] + tt
                    evacuate(VV[:, tt, :], obank(o)[:, 0:T], o, blk(f"vv{l}", 16), ACT.Gelu_apprx_tanh)
                mark()
                for tt in range(2):
                    act.activation(TN[:, 6 + tt, :], VV[:, tt, :], ACT.Square, accum_out=VS[:, tt:tt + 1])
                act.activation(SQ[:, 4:8, :], QB[:, 0:4, :], ACT.Square).then_inc(qk_sq, 1)
                act.wait_ge(qk_sq, l + 1)
                act.activation(VS[:, 2:4], VS[:, 0:2], ACT.Sqrt, bias=eps, scale=1.0 / 256).then_inc(vv_std, 1)
                memory_hi(l)
                act.wait_ge(qk_sum, l + 1)
                act.wait_ge(n_lo, NTILES[f"c{l}"] + 3)
                for j in range(2):
                    last = act.activation(STD[:, 2 * j:2 * j + 2, :].rearrange("p a t -> p (a t)"), bank[2 + j][:, :],
                                          ACT.Sqrt, bias=eps, scale=1.0 / 64)
                last.then_inc(qk_std, 1)
                o = O0[f"gvt{l}"]
                evacuate(VB[:, :, :].rearrange("p a t -> p (a t)"), obank(o)[:, 0:T], o, None)
                MK, MV, MQ = ar(A_MK, 4), ar(A_MV, 2, 512), ar(A_MQ, 4)
                for m in range(4):
                    o = O0[f"mk{l}"] + m
                    evacuate(MK[:, m, :], obank(o)[:, 0:T], o, blk(f"mk{l}", 8 * m + 8))
                for m in range(6):
                    o = O0[f"uq{l}"] + m
                    evacuate(QM[:, m, :], obank(o)[:, 0:T], o, blk(f"uq{l}", 2 * m + 2), scale=96.0 ** -0.5)
                mark()
                for m in range(3):
                    o = O0[f"nope{l}"] + m
                    hi_upto(blk(f"nope{l}", m + 1) + 2)
                    wait_full(act, o)
                    act.activation(KM[0:64, 2 * m, :], obank(o)[0:64, 0:T], ACT.Copy)
                    act.activation(KM[64:128, 2 * m + 1, :], obank(o)[64:128, 0:T], ACT.Copy).then_inc(free[o % 4], 1)
                for tt in range(2):
                    o = O0[f"va{l}"] + tt
                    evacuate(VM[:, tt, :], obank(o)[:, 0:384], o, blk(f"va{l}", 3))
                mark()
                hi_upto(blk(f"pad{l}", 6) + 2)
                act.wait_ge(mixed_done, l + 1)
                for j in range(4):
                    o = O0[f"mv{l}"] + j
                    evacuate(MV[:, j % 2, T * (j // 2):T * (j // 2) + T], obank(o)[:, 0:T], o, blk(f"mv{l}", 16 * (j // 2) + 16))
                attend(16 * l, 12, O0[f"att{l}"], T, False)
                norm(f"y{l}")
                for m in range(8):
                    hi_upto(blk(f"out{l}", 8 * m + 8) + 2)
                    if m:
                        norm_square(f"memx{l}", range(m - 1, m))
                norm_square(f"memx{l}", range(KT - 1, KT))
                norm_rest(f"memx{l}")
                for m in range(4):
                    o = O0[f"mq{l}"] + m
                    evacuate(MQ[:, m, :], obank(o)[:, 0:T], o, blk(f"mq{l}", 8 * m + 8), scale=128.0 ** -0.5)
                mark()
                attend(16 * l + 12, 4, O0[f"matt{l}"], T, False)
                norm(f"my{l}")
                if l == 0:
                    act.wait_ge(c_in, 32)
                    act.activation(cb[:, :, :], cb[:, :, :], ACT.Silu).then_inc(c_silu, 1)
                hi_upto(blk(f"mo{l}", 16) + 2)
                hi_upto(blk(f"mo{l}", 32) + 2)
                norm(f"f{l}")
                ffn(f"f{l}")
            ffn("ctx")
            ffn("x0a")
            Q, KL, KC, VL, VC, UT = ar(A_Q, 4), ar(A_KL, 4), ar(A_KC, 4), ar(A_VL, 2, 512), ar(A_VC, 2, 512), ar(A_UT, 2, 512)

            def feat(stage, buf, scale=1.0, order=lambda v: v):
                for m in range(4):
                    o = O0[stage] + m
                    src = obank(o)[:, 0:T] if order is not backwards else obank(o)[:, 0:T].rearrange("p (r c) -> p r c", r=4)
                    evacuate(order(buf[:, m, :]), src, o, blk(stage, 8 * m + 8), scale=scale)

            def tok(stage, buf):
                for j in range(4):
                    o = O0[stage] + j
                    evacuate(buf[:, j % 2, T * (j // 2):T * (j // 2) + T], obank(o)[:, 0:T], o, blk(stage, 16 * (j // 2) + 16))

            feat("ck", KC)
            tok("cv", VC)
            norm("xn")
            feat("eq", Q, 0.125, backwards)
            feat("ek", KL)
            tok("ev", VL)
            tok("eu", UT)
            mark()
            for g in range(4):
                o = O0["pooled"] + g
                wait_full(act, o)
                act.activation(Gh[:, g, :], obank(o)[:, 0:T], ACT.Copy).then_inc(g_hi, 1)
                hi_upto(blk("pool", 4) + 2)
            for g in range(4):
                o = O0["pool"] + g
                wait_full(act, o)
                act.activation(Y[:, 4 + g, :], obank(o)[:, 0:T], ACT.Copy, scale=par("ps", g)).then_inc(free[o % 4], 1)
            mark()
            attend(32, 8, O0["natt"], 512, True)
            norm("ey")
            for m in range(8):
                hi_upto(blk("eo", 8 * m + 8) + 2)
            norm("x0b")
            ffn("x0b")
            norm("x1a")
            ffn("x1a")
            norm("x1n")
            for t in range(KT):
                o = O0["cin"] + 3 * t + 1
                if t >= 2:
                    act.wait_ge(y_half, YV("cin", t - 2))
                hi_upto(blk("cin", 24 * t + 8) + 2)
                wait_full(act, o - 1)
                act.activation(AR[:, A_BG + T * (t % 2):A_BG + T * (t % 2) + T], obank(o - 1)[:, 0:T],
                               ACT.Copy).then_inc(free[(o - 1) % 4], 1)
                hi_upto(blk("cin", 24 * t + 16) + 2)
                wait_full(act, o)
                act.activation(AR[:, A_CG + T * (t % 2):A_CG + T * (t % 2) + T], obank(o)[:, 0:T],
                               ACT.Copy).then_inc(z_copy, 1)
                hi_upto(blk("cin", 24 * t + 24) + 2)
            norm("oy")
            for m in range(8):
                hi_upto(blk("co", 8 * m + 8) + 2)
            norm("x1b")
            ffn("x1b")
            norm("final")

        @block.vector
        def _(dve):
            chain = Chain(dve, dve_step)
            link = chain.link
            st = {"lo": 0, "y": 0}
            fl = lambda v: v.rearrange("p a t -> p (a t)")

            def split_lo(n, i=None):
                dve.wait_ge(hi_ready, n + 1 if i is None else i * PERIT + (n + 1))
                dve.tensor_tensor(wlo[:, n % RING, :], wraw[:, n % RAW, :], whi[:, n % RING, :].bitcast(F32),
                                  ALU.subtract).then_inc(lo_ready, 1)

            def lo_upto(n):
                while st["lo"] <= min(n, NBLK):
                    split_lo(st["lo"])
                    st["lo"] += 1

            def blk(stage, tiles):
                return (P0[stage] + tiles - 1) // TPB

            def norm(name):
                n, groups = NINFO[name]
                src, (hh, hl) = source(name), target(name)
                k = NSUMS[name]
                if groups:
                    if name in MODULATED:
                        modulated_gain(name)
                    dve.wait_ge(n_std, k + 1)
                    if NTILES[name]:
                        dve.wait_ge(n_lo, NTILES[name])
                    group_of = {t: g for g, (a, b, _) in enumerate(groups) for t in range(a, b)}

                    if name == "mix0":
                        lo_upto(0)

                    def apply(t):
                        rstd = STD[:, group_of[t], :]
                        if t == groups[group_of[t]][0]:
                            link(dve.reciprocal(rstd, rstd))
                        if name == "memory":
                            dve.tensor_tensor(CX[:, t, :], CX[:, t, :], rstd, ALU.mult).then_inc(res_tile, 1)
                            return
                        if name in ("mid", "final"):
                            dst, done_ = (X, res_tile) if name == "mid" else (SQ, n_app)
                        else:
                            dst, done_ = TN, n_app
                        dve.scalar_tensor_tensor(dst[:, t, :], src[:, t, :], gain(name, t), rstd, ALU.mult,
                                                 ALU.mult).then_inc(done_, 1)

                    if name in ("memory", "mid", "final"):
                        for t in range(n):
                            apply(t)
                        return
                    for t in range(n + 1):
                        if t < n:
                            apply(t)
                        if t:
                            low(name, t - 1)
                    return
                for t in range(n):
                    dve.wait_ge(n_hi, NTILES[name] + t + 1)
                    if name in ("mem0", "mem1"):
                        dve.scalar_tensor_tensor(hl[:, t, :], CX[:, t, :], par(name, t), hh[:, t, :].bitcast(F32),
                                                 ALU.mult, ALU.subtract).then_inc(n_lo, 1)
                    else:
                        dve.tensor_tensor(hl[:, t, :], Y[:, t, :], hh[:, t, :].bitcast(F32),
                                          ALU.subtract).then_inc(n_lo, 1)

            def low(name, t):
                hh, hl = target(name)
                dve.wait_ge(n_hi, NTILES[name] + t + 1)
                if name in MODULATED:
                    dve.scalar_tensor_tensor(hl[:, t, :], TN[:, t, :], shift(name, t), hh[:, t, :].bitcast(F32),
                                             ALU.add, ALU.subtract).then_inc(n_lo, 1)
                else:
                    dve.tensor_tensor(hl[:, t, :], TN[:, t, :], hh[:, t, :].bitcast(F32),
                                      ALU.subtract).then_inc(n_lo, 1)

            def modulated_gain(name):
                m, base, j, g = MODULATED[name]
                if name in UPDATED:
                    dve.wait_ge(res_tile, KT * (UPDATES.index(UPDATED[name]) + 1))
                link(dve.scalar_tensor_tensor(GS[:, :], m[:, base + 8 * (j + 1):base + 8 * (j + 2)], 1.0, par(g, 0, 8),
                                              ALU.add, ALU.mult))
                if name not in EARLY.values():
                    residual_gate(name)
                dve.nop().then_inc(gain_ready, 1)

            def residual_gate(name):
                m, base, j, _ = MODULATED[name]
                link(dve.tensor_scalar(HG[:, :], m[:, base + 8 * (j + 2):base + 8 * (j + 3)], 1.0 if j == 3 else 0.5, None,
                                       ALU.mult))

            def attend(h0, n, o0, keys, single, put, bias=None):
                for a in range(n + 3):
                    if a < n:
                        h = h0 + a
                        dve.wait_ge(s_full, h + 1)
                        c = 2 * (h % 2)
                        if bias is not None:
                            for qt in range(2):
                                b = bank[4 * (h % 2) + qt]
                                last = dve.tensor_tensor(b[:, 0:T], b[:, 0:T], bias(a, qt), ALU.add)
                            link(last)
                        if h >= 2:
                            dve.wait_ge(exp_done, h - 1)
                        if single:
                            for qt in range(2):
                                last = dve.tensor_reduce(NM[:, c + qt:c + qt + 1], bank[4 * (h % 2) + qt][:, :], AXX, ALU.max, negate=True)
                            last.then_inc(max_ready, 1)
                        else:
                            dve.tensor_reduce(NM[:, c:c + 2], bank[h % 2][:, :].rearrange("p (q k) -> p q k", q=2), AXX,
                                              ALU.max, negate=True).then_inc(max_ready, 1)
                    if 1 <= a <= n:
                        h = h0 + a - 1
                        c = 2 * (h % 2)
                        dve.wait_ge(exp_done, h + 1)
                        link(dve.reciprocal(RI[:, c:c + 2], SM[:, c:c + 2]))
                        for qt in range(2):
                            p = probs(h, single)[:, qt, :]
                            last = dve.tensor_scalar(p, p, RI[:, c + qt:c + qt + 1], None, ALU.mult)
                        last.then_inc(prob_ready, 1)
                    if a >= 3:
                        o = natt_output(a - 3) if single else o0 + a - 3
                        wait_full(dve, o)
                        dst, rows = put(a - 3)
                        src = obank(o)[rows, 0:T]
                        if single:
                            dst, src = backwards(dst), src.rearrange("p (r c) -> p r c", r=4)
                        dve.tensor_copy(dst, src).then_inc(free[o % 4], 1)
                if single:
                    for o in range(O0["natt"], O0["natt"] + 16):
                        if o % 4 < 2:
                            dve.nop().then_inc(free[o % 4], 1)
                done()

            def done():
                st["y"] += 1
                dve.tensor_copy(VS[:, 4:5], eps).then_inc(y_half, 1)
                dve.wait_ge(y_half, st["y"])

            def ffn(name):
                f, b0 = FI[name], P0[name] // TPB
                conv = name in ("f0", "f1")
                l = 0 if name == "f0" else 1
                per = MODS_PER_IT.get(name, 0)
                if name == "f0":
                    dve.wait_ge(c_silu, 1)
                lo_upto(b0 + 3)

                def group(g2, cnt, i, gs):
                    def at(m):
                        return cnt + m if i is None else i * 2 + (cnt + m)
                    gb, vb = bank[4 + 2 * g2], bank[5 + 2 * g2]
                    if conv:
                        dve.wait_ge(affine, at(1))
                        for tap, (d0, s0) in ((0, (1, 0)), (2, (0, 1))):
                            for part, (b, buf) in enumerate(((gb, A_CG), (vb, A_CV))):
                                for ft in range(2):
                                    col = PCOL[f"conv{l}"] + 4 * (NF * part + ft) + tap + 8 * gs
                                    w = PAR[:, col:col + 1] if i is None else PAR[:, bass.ds(i * 16 + col, 1)]
                                    dst = AR[:, buf + ft * T + d0:buf + ft * T + d0 + T - 1]
                                    last = dve.scalar_tensor_tensor(dst, b[:, ft * T + s0:ft * T + s0 + T - 1], w, dst,
                                                                    ALU.mult, ALU.add)
                            if tap == 0:
                                link(last)
                        last.then_inc(up_free, 1)

                def product(g2, cnt, i, gs):
                    def at(m):
                        return cnt + m if i is None else i * 2 + (cnt + m)
                    vb = bank[5 + 2 * g2]
                    dve.wait_ge(silu_done, at(1))
                    if conv:
                        dve.tensor_tensor(AR[:, A_CV:A_CV + 512], AR[:, A_CG:A_CG + 512], AR[:, A_CV:A_CV + 512],
                                          ALU.mult).then_inc(gate_out, 1)
                    else:
                        dve.wait_ge(g_lo, at(0))
                        dve.tensor_tensor(AR[:, A_CV:A_CV + 512], AR[:, A_CG:A_CG + 512], vb[:, :],
                                          ALU.mult).then_inc(up_free, 1)

                def low(g2, cnt, i):
                    dve.wait_ge(g_hi, GX(name) + cnt + 1 if i is None else i * 2 + (GX(name) + cnt + 1))
                    dve.tensor_tensor(fl(Gl[:, 2 * g2:2 * g2 + 2, :]), AR[:, A_CV:A_CV + 512],
                                      fl(Gh[:, 2 * g2:2 * g2 + 2, :]).bitcast(F32), ALU.subtract).then_inc(g_lo, 1)

                def mods(u, count, i):
                    for k in range(count):
                        mod(u + k, k, i)
                    mod_columns(u, count, i)

                def mod(uu, k, i):
                    ld = 16 * (uu // MODRING + 1)
                    dve.wait_ge(mod_loaded[uu % MODRING], ld if i is None else i * (16 * per // MODRING) + ld)
                    slot = modw[:, uu % MODRING, :]
                    sc = PR[:, :, :].rearrange("p a k -> p (a k)")
                    if name in MOD_BOTH:
                        dve.wait_ge(mod_used, uu + MODRING if i is None else i * per + (uu + MODRING))
                        dve.tensor_tensor_reduce(sc, slot, cb[:, 1, :], 1.0, 0.0, ALU.mult, ALU.add, MSC[:, 1, k:k + 1])
                    dve.tensor_tensor_reduce(slot, slot, cb[:, 0, :], 1.0, 0.0, ALU.mult, ALU.add,
                                             MSC[:, 0, k:k + 1]).then_inc(mod_used, 1)

                def mod_columns(u, count, i):
                    dve.wait_ge(mod_used, u + count + MODRING if i is None else i * per + (u + count + MODRING))
                    if i is None:
                        if name in MOD_BOTH:
                            dve.tensor_copy(MODC[:, u:u + count], MSC[:, 1, 0:count])
                        link(dve.tensor_copy(MODL[:, u:u + count], MSC[:, 0, 0:count]))
                    else:
                        if name in MOD_BOTH:
                            dve.tensor_copy(MODC[:, bass.ds(i * per + u, count)], MSC[:, 1, 0:count])
                        link(dve.tensor_copy(MODL[:, bass.ds(i * per + u, count)], MSC[:, 0, 0:count]))

                first = MODS_FIRST.get(name, 0)
                if first:
                    mods(MOD_START[name], 2, None)
                if name == "ctx":
                    norm("mid")
                group(0, NG * f, None, 0)
                product(0, NG * f, None, 0)
                low(0, NG * f, None)
                if first > 2:
                    mods(MOD_START[name] + 2, first - 2, None)
                with dve.Fori(0, LOOPS) as i:
                    chain.enter(i, (2 if conv else 0) + (2 if per else 0))
                    for c in range(2):
                        n0 = b0 + 2 + 3 * c
                        g2 = (1 + c) % 2
                        u0 = MOD_START.get(name, 0) + first + per // 2 * c
                        split_lo(n0 + 2, i)
                        if per > 2:
                            mod(u0, 0, i)
                        split_lo(n0 + 3, i)
                        if per > 4:
                            mod(u0 + 1, 1, i)
                        group(g2, NG * f + 1 + c, i, 1 + c)
                        if not conv:
                            product(g2, NG * f + 1 + c, i, 1 + c)
                        split_lo(n0 + 4, i)
                        if conv:
                            product(g2, NG * f + 1 + c, i, 1 + c)
                        low(g2, NG * f + 1 + c, i)
                        if per:
                            mod(u0 + per // 2 - 1, per // 2 - 1, i)
                            mod_columns(u0, per // 2, i)
                    chain.leave(LOOPS)
                st["lo"] = b0 + 34
                if name in ("f1", "ctx", "x0a", "x0b", "x1a"):
                    u = 0 if name == "f1" else MOD_START[name]
                    e = MOD_START[name] + per * LOOPS + MODS_FIRST.get(name, 0)
                    if name in MOD_BOTH:
                        dve.tensor_tensor(MODC[:, u:e], MODC[:, u:e], par("mb0", u, e - u), ALU.add)
                    link(dve.tensor_tensor(MODL[:, u:e], MODL[:, u:e], par("mb0", u, e - u), ALU.add))
                if name in EARLY:
                    norm(EARLY[name])
                    lo_upto(b0 + 34)
                res = CX if name == "ctx" else X
                for m in range(KT):
                    if m % 2 == 0:
                        if m < KT - 2:
                            dve.wait_ge(down_full, 3 * f + m // 2 + 1)
                        else:
                            dve.wait_ge(w_used, b0 + 33)
                    b = bank[m // 2][:, T * (m % 2):T * (m % 2) + T]
                    if conv:
                        dve.tensor_tensor(res[:, m, :], res[:, m, :], b, ALU.add).then_inc(res_tile, 1)
                    else:
                        dve.scalar_tensor_tensor(res[:, m, :], b, HG[:, m:m + 1], res[:, m, :], ALU.mult,
                                                 ALU.add).then_inc(res_tile, 1)
                if name in EARLY and EARLY[name] != "cn":
                    dve.wait_ge(res_tile, KT * (UPDATES.index(name) + 1))
                    residual_gate(EARLY[name])

            def residual(stage, kt, gated=False):
                for m in range(KT):
                    o = O0[stage] + m
                    lo_upto(blk(stage, kt * m + kt) + 2)
                    wait_full(dve, o)
                    b = obank(o)[:, 0:T]
                    if gated:
                        dve.scalar_tensor_tensor(X[:, m, :], b, HG[:, m:m + 1], X[:, m, :], ALU.mult,
                                                 ALU.add).then_inc(res_tile, 1)
                    else:
                        dve.tensor_tensor(X[:, m, :], X[:, m, :], b, ALU.add).then_inc(res_tile, 1)
                    if m < KT - 4:
                        dve.wait_ge(res_tile, KT * UPDATES.index(stage) + m + 1)
                        dve.nop().then_inc(free[o % 4], 1)
                dve.wait_ge(res_tile, KT * UPDATES.index(stage) + KT)
                for m in range(KT - 4, KT):
                    dve.nop().then_inc(free[(O0[stage] + m) % 4], 1)

            dve.memset(VS[:, 0:1], 0.0).then_inc(up_free, 1)
            for j in range(MODRING):
                dve.memset(VS[:, 1 + j:2 + j], 0.0).then_inc(mod_used, 1)
            dve.memset(ZB[:, :], 0.0).then_inc(zeros_ready, 1)
            dve.wait_ge(par_in, 16)
            dve.wait_ge(x_in, 32)
            for l in range(DEPTH):
                QM, KM, QB = ar(A_QM, 6), ar(A_KM, 6), ar(A_QB, 4)
                KP, U, VV, RT = ar(A_KP, 1), ar(A_U, 2), ar(A_VV, 2), ar(A_RT, 2)
                norm(f"mix{l}")
                lo_upto(P0[f"in{l}"] // TPB + 2)
                if l == 0:
                    dve.wait_ge(const_rest, 16)
                    dve.wait_ge(par_rest, 16)
                lo_upto(blk(f"in{l}", 56) + 2)
                norm(f"c{l}")
                lo_upto(blk(f"in{l}", 88) + 2)
                lo_upto(blk(f"vv{l}", 16) + 2)
                if l == 0:
                    norm("memory")
                dve.wait_ge(vv_std, l + 1)
                link(dve.reciprocal(VS[:, 2:4], VS[:, 2:4]))
                dve.wait_ge(sw_in, 96 * (l + 1))
                for tt in range(2):
                    last = dve.scalar_tensor_tensor(VV[:, tt, :], VV[:, tt, :], VS[:, 2 + tt:3 + tt], SW[:, 512:768],
                                                    ALU.mult, ALU.mult)
                last.then_inc(vv_ready, 1)
                o = O0[f"krot{l}"]
                wait_full(dve, o)
                link(dve.tensor_tensor(RT[:, 0, :], obank(o)[:, 0:T], con("sk", T), ALU.mult))
                dve.nop().then_inc(free[o % 4], 1)
                link(dve.tensor_tensor(KP[:, 0, :], KP[:, 0, :], con("ck", T), ALU.mult))
                for par_, r in ((0, slice(64, 128)), (1, slice(0, 64))):
                    last = dve.tensor_tensor(KM[r, par_:6:2, :], KP[r, 0:1, :].to_broadcast([64, 3, T]),
                                             RT[r, 0:1, :].to_broadcast([64, 3, T]), ALU.add)
                link(last)
                norm(f"mem{l}")
                dve.wait_ge(qk_std, l + 1)
                link(dve.reciprocal(STD[:, :, :], STD[:, :, :]))
                link(dve.tensor_tensor(QB[:, :, :], QB[:, :, :], STD[:, :, :], ALU.mult))
                dve.tensor_scalar(QB[:, 0:3, :], QB[:, 0:3, :], par(f"gq{l}"), 0.125, ALU.mult, ALU.mult)
                dve.tensor_scalar(QB[:, 3, :], QB[:, 3, :], par(f"gk{l}"), None, ALU.mult).then_inc(qk_norm, 1)
                o = O0[f"mix{l}"]
                wait_full(dve, o)
                MX = obank(o)[:, :].rearrange("p (g n t) -> p g n t", g=2, n=2)
                YC = Y[:, 6:8, :].rearrange("p g (n t) -> p g n t", n=2)
                BS = SW[:, 768:1024].rearrange("p (g t) -> p g t", g=2)
                for n in range(2):
                    last = dve.tensor_tensor(YC[:, :, n, :], MX[:, :, n, :], BS, ALU.add)
                link(last)
                dve.nop().then_inc(free[o % 4], 1)
                dve.tensor_tensor(Y[:, 6:8, :], Y[:, 6:8, :], U[:, :, :], ALU.mult).then_inc(mixed_done, 1)
                lo_upto(blk(f"uq{l}", 12) + 2)
                lo_upto(blk(f"pad{l}", 6) + 2)
                dve.wait_ge(mixed_done, l + 1)
                dve.wait_ge(qk_norm, l + 1)
                for j in range(2):
                    dve.wait_ge(rope_full, 5 * l + j + 1)
                    link(dve.tensor_tensor(RT[:, :, :], rope_bank(l, j)[:, :].rearrange("p (a t) -> p a t", a=2),
                                           con("sg", T)[:, None, :].to_broadcast([P, 2, T]), ALU.mult))
                    q = QB[:, 2 * j:2 * j + 2, :]
                    link(dve.tensor_tensor(q, q, con("cg", T)[:, None, :].to_broadcast([P, 2, T]), ALU.mult))
                    link(dve.tensor_tensor(q, q, RT[:, :, :], ALU.add))
                for j in range(3):
                    dve.wait_ge(rope_full, 5 * l + j + 3)
                    for e, r in ((0, slice(64, 128)), (1, slice(0, 64))):
                        last = dve.tensor_tensor(RT[r, e, :], rope_bank(l, 2 + j)[r, e * T:e * T + T], con("sk", T)[r, :],
                                                 ALU.mult)
                    link(last)
                    if j == 2:
                        dve.nop().then_inc(free[O0[f"qrot{l}"] % 4], 1)
                    for e, r in ((0, slice(64, 128)), (1, slice(0, 64))):
                        last = dve.tensor_tensor(QM[r, 2 * j + e, :], QM[r, 2 * j + e, :], con("ck", T)[r, :], ALU.mult)
                    link(last)
                    for e, r in ((0, slice(64, 128)), (1, slice(0, 64))):
                        last = dve.tensor_tensor(QM[r, 2 * j + e, :], QM[r, 2 * j + e, :], RT[r, e, :], ALU.add)
                    link(last)
                dve.nop().then_inc(rope_in, 1)
                lo_upto(blk(f"mv{l}", 32) + 1)

                def put(a):
                    if a < 6:
                        r = slice(64 * (a % 2), 64 * (a % 2) + 64)
                        return Y[r, a // 2, :], r
                    b = a - 6
                    r = slice(64 * (b // 3), 64 * (b // 3) + 64)
                    return Y[r, 3 + b % 3, :], r

                attend(16 * l, 12, O0[f"att{l}"], T, False, put)
                norm(f"y{l}")
                residual(f"out{l}", 8)
                norm(f"memx{l}")
                lo_upto(blk(f"mq{l}", 32) + 2)
                attend(16 * l + 12, 4, O0[f"matt{l}"], T, False, lambda a: (Y[:, a, :], slice(0, P)))
                norm(f"my{l}")
                residual(f"mo{l}", 4)
                norm(f"f{l}")
                ffn(f"f{l}")
            ffn("ctx")
            ffn("x0a")
            lo_upto(blk("ck", 32) + 2)
            lo_upto(blk("cv", 32) + 2)
            norm("xn")
            for s in ("eq", "ek", "ev", "eu"):
                lo_upto(blk(s, 32) + 2)

            def mask(tab, rows):
                v = tab.rearrange("p (r c) -> p r c", c=64)
                return dve.tensor_tensor(v, v, con("mask", 64)[:, None, :].to_broadcast([P, rows, 64]), ALU.add)

            dve.wait_ge(bias_in, 32 * 7)
            mask(SW[:, 0:768], 12)
            link(mask(CX.rearrange("p k t -> p (k t)")[:, 0:1920], 30))
            for g in range(4):
                o = O0["pooled"] + g
                dve.wait_ge(g_hi, NG * 4 + g + 1)
                dve.tensor_tensor(Gl[:, g, :], obank(o)[:, 0:T], Gh[:, g, :].bitcast(F32), ALU.subtract).then_inc(free[o % 4], 1)
                done()
            lo_upto(blk("pool", 4) + 2)
            dve.wait_ge(last_bias_in, 32)
            link(mask(NS[:, 0].rearrange("p k t -> p (k t)")[:, 0:384], 6))
            attend(32, 8, O0["natt"], 512, True,
                   lambda a: (Y[64 * (a % 2):64 * (a % 2) + 64, a // 2, :], slice(64 * (a % 2), 64 * (a % 2) + 64)),
                   bias=lambda a, qt: bias_table(a)[:, 64 * (2 - 2 * qt):64 * (6 - 2 * qt)])
            dve.wait_ge(evac, EV(2, "ps"))
            norm("ey")
            residual("eo", 8, gated=True)
            norm("x0b")
            ffn("x0b")
            norm("x1a")
            ffn("x1a")
            norm("x1n")
            for t in range(KT):
                oc, ox = (O0["cin"] + 3 * t + j for j in (1, 2))
                lo_upto(blk("cin", 24 * t + 24) + 2)
                dve.wait_ge(z_copy, t + 1)
                dve.nop().then_inc(free[oc % 4], 1)
                wait_full(dve, ox)
                z, zc, cg = AR[:, 512:512 + T], AR[:, 1024:1024 + T], AR[:, A_CG + T * (t % 2):A_CG + T * (t % 2) + T]
                link(dve.tensor_tensor(z, cg, obank(ox)[:, 0:T], ALU.mult))
                dve.nop().then_inc(free[ox % 4], 1)
                link(dve.tensor_scalar(zc, z, par("cw", 8 + t), None, ALU.mult))
                link(dve.scalar_tensor_tensor(zc[:, 1:T], z[:, 0:T - 1], par("cw", t), zc[:, 1:T], ALU.mult, ALU.add))
                link(dve.scalar_tensor_tensor(zc[:, 0:T - 1], z[:, 1:T], par("cw", 16 + t), zc[:, 0:T - 1], ALU.mult, ALU.add))
                link(dve.tensor_tensor(Y[:, t, :], zc, AR[:, A_BG + T * (t % 2):A_BG + T * (t % 2) + T], ALU.mult))
                done()
            norm("oy")
            residual("co", 8, gated=True)
            norm("x1b")
            ffn("x1b")
            norm("final")


def weight_blocks(a):
    stream = np.zeros((NBLK + 1, P, TPB, P), np.float32)
    tiles = stream.transpose(0, 2, 1, 3)

    def put(p, rows, cols=slice(0, P)):
        tiles[p // TPB, p % TPB][:, cols] = rows

    def feature(stage, w, cols, p=None):
        p = P0[stage] if p is None else p
        for c in cols:
            for k in range(w.shape[0] // P):
                put(p, w[k * P:k * P + P, c])
                p += 1
        return p

    def wide(stage, w, cols):
        p = P0[stage]
        for k in range(w.shape[0] // P):
            for c in cols:
                put(p, w[k * P:k * P + P, c])
                p += 1

    def span(n, off=0):
        return [slice(off + m * P, off + m * P + P) for m in range(n)]

    def ffn(stage, up, down):
        b0 = P0[stage] // TPB
        for g in range(NG):
            n = b0 if g == 0 else b0 + 2 + 3 * (g - 1)
            d = b0 + 4 + 3 * g if g < NG - 1 else b0 + 32
            feature(None, up, span(2, 2 * g * P), n * TPB)
            feature(None, up, span(2, DFF + 2 * g * P), (n + 1) * TPB)
            for ft in range(2):
                r = (2 * g + ft) * P
                for m in range(KT):
                    put(d * TPB + ft * KT + m, down[r:r + P, m * P:m * P + P])

    for l in range(DEPTH):
        w = a["w_in"][l]
        q0, kr, gq, gk, gv, gm = 0, 384, 416, 800, 928, 1056
        pair = np.arange(64)
        p = feature(f"in{l}", w, [slice(256, 384), slice(0, 128), slice(128, 256)])
        for k in range(KT):
            put(p, w[k * P:k * P + P, kr:kr + 32], slice(32, 64))
            put(p, w[k * P:k * P + P, kr:kr + 32], slice(64, 96))
            p += 1
        p = feature(None, w, [np.concatenate([gq + 64 * t + pair, gq + 64 * (3 + t) + pair]) for t in range(3)], p)
        p = feature(None, w, [slice(gk, gk + P), slice(gv, gv + P), slice(gm, gm + P), slice(gm + P, gm + 2 * P)], p)
        wide(f"vv{l}", w, span(2, gm + 256))
        p = P0[f"uq{l}"]
        for h in range(6):
            for k in range(2):
                u = a["mla_w_uq"][l][k * P:k * P + P, h * 96:h * 96 + 96]
                put(p, u[:, 0:64], slice(64 * (h % 2), 64 * (h % 2) + 64))
                put(p, u[:, 64:96], slice(64, 96) if h % 2 == 0 else slice(32, 64))
                p += 1
        u = a["mla_w_ukv"][l]
        for m in range(3):
            for e in range(2):
                h = 2 * m + e
                put(P0[f"nope{l}"] + m, u[:, h * P:h * P + 64], slice(64 * e, 64 * e + 64))
                put(P0[f"va{l}"] + m, u[:, h * P + 64:h * P + P], slice(64 * e, 64 * e + 64))
        feature(f"out{l}", a["w_out"][l][mixed_order()], span(8))
        feature(f"mk{l}", a["mem_w_kv"][l], span(4))
        wide(f"mv{l}", a["mem_w_kv"][l], span(2, 512))
        p = P0[f"mv{l}"] + 16
        for k in range(KT):
            for c in span(2, 768):
                put(p, a["mem_w_kv"][l][k * P:k * P + P, c])
                p += 1
        feature(f"mq{l}", a["mem_w_q"][l], span(4))
        feature(f"mo{l}", a["mem_w_o"][l], span(8))
        ffn(f"f{l}", a["ffn_w_up"][l], a["ffn_w_down"][l])
    w13, w2, ein = a["ffn_w13_2"], a["ffn_w2_2"], a["even_w_in_2"][0]
    for name, i, j in (("ctx", 0, 0), ("x0a", 0, 0), ("x0b", 0, 1), ("x1a", 1, 0), ("x1b", 1, 1)):
        ffn(name, w13[i, j], w2[i, j])

    def halves(stage, w, off):
        for half in range(2):
            p = P0[stage] + 16 * half
            for k in range(KT):
                for c in span(2, off + 256 * half):
                    put(p, w[k * P:k * P + P, c])
                    p += 1

    feature("ck", ein, span(4, 512))
    halves("cv", ein, 1024)
    feature("eq", ein, span(4))
    feature("ek", ein, span(4, 512))
    halves("ev", ein, 1024)
    halves("eu", ein, 1536)
    for g in range(4):
        put(P0["pool"] + g, a["pool_w_2"][0, g])
    feature("eo", a["even_w_out_2"][0], span(8))
    cin = a["conv_w_in_2"][0]
    feature("cin", cin, [slice(j * D + t * P, j * D + t * P + P) for t in range(KT) for j in range(3)])
    feature("co", a["conv_w_out_2"][0], span(8))
    return stream.reshape(NBLK + 1, P, TPB * P)


def mixed_order():
    order = list(range(384))
    for t in range(3):
        order += list(range(384 + 64 * t, 384 + 64 * t + 64)) + list(range(384 + 64 * (3 + t), 384 + 64 * (3 + t) + 64))
    return np.array(order + list(range(768, 1024)))


def param_columns(a):
    out = np.zeros((P, NPAR), np.float32)

    def put(name, v):
        v = np.asarray(v).reshape(-1, P)
        out[:, PCOL[name]:PCOL[name] + v.shape[0]] = v.T

    for l in range(DEPTH):
        put(f"mix{l}", a["mix_norm"][l])
        put(f"c{l}", np.concatenate([a["mla_kv_norm"][l], a["mla_q_norm"][l]]))
        put(f"gq{l}", np.concatenate([a["gqa_q_norm"][l]] * 2))
        put(f"gk{l}", np.concatenate([a["gqa_k_norm"][l]] * 2))
        put(f"y{l}", a["out_norm"][l][mixed_order()])
        put(f"mem{l}", a["mem_kv_norm"][l])
        put(f"memx{l}", a["mem_x_norm"][l])
        put(f"f{l}", a["ffn_norm"][l])
        conv = out[:, PCOL[f"conv{l}"]:PCOL[f"conv{l}"] + 8 * NF].reshape(P, 2 * NF, 4)
        for tap in range(3):
            conv[:, :, tap] = a["ffn_conv_w"][l, tap].reshape(2 * NF, P).T
        conv[:, :, 3] = a["ffn_conv_b"][l].reshape(2 * NF, P).T
        out[:, PCOL[f"conv{l}"]:PCOL[f"conv{l}"] + 8 * NF] = conv.reshape(P, 8 * NF)
    for i in range(DEPTH):
        for j in range(3):
            put(f"ng{i}{j}", a["norm_g_2"][i, j])
        put(f"mb{i}", a["mod_b_2"][i])
    put("ps", a["pool_scale_2"][0])
    put("cw", a["conv_w_2"][0])
    put("mid", a["final_norm"])
    put("final", a["final_g_2"])
    return out


def rotary(d):
    n = d // 4
    inv = (np.float32(10000.0) ** (-np.arange(n, dtype=np.float32) / np.float32(n))).astype(np.float32)
    t = np.arange(T)
    ang = np.concatenate([(t // 64).astype(np.float32)[:, None] * inv, (t % 64).astype(np.float32)[:, None] * inv], axis=-1)
    ang = np.repeat(ang.T, 2, axis=0).astype(np.float32)
    return np.cos(ang), np.sin(ang)


def shape_constants():
    con = np.zeros((P, NCON), np.float32)

    def put(name, v):
        con[:, CCOL[name]:CCOL[name] + v.shape[1]] = v

    i = np.arange(P)
    put("ident", np.eye(P))
    put("ones", np.ones((P, P)))
    put("bd", (i[:, None] // 64 == i[None, :] // 64).astype(np.float32))
    rot = np.zeros((P, P))
    rot[i[1::2], i[0::2]] = -1.0
    rot[i[0::2], i[1::2]] = 1.0
    put("rot", rot)
    c, s = rotary(32)
    ck, sk = np.zeros((P, T)), np.zeros((P, T))
    for r in (32, 64):
        ck[r:r + 32], sk[r:r + 32] = c, s
    put("ck", ck)
    put("sk", sk)
    c, s = rotary(64)
    put("cg", np.concatenate([c, c]))
    put("sg", np.concatenate([s, s]))
    put("eps", np.full((P, 1), 1e-6))
    q = 63 - (i % 64)[:, None]
    start = np.clip(q - 8, 0, 48)
    kc = np.arange(64)[None, :]
    put("mask", np.where((kc >= start) & (kc < start + 16), 0.0, -1e30))
    pool = np.zeros((4, T, T))
    for g, w in enumerate((2, 4, 8, 16)):
        for t in range(T):
            lo, hi = max(t - w // 2, 0), min(t - w // 2 + w, T)
            pool[g, lo:hi, t] = 1.0 / (hi - lo)
            pool[g, t, t] -= 1.0
    bp = pool.reshape(4, 2, P, T).transpose(2, 0, 1, 3).reshape(P, 2048).astype(np.float32)
    return con, np.ascontiguousarray(bp)


def feature_major(x):
    return np.ascontiguousarray(np.asarray(x).reshape(T, KT, P).transpose(2, 1, 0))


def kernel(**inputs):
    import concourse.bacc as bacc
    from concourse.bass_utils import run_bass_kernel_spmd

    a = {k: np.asarray(v) for k, v in inputs.items()}
    con, bp = shape_constants()
    rpb = np.zeros((8, 15, 128), np.float32)
    rpb[:, :, 48:79] = a["na_rpb_2"][0]
    mod = a["mod_w_2"].transpose(0, 2, 1).reshape(DEPTH * NMOD, P, D)
    arrays = {
        "stream": weight_blocks(a), "modstream": np.ascontiguousarray(mod),
        "x": feature_major(a["x"][0]), "mem": feature_major(a["mem"][0]), "ctxin": feature_major(a["ctx_2"][0]),
        "crow": np.ascontiguousarray(a["c_2"][0]), "ccrow": np.ascontiguousarray(a["c_ctx_2"]),
        "params": param_columns(a), "consts": con,
        "smallw": np.ascontiguousarray(a["gmlp_w_s"].transpose(0, 3, 1, 2).reshape(DEPTH, P, 512)),
        "smallb": np.ascontiguousarray(a["gmlp_b_s"]), "smallg": np.ascontiguousarray(a["gmlp_v_norm"]),
        "bpool": bp, "rpb": rpb,
    }
    nc = bacc.Bacc("TRN2", target_bir_lowering=False, num_devices=1)
    args = [nc.dram_tensor(k, v.shape, mybir.dt.from_np(v.dtype), kind="ExternalInput").ap() for k, v in arrays.items()]
    res = nc.dram_tensor("result", (P, KT, T), F32, kind="ExternalOutput").ap()
    two_blocks(nc, *args, res)
    r = run_bass_kernel_spmd(nc, [arrays], core_ids=[0])
    return np.ascontiguousarray(r.results[0]["result"].transpose(2, 1, 0)).reshape(1, T, D)
```
